# Optimizing a Trainium2 kernel written in Bass

```python
import math, functools
import jax, jax.numpy as jnp
from jax import lax
import numpy as np

D_MODEL = 1024
BATCH = 1
SEQ = 512
DEPTH = 1
DEC_BATCH = 8
DEC_SEQ = 1
PAST_LEN = 4096
PAGE_SIZE = 128

A_HEADS = 8
A_HEAD_DIM = 64
A_WIDTH = A_HEADS * A_HEAD_DIM
DECAY_RANK = 64
ICLR_RANK = 64
GATE_RANK = 128
GN_EPS = 64e-5
B_HEADS = 8
B_HEAD_DIM = 64
B_WIDTH = B_HEADS * B_HEAD_DIM
Q_BLOCK = 128
SHIFT_COLS = 3 * A_WIDTH + DECAY_RANK + ICLR_RANK + GATE_RANK
FOX_COLS = 3 * B_WIDTH + B_HEADS
GATE_COLS = 2 * D_MODEL
IN_COLS = SHIFT_COLS + FOX_COLS + GATE_COLS
A_SPLITS = [A_WIDTH, 2 * A_WIDTH, 3 * A_WIDTH, 3 * A_WIDTH + DECAY_RANK, 3 * A_WIDTH + DECAY_RANK + ICLR_RANK]
PEER_HEADS = 8
PEER_N_KEYS = 128
PEER_N_EXPERTS = PEER_N_KEYS * PEER_N_KEYS
PEER_TOPK = 16
PEER_QDIM = 256
PEER_HALF = PEER_QDIM // 2
PEER_BLOCK = 128
DN_ALPHA = (2.0 * DEPTH) ** 0.25
DN_BETA = (8.0 * DEPTH) ** -0.25
LN_EPS = 1e-5

kernel_name = 'rwkv7_fox_peer_hybrid_step'

def layer_norm(x, g, b):
    xf = x.astype(jnp.float32)
    mu = jnp.mean(xf, axis=-1, keepdims=True)
    var = jnp.mean(jnp.square(xf - mu), axis=-1, keepdims=True)
    return ((xf - mu) * lax.rsqrt(var + LN_EPS) * g + b).astype(x.dtype)

def ada_modulation(c, w_ada, b_ada):
    m = jax.nn.silu(c) @ w_ada + b_ada
    return jnp.split(m[:, None, :], 6, axis=-1)

def rwkv_recurrence(r, decay, k, v, kk, a, s0):
    tm = lambda t: jnp.moveaxis(t, 1, 0)

    def step(s, inp):
        r_t, d_t, k_t, v_t, kk_t, a_t = inp
        sa = jnp.einsum('bhij,bhj->bhi', s, kk_t)
        s = (s * d_t[:, :, None, :] - sa[..., None] * (kk_t * a_t)[:, :, None, :]
             + v_t[..., None] * k_t[:, :, None, :])
        return s, jnp.einsum('bhij,bhj->bhi', s, r_t)

    s_final, o = lax.scan(step, s0.astype(jnp.float32), (tm(r), tm(decay), tm(k), tm(v), tm(kk), tm(a)))
    return jnp.moveaxis(o, 0, 1), s_final

def rwkv7_branch(zs_mix, wkv_prev, w):
    f32 = jnp.float32
    bsz, t, _ = zs_mix.shape
    r, k, v, xw, xa, xg = jnp.split(zs_mix, A_SPLITS, axis=-1)
    w_log = -jax.nn.softplus(-(w['w0'] + jnp.tanh(xw) @ w['w2_decay']).astype(f32)) - 0.5
    decay = jnp.exp(-jnp.exp(w_log))
    a = jax.nn.sigmoid(w['a0'] + xa @ w['a2_iclr'])
    g = jax.nn.sigmoid(xg) @ w['g2_gate']
    heads = lambda u: u.reshape(bsz, t, A_HEADS, A_HEAD_DIM).astype(f32)
    kk = heads(k * w['k_k'])
    kk = kk / jnp.maximum(jnp.sqrt(jnp.sum(kk * kk, axis=-1, keepdims=True)), 1e-12)
    k = k * (1 + (a - 1) * w['k_a'])
    r_h, k_h, v_h, a_h, d_h = heads(r), heads(k), heads(v), heads(a), heads(decay)
    o, s_new = rwkv_recurrence(r_h, d_h, k_h, v_h, kk, a_h, wkv_prev)
    mu = jnp.mean(o, axis=-1, keepdims=True)
    var = jnp.mean(jnp.square(o - mu), axis=-1, keepdims=True)
    on = ((o - mu) * lax.rsqrt(var + GN_EPS)).reshape(bsz, t, A_WIDTH) * w['ln_x_w'] + w['ln_x_b']
    bonus = jnp.sum(r_h * k_h * w['r_k'], axis=-1, keepdims=True) * v_h
    out = (on + bonus.reshape(bsz, t, A_WIDTH)) * g
    return out.astype(zs_mix.dtype), s_new.astype(wkv_prev.dtype)

def fox_prompt(q, k, v, logf):
    bsz, t, nh, dh = q.shape
    nb = t // Q_BLOCK
    scale = dh ** -0.5
    F = jnp.cumsum(logf, axis=1)
    Fk = jnp.moveaxis(F, 2, 1)[:, :, None, :]
    kpos = jnp.arange(t)
    qb = q.reshape(bsz, nb, Q_BLOCK, nh, dh).swapaxes(0, 1)
    Fb = F.reshape(bsz, nb, Q_BLOCK, nh).swapaxes(0, 1)
    qpos = jnp.arange(t).reshape(nb, Q_BLOCK)

    def block(args):
        q_i, F_i, pos_i = args
        s = jnp.einsum('bqhd,bkhd->bhqk', q_i, k).astype(jnp.float32) * scale
        s = s + jnp.moveaxis(F_i, 2, 1)[..., None] - Fk
        s = jnp.where(kpos[None, None, None, :] <= pos_i[None, None, :, None], s, -jnp.inf)
        p = jax.nn.softmax(s, axis=-1)
        return jnp.einsum('bhqk,bkhd->bqhd', p.astype(v.dtype), v)

    o = lax.map(block, (qb, Fb, qpos))
    return o.swapaxes(0, 1).reshape(bsz, t, nh * dh)

def fox_sample(q, k, v, logf, past_k, past_v, past_logf):
    bsz, t, nh, dh = q.shape
    p_len = past_k.shape[1]
    scale = dh ** -0.5
    F = jnp.cumsum(jnp.concatenate([past_logf.astype(jnp.float32), logf], axis=1), axis=1)
    F_past = jnp.moveaxis(F[:, :p_len], 2, 1)[:, :, None, :]
    F_new = jnp.moveaxis(F[:, p_len:], 2, 1)
    s_past = (jnp.einsum('bqhd,bkhd->bhqk', q, past_k).astype(jnp.float32) * scale
              + F_new[..., None] - F_past)
    s_new = (jnp.einsum('bqhd,bkhd->bhqk', q, k).astype(jnp.float32) * scale
             + F_new[..., None] - F_new[:, :, None, :])
    s_new = jnp.where(jnp.tril(jnp.ones((t, t), bool)), s_new, -jnp.inf)
    p = jax.nn.softmax(jnp.concatenate([s_past, s_new], axis=-1), axis=-1)
    o = (jnp.einsum('bhqk,bkhd->bqhd', p[..., :p_len].astype(past_v.dtype), past_v)
         + jnp.einsum('bhqk,bkhd->bqhd', p[..., p_len:].astype(v.dtype), v))
    return o.reshape(bsz, t, nh * dh)

def peer_ffn(h, wq, keys1, keys2, u_tab, v_tab):
    f32 = jnp.float32
    n = h.shape[0]
    q = (h @ wq).reshape(n, PEER_HEADS, 2, PEER_HALF).astype(f32)
    s1 = jnp.einsum('thc,nc->thn', q[:, :, 0], keys1.astype(f32))
    s2 = jnp.einsum('thc,nc->thn', q[:, :, 1], keys2.astype(f32))
    t1, i1 = lax.top_k(s1, PEER_TOPK)
    t2, i2 = lax.top_k(s2, PEER_TOPK)
    cand_s = (t1[..., :, None] + t2[..., None, :]).reshape(n, PEER_HEADS, PEER_TOPK * PEER_TOPK)
    cand_i = (i1[..., :, None] * PEER_N_KEYS + i2[..., None, :]).reshape(n, PEER_HEADS, PEER_TOPK * PEER_TOPK)
    top_s, pos = lax.top_k(cand_s, PEER_TOPK)
    idx = jnp.take_along_axis(cand_i, pos, axis=-1)
    gate = jax.nn.softmax(top_s, axis=-1)
    u_e = u_tab[idx]
    v_e = v_tab[idx]
    act = jax.nn.gelu(jnp.einsum('td,thkd->thk', h, u_e).astype(f32))
    return jnp.einsum('thk,thkd->td', (gate * act).astype(h.dtype), v_e)

def peer_apply(h, wq, keys1, keys2, u_tab, v_tab):
    bsz, t, d = h.shape
    flat = h.reshape(bsz * t, d)
    n = flat.shape[0]
    ffn = lambda blk: peer_ffn(blk, wq, keys1, keys2, u_tab, v_tab)
    if n % PEER_BLOCK == 0 and n > PEER_BLOCK:
        out = lax.map(ffn, flat.reshape(n // PEER_BLOCK, PEER_BLOCK, d)).reshape(n, d)
    else:
        out = ffn(flat)
    return out.reshape(bsz, t, d)

def trunk_layer(x, c, shift_prev, wkv_prev, attend, w):
    bsz, t, _ = x.shape
    sh1, sc1, g1, sh2, sc2, g2 = ada_modulation(c, w['w_ada'], w['b_ada'])
    h = x * (1 + sc1) + sh1
    z = h @ w['w_in']
    zs = z[..., :SHIFT_COLS]
    zf = z[..., SHIFT_COLS:SHIFT_COLS + FOX_COLS]
    zg = z[..., SHIFT_COLS + FOX_COLS:]
    prev = jnp.concatenate([shift_prev[:, None, :].astype(zs.dtype), zs[:, :-1]], axis=1)
    zs_mix = zs + w['mu_shift'] * (prev - zs)
    a_out, wkv_new = rwkv7_branch(zs_mix, wkv_prev, w)
    q, k, v, f = jnp.split(zf, [B_WIDTH, 2 * B_WIDTH, 3 * B_WIDTH], axis=-1)
    heads = lambda u: u.reshape(bsz, t, B_HEADS, B_HEAD_DIM)
    q, k, v = heads(q), heads(k), heads(v)
    logf = jax.nn.log_sigmoid((f + w['b_forget']).astype(jnp.float32))
    b_out = attend(q, k, v, logf)
    gate_a, gate_b = jnp.split(zg, 2, axis=-1)
    mixed = (jax.nn.sigmoid(gate_a) * (a_out @ w['w_up_a'])
             + jax.nn.sigmoid(gate_b) * (b_out @ w['w_up_b']))
    x1 = layer_norm(DN_ALPHA * x + g1 * (mixed @ w['w_o']), w['ln1_g'], w['ln1_b'])
    h2 = x1 * (1 + sc2) + sh2
    ffn = peer_apply(h2, w['peer_wq'], w['peer_keys1'], w['peer_keys2'], w['peer_u'], w['peer_v'])
    y = layer_norm(DN_ALPHA * x1 + g2 * ffn, w['ln2_g'], w['ln2_b'])
    return y, k, v, logf, wkv_new, zs[:, -1]

def setup_inputs(seed: int = 0) -> dict:
    key = jax.random.key(seed)
    ks = iter(jax.random.split(key, 40))
    f32 = jnp.float32
    L = DEPTH
    n_pages = PAST_LEN // PAGE_SIZE
    n_pool = (DEC_BATCH * n_pages * 5) // 4

    def normal(shape, scale):
        return scale * jax.random.normal(next(ks), shape, f32)

    inp = {}
    inp['x_prompt'] = normal((BATCH, SEQ, D_MODEL), 1.0)
    inp['x_sample'] = normal((DEC_BATCH, DEC_SEQ, D_MODEL), 1.0)
    inp['cache_k'] = normal((L, n_pool, PAGE_SIZE, B_HEADS, B_HEAD_DIM), 1.0)
    inp['cache_v'] = normal((L, n_pool, PAGE_SIZE, B_HEADS, B_HEAD_DIM), 1.0)
    inp['cache_logf'] = jax.nn.log_sigmoid(3.0 + normal((L, n_pool, PAGE_SIZE, B_HEADS), 1.0))
    inp['state_wkv'] = normal((L, DEC_BATCH, A_HEADS, A_HEAD_DIM, A_HEAD_DIM), 0.3)
    inp['state_shift'] = normal((L, DEC_BATCH, SHIFT_COLS), 1.0)
    perm = jax.random.permutation(next(ks), n_pool)
    inp['page_table'] = perm[: DEC_BATCH * n_pages].reshape(DEC_BATCH, n_pages).astype(jnp.int32)
    inp['c_prompt'] = normal((BATCH, D_MODEL), 1.0)
    inp['c_sample'] = normal((DEC_BATCH, D_MODEL), 1.0)
    inp['w_ada'] = normal((L, D_MODEL, 6 * D_MODEL), D_MODEL ** -0.5)
    inp['b_ada'] = normal((L, 6 * D_MODEL), 0.02)
    inp['w_in'] = normal((L, D_MODEL, IN_COLS), D_MODEL ** -0.5)
    inp['mu_shift'] = jax.random.uniform(next(ks), (L, SHIFT_COLS), f32)
    inp['w0'] = jax.random.uniform(next(ks), (L, A_WIDTH), f32, -6.0, 1.0)
    inp['w2_decay'] = normal((L, DECAY_RANK, A_WIDTH), 0.5 * DECAY_RANK ** -0.5)
    inp['a0'] = normal((L, A_WIDTH), 0.5)
    inp['a2_iclr'] = normal((L, ICLR_RANK, A_WIDTH), ICLR_RANK ** -0.5)
    inp['g2_gate'] = normal((L, GATE_RANK, A_WIDTH), GATE_RANK ** -0.5)
    inp['k_k'] = 1.0 + normal((L, A_WIDTH), 0.1)
    inp['k_a'] = 1.0 + normal((L, A_WIDTH), 0.1)
    inp['r_k'] = normal((L, A_HEADS, A_HEAD_DIM), 0.1)
    inp['ln_x_w'] = 1.0 + normal((L, A_WIDTH), 0.1)
    inp['ln_x_b'] = normal((L, A_WIDTH), 0.02)
    inp['b_forget'] = jnp.linspace(1.0, 6.0, B_HEADS, dtype=f32) + normal((L, B_HEADS), 0.1)
    inp['w_up_a'] = normal((L, A_WIDTH, D_MODEL), A_WIDTH ** -0.5)
    inp['w_up_b'] = normal((L, B_WIDTH, D_MODEL), B_WIDTH ** -0.5)
    inp['w_o'] = normal((L, D_MODEL, D_MODEL), DN_BETA * D_MODEL ** -0.5)
    inp['ln1_g'] = 1.0 + normal((L, D_MODEL), 0.05)
    inp['ln1_b'] = normal((L, D_MODEL), 0.02)
    inp['peer_wq'] = normal((L, D_MODEL, PEER_HEADS * PEER_QDIM), D_MODEL ** -0.5)
    inp['peer_keys1'] = normal((L, PEER_N_KEYS, PEER_HALF), PEER_HALF ** -0.5)
    inp['peer_keys2'] = normal((L, PEER_N_KEYS, PEER_HALF), PEER_HALF ** -0.5)
    inp['peer_u'] = normal((L, PEER_N_EXPERTS, D_MODEL), D_MODEL ** -0.5)
    inp['peer_v'] = normal((L, PEER_N_EXPERTS, D_MODEL), DN_BETA)
    inp['ln2_g'] = 1.0 + normal((L, D_MODEL), 0.05)
    inp['ln2_b'] = normal((L, D_MODEL), 0.02)
    return inp

def reference(x_prompt, x_sample, cache_k, cache_v, cache_logf, state_wkv, state_shift, page_table,
              c_prompt, c_sample, w_ada, b_ada, w_in, mu_shift, w0, w2_decay, a0, a2_iclr, g2_gate,
              k_k, k_a, r_k, ln_x_w, ln_x_b, b_forget, w_up_a, w_up_b, w_o, ln1_g, ln1_b,
              peer_wq, peer_keys1, peer_keys2, peer_u, peer_v, ln2_g, ln2_b):
    n_seq, n_pages = page_table.shape
    yp, ys = x_prompt, x_sample
    outs_p = ([], [], [], [], [])
    outs_s = ([], [], [], [], [])
    for l in range(DEPTH):
        lw = {'w_ada': w_ada[l], 'b_ada': b_ada[l], 'w_in': w_in[l], 'mu_shift': mu_shift[l],
              'w0': w0[l], 'w2_decay': w2_decay[l], 'a0': a0[l], 'a2_iclr': a2_iclr[l],
              'g2_gate': g2_gate[l], 'k_k': k_k[l], 'k_a': k_a[l], 'r_k': r_k[l],
              'ln_x_w': ln_x_w[l], 'ln_x_b': ln_x_b[l], 'b_forget': b_forget[l],
              'w_up_a': w_up_a[l], 'w_up_b': w_up_b[l], 'w_o': w_o[l],
              'ln1_g': ln1_g[l], 'ln1_b': ln1_b[l], 'peer_wq': peer_wq[l],
              'peer_keys1': peer_keys1[l], 'peer_keys2': peer_keys2[l],
              'peer_u': peer_u[l], 'peer_v': peer_v[l], 'ln2_g': ln2_g[l], 'ln2_b': ln2_b[l]}
        shift0 = jnp.zeros((yp.shape[0], SHIFT_COLS), yp.dtype)
        wkv0 = jnp.zeros((yp.shape[0], A_HEADS, A_HEAD_DIM, A_HEAD_DIM), state_wkv.dtype)
        yp, kp, vp, lfp, wkvp, shp = trunk_layer(yp, c_prompt, shift0, wkv0, fox_prompt, lw)
        past_k = cache_k[l][page_table].reshape(n_seq, n_pages * PAGE_SIZE, B_HEADS, B_HEAD_DIM)
        past_v = cache_v[l][page_table].reshape(n_seq, n_pages * PAGE_SIZE, B_HEADS, B_HEAD_DIM)
        past_logf = cache_logf[l][page_table].reshape(n_seq, n_pages * PAGE_SIZE, B_HEADS)
        attend = functools.partial(fox_sample, past_k=past_k, past_v=past_v, past_logf=past_logf)
        ys, ks_, vs_, lfs, wkvs, shs = trunk_layer(ys, c_sample, state_shift[l], state_wkv[l], attend, lw)
        for lst, arr in zip(outs_p, (kp, vp, lfp, wkvp, shp)):
            lst.append(arr)
        for lst, arr in zip(outs_s, (ks_, vs_, lfs, wkvs, shs)):
            lst.append(arr)
    new_k_prompt = jnp.stack(outs_p[0]).astype(cache_k.dtype)
    new_v_prompt = jnp.stack(outs_p[1]).astype(cache_v.dtype)
    new_logf_prompt = jnp.stack(outs_p[2]).astype(cache_logf.dtype)
    new_wkv_prompt = jnp.stack(outs_p[3]).astype(state_wkv.dtype)
    new_shift_prompt = jnp.stack(outs_p[4]).astype(state_shift.dtype)
    new_k_sample = jnp.stack(outs_s[0]).astype(cache_k.dtype)
    new_v_sample = jnp.stack(outs_s[1]).astype(cache_v.dtype)
    new_logf_sample = jnp.stack(outs_s[2]).astype(cache_logf.dtype)
    new_wkv_sample = jnp.stack(outs_s[3]).astype(state_wkv.dtype)
    new_shift_sample = jnp.stack(outs_s[4]).astype(state_shift.dtype)
    return (yp, ys, new_k_prompt, new_v_prompt, new_logf_prompt, new_wkv_prompt, new_shift_prompt,
            new_k_sample, new_v_sample, new_logf_sample, new_wkv_sample, new_shift_sample)


_drawn_inputs = setup_inputs


def setup_inputs(seed=0):
    import zlib

    import numpy as np

    out = dict(_drawn_inputs(seed))
    spreads = {}
    factors = {'ln_x_w': 3.047, 'ln_x_b': 7.677, 'ln2_b': 2.691, 'cache_logf': 3.112}
    for name, (base, spread) in spreads.items():
        noise = np.random.default_rng([zlib.crc32(name.encode()), seed]).standard_normal(out[name].shape)
        drawn = base * np.exp(spread * noise) if base else spread * noise
        out[name] = __import__('jax').numpy.asarray(drawn.astype(out[name].dtype))
    for name, factor in factors.items():
        out[name] = (out[name] * factor).astype(out[name].dtype)
    return out
```

```python
from contextlib import ExitStack

import numpy as np

import concourse.bass as bass
from concourse import mybir

P = 128
D = 1024
KD = D // P
T = 512
NT = T // P
NS = 8
TT = T + NS
H = 8
HD = 64
W = H * HD
NC = W // P
SHIFT = 3 * W + 64 + 64 + 128
MS = SHIFT // P
QCOL, KCOL, VCOL, FCOL = SHIFT, SHIFT + W, SHIFT + 2 * W, SHIFT + 3 * W
GCOL = FCOL + H
IN_COLS = GCOL + 2 * D
PAGES = 32
PAGE = 128
POOL = 320
RING = 8
C = 64
NCH = T // C
NG = NCH // 2
LEVELS = 6
PH = 8
KEYS = 128
TOP = 16
SLOTS = PH * TOP
ALPHA = 2.0 ** 0.25
LN_EPS = 1e-5
GN_EPS = 64e-5
DECAY = float(np.exp(-0.5))
SCALE = HD ** -0.5
NEG = -1.0e30
LOW = -3.0e38

CONST = {}
_at = 0
for _name, _n in [("ident", P), ("ones", P), ("rows", (NS + 1) * P), ("iota", TOP), ("eye", NS * NS),
                  ("causal", P), ("suffix", P),
                  ("headones", P), ("gmask", P), ("levels", LEVELS * C), ("reset", T)]:
    CONST[_name] = (_at, _n)
    _at += _n
CONST_COLS = _at
CONST_B = CONST["causal"][0]
CONST_C = CONST["headones"][0]

PAR = {}
_at = 0
for _name, _n in [("mu_shift", MS), ("w0", NC), ("a0", NC), ("k_k", NC), ("k_a", NC), ("r_k", NC),
                  ("ln_x_w", NC), ("ln_x_b", NC), ("b_ada", 16)]:
    PAR[_name] = (_at, _n)
    _at += _n
PAR_ROWS = _at


def constants():
    c = np.zeros((P, CONST_COLS), np.float32)
    p = np.arange(P)

    def put(name, value):
        at, n = CONST[name]
        c[:value.shape[0], at:at + n] = value

    put("ident", np.eye(P))
    put("headones", (p[:, None] // HD == p[None, :] // HD) * 1.0)
    put("ones", np.ones((P, P)))
    put("causal", np.where(p[None, :] <= p[:, None], 0.0, NEG))
    s, t = (p % C)[:, None], np.arange(C)[None, :]
    put("gmask", np.concatenate([s < t, s <= t], 1) * 1.0)
    put("suffix", ((p[:, None] // PAGES == p[None, :] // PAGES) & (p[:, None] > p[None, :])) * 1.0)
    lv = []
    for n in range(LEVELS):
        b = 2 ** n
        lv.append((s // (2 * b) == t // (2 * b)) & (s % (2 * b) < b) & (t % (2 * b) >= b))
    put("levels", np.concatenate(lv, 1) * 1.0)
    put("reset", np.broadcast_to((np.arange(T) % C != 0) * 1.0, (P, T)))
    rows = np.zeros((NS + 1, NS + 1, P))
    for n in range(NS + 1):
        rows[n, n] = 1.0
    put("rows", rows.reshape(NS + 1, (NS + 1) * P))
    put("eye", np.broadcast_to(np.eye(NS).reshape(1, NS * NS), (P, NS * NS)))
    put("iota", np.broadcast_to(np.arange(TOP) * 1.0, (P, TOP)))
    return c


(LOAD, PROJ, SAMPLE, FOX, PRE, STATE, CHAIN, MIX, OUT, QUERY, PEER) = range(11)


def place_buffers(buffers, limit):
    placed = {}
    for name, n, a, b in sorted(buffers, key=lambda x: -(x[1] + 1200 * (x[3] - x[2]))):
        at, moved = 0, True
        while moved:
            moved = False
            for o, (oat, on, oa, ob) in placed.items():
                if not (b < oa or ob < a) and at < oat + on and oat < at + n:
                    at, moved = oat + on, True
        placed[name] = (at, n, a, b)
        assert at + n <= limit, (name, at + n, limit)
    return placed


BUFFERS = [
    ("const", CONST_B, LOAD, PEER), ("const_b", CONST_C - CONST_B, LOAD, FOX),
    ("const_c", CONST_COLS - CONST_C, PRE, MIX), ("par", PAR_ROWS + 24, LOAD, MIX), ("c_t", KD * 9, LOAD, OUT),
    ("stats", 64, LOAD, PEER), ("eps", 2, LOAD, PEER),
    ("x_rows", NT * D, LOAD, LOAD), ("xs_rows", D, LOAD, LOAD), ("c_rows", 2 * D, LOAD, LOAD),
    ("par_rows", P, LOAD, LOAD), ("shift_rows", SHIFT, LOAD, LOAD), ("shift_t", MS * NS, LOAD, PROJ),
    ("logf_rows", 2 * D, LOAD, LOAD), ("prefix", 2 * D, LOAD, LOAD), ("page_tot", 64, LOAD, LOAD),
    ("ada_t", 16 * 9, LOAD, PROJ), ("h_t", KD * TT, LOAD, MIX), ("w_f", KD * H, LOAD, PROJ),
    ("wring0", 4096, LOAD, QUERY), ("wring1", 4096, LOAD, QUERY),
    ("mix", MS * TT, PROJ, MIX), ("prev", MS * TT, PROJ, PROJ), ("z9", MS * 9, PROJ, PROJ),
    ("shift_out", 512, PROJ, PROJ),
    ("q_t", NC * T, PROJ, FOX), ("k_t", NC * T, PROJ, FOX), ("v_rows", NT * W, PROJ, FOX),
    ("k_rows", W, PROJ, PROJ), ("f", TT, PROJ, FOX), ("f2", TT, PROJ, FOX), ("logf_out", NT * H, PROJ, PROJ),
    ("qs", W, PROJ, SAMPLE), ("ks", W, PROJ, SAMPLE), ("vs", W, PROJ, CHAIN), ("bf", 16, LOAD, PROJ),
    ("qb", NS * W, PROJ, SAMPLE), ("pages", RING * W, PROJ, CHAIN), ("scores", H * 256, PROJ, CHAIN),
    ("bias", H * 256, LOAD, SAMPLE), ("small", 649, SAMPLE, CHAIN),
    ("probs", 2 * T, FOX, FOX), ("probs_t", 2 * T, FOX, FOX), ("rowstat", 3 * NT * H, FOX, FOX),
    ("b_out", NC * TT, FOX, MIX),
    ("lora", 512 * 2, LOAD, PRE),
    ("bk", NC * NCH * P, PRE, CHAIN), ("rk", NC * NCH * P, PRE, CHAIN), ("kk", NC * TT, PRE, PRE),
    ("sig", NC * TT, PRE, PRE), ("iclr", NC * TT, PRE, PRE), ("t1", NC * TT, PRE, PRE),
    ("svec", 6 * NC * NS, PRE, STATE), ("snat", 6 * W, STATE, STATE), ("shead", 6 * HD, STATE, STATE),
    ("wkv", 2048, STATE, STATE), ("wkv_tmp", 2048, STATE, STATE), ("gate", NC * TT, PRE, MIX), ("lam", NC * NCH, PRE, CHAIN),
    ("so_rows", W, STATE, MIX),
    ("g", 2 * H * P, CHAIN, CHAIN), ("bkn", 2 * NC * P, CHAIN, CHAIN), ("uv", 3 * W, CHAIN, CHAIN),
    ("inv", 2 * NC * C, CHAIN, CHAIN), ("inv_t", 2 * NC * C, CHAIN, CHAIN), ("y", 2 * NC * C, CHAIN, CHAIN),
    ("xt", 2 * NC * C, CHAIN, CHAIN), ("r_sb", NC * C, CHAIN, CHAIN), ("state", NC * C, CHAIN, CHAIN),
    ("o_t", NC * TT, CHAIN, MIX),
    ("n1", NC * TT, MIX, MIX), ("n2", NC * TT, MIX, MIX), ("mixed", KD * TT, MIX, OUT), ("sg", 2 * TT, MIX, MIX),
    ("sgs", KD * NS, MIX, MIX),
    ("x2", NT * D, OUT, OUT), ("xs2", D, OUT, OUT), ("an", 4 * D, OUT, OUT), ("bc", 4 * D, OUT, PEER),
    ("lng", 4 * D, OUT, PEER), ("x1", 5 * D, OUT, PEER), ("h2", 5 * D, OUT, PEER), ("g2s", D, OUT, PEER),
    ("h2_t", KD * TT, OUT, QUERY), ("key_t", 2 * P, OUT, PEER), ("key_rows", 2 * P, OUT, OUT),
    ("qp", 16 * TT, QUERY, PEER), ("ta", 2048, QUERY, PEER), ("tb", 2048, QUERY, PEER),
    ("idx", 5 * SLOTS, QUERY, PEER), ("coef", 5 * SLOTS, QUERY, PEER), ("top", 1552, QUERY, PEER),
    ("rows", RING * D, PEER, PEER), ("diag", RING * P, PEER, PEER), ("stage", 2 * RING, PEER, PEER),
    ("ids_row", NS * PAGES, LOAD, CHAIN), ("ids_col", 2, LOAD, LOAD), ("svalue", 32, STATE, STATE),
    ("so_col", 32, STATE, STATE), ("idx_f", SLOTS, QUERY, PEER), ("idx_s", NS, PEER, PEER),
    ("coef_s", NS * NS, PEER, PEER), ("zero", P, PEER, PEER), ("gelu", 288, PEER, PEER),
]


def psum_jobs():
    jobs = []

    def ring(*names):
        jobs.extend((n, None) for n in names)

    def fixed(bank, name):
        jobs.append((name, bank))

    ring("par", "c_t", "shift_t")
    ring(*[f"ada{j}" for j in range(4)])
    ring(*[f"x{t}_{u}" for t in range(NT) for u in range(2)], "xs", "suffix", *[f"bias{u}" for u in range(4)])
    ring("qs", *[f"q{c}" for c in range(NC)], *[f"qb{b}" for b in range(NS)])
    ring("ks", *[f"k{c}" for c in range(NC)], "vs", *[f"v{t}" for t in range(NT)], "f", "fs")
    ring(*[f"z{m}" for m in range(MS)])
    fixed(7, "zs")
    ring(*[f"shift{u}" for u in range(4)], *[f"krows{t}" for t in range(NT)], "logf")
    ring("s_new", "max_t", "max_b", "sum_b")
    for i in range(NT * H + 2):
        if i < NT * H:
            ring(f"qk{i}")
        if 1 <= i <= NT * H:
            ring(f"pt{i - 1}")
        if i >= 2 and (i - 2) % H == 0:
            fixed(6, f"o{(i - 2) // H}")
    fixed(7, "lora_s")
    fixed(6, "iclr_s")
    ring(*[f"{x}{c}" for x in ("dec", "iclr", "gate") for c in range(NC)])
    ring(*[f"norm{c}" for c in range(NC)], "norm_s", *[f"bonus{c}" for c in range(NC)], "bonus_s")
    ring(*[f"svec{i}" for i in range(6)], "so")
    fixed(7, "vo")
    for gp in range(NG):
        for n in (2 * gp, 2 * gp + 1):
            ring(f"bk{n}", f"gm{n}_0", f"gm{n}_1")
        for m in (range(0, 3) if gp == 0 else range(2 * gp + 1, 2 * gp + 3)):
            ring(f"vw{m}")
        for lv in range(LEVELS):
            ring(f"iy{gp}_{lv}", *([f"inv{gp}_{lv}"] if lv < LEVELS - 1 else []), f"invt{gp}_{lv}")
        for n in (2 * gp, 2 * gp + 1):
            ring(f"r{n}", f"u{n}", f"oc{n}", f"st{n}")
    ring("state")
    ring(*[f"mean{c}" for c in range(NC)], "mean_s", *[f"var{c}" for c in range(NC)], "var_s")
    for br in "AB":
        fixed(6, f"gs{br}")
        fixed(7, f"us{br}")
        ring(*[f"{x}{br}{m}" for m in range(KD) for x in ("g", "u")])
    ring("keys", *[f"{x}{j}" for j in range(8) for x in ("an", "ab")])
    ring(*[f"wo{u}_{t}" for u in range(2) for t in range(NT + 1)])
    ring(*[f"h2{t}_{u}" for t in range(NT) for u in range(2)], "h2s")
    fixed(7, "pqs")
    ring(*[f"pq{m}" for m in range(16)])
    for t in range(NT + 1):
        ring(*[f"s{t}_{g}" for g in range(4)])
        if t:
            fixed(6, f"y{t - 1}_0")
            fixed(7, f"y{t - 1}_1")
    ring("tg", *[f"hb{b}_{u}" for b in range(NS) for u in range(2)])
    fixed(6, "ys_0")
    fixed(7, "ys_1")
    place, used, r = {}, [0] * 8, 0
    for name, bank in jobs:
        if bank is None:
            bank, r = r, (r + 1) % 6
        place[name] = (bank, used[bank])
        used[bank] += 1
    return place


def hybrid_step(nc, x_prompt, x_sample, cache_k, cache_v, cache_logf, state_wkv, state_shift, page_table,
                c_prompt, c_sample, w_ada, b_ada, w_in, mu_shift, w0, w2_decay, a0, a2_iclr, g2_gate,
                k_k, k_a, r_k, ln_x_w, ln_x_b, b_forget, w_up_a, w_up_b, w_o, ln1_g, ln1_b,
                peer_wq, peer_keys1, peer_keys2, peer_u, peer_v, ln2_g, ln2_b, consts, scratch, scratch_o,
                y_prompt, y_sample, new_k_prompt, new_v_prompt, new_logf_prompt, new_wkv_prompt, new_shift_prompt,
                new_k_sample, new_v_sample, new_logf_sample, new_wkv_sample, new_shift_sample):
    F32 = mybir.dt.float32
    I32 = mybir.dt.int32
    U32 = mybir.dt.uint32
    ALU = mybir.AluOpType
    ACT = mybir.ActivationFunctionType
    AX = mybir.AxisListType
    OFF = bass.IndirectOffsetOnAxis
    ds = bass.ds
    JOB = psum_jobs()
    limit = (nc.sbuf_usable_end - nc.sbuf_base - 64) // 4
    PLACE = place_buffers(BUFFERS, limit)

    ctx = ExitStack()
    with ctx:
        ctx.enter_context(nc.allow_non_contiguous_dma(reason="a page's index a partition"))
        arena = ctx.enter_context(nc.sbuf_tensor("arena", [P, limit], F32))
        bank_of = [ctx.enter_context(nc.psum_tensor(f"bank{i}", [P, 512], F32)) for i in range(8)]

        def sem(name):
            return ctx.enter_context(nc.semaphore(name))

        def buf(name):
            at, n, _, _ = PLACE[name]
            return arena[:, at:at + n]

        def const(name):
            at, n = CONST[name]
            part, base = ("const", 0) if at < CONST_B else ("const_b", CONST_B) if at < CONST_C else ("const_c", CONST_C)
            return buf(part)[:, at - base:at - base + n]

        ident, ones, iota = const("ident"), const("ones"), const("iota")
        rows = const("rows").rearrange("p (n q) -> p n q", n=NS + 1)
        eye = const("eye").rearrange("p (b t) -> p b t", b=NS)
        stats = buf("stats")
        par = buf("par")[:, 0:PAR_ROWS]
        par_more = buf("par")[:, PAR_ROWS:PAR_ROWS + 24]
        one_minus_mu, one_minus_ka = par_more[:, 0:MS], par_more[:, MS:MS + NC]

        def param(name, a=0, b=None):
            at, n = PAR[name]
            return par[:, at + a:at + (n if b is None else b)]

        def blocks(name, n):
            return buf(name).rearrange("p (n x) -> p n x", n=n)

        h_t = blocks("h_t", KD)
        c_t = blocks("c_t", KD)
        ada_t = blocks("ada_t", 16)
        mix = blocks("mix", MS)
        prev = blocks("prev", MS)
        z9 = blocks("z9", MS)
        q_t, k_t, v_rows = blocks("q_t", NC), blocks("k_t", NC), blocks("v_rows", NT)
        f, f2 = buf("f"), buf("f2")
        qb, pages = blocks("qb", NS), blocks("pages", RING)
        scores = blocks("scores", H)
        b_out = blocks("b_out", NC)
        wring = [buf("wring0"), buf("wring1")]


        def sm(a, b):
            return buf("small")[:, a:b]

        pn_rows = sm(585, 649).rearrange("p (b h) -> p b h", b=NS)
        probs, probs_t = blocks("probs", 2), blocks("probs_t", 2)
        kk, sig, iclr, t1, gate = (blocks(x, NC) for x in ("kk", "sig", "iclr", "t1", "gate"))
        bk = buf("bk").rearrange("p (c n x) -> p c n x", c=NC, n=NCH)
        rk = buf("rk").rearrange("p (c n x) -> p c n x", c=NC, n=NCH)
        lam = blocks("lam", NC)
        svec = buf("svec").rearrange("p (i c b) -> p i c b", i=6, c=NC)
        g = buf("g").rearrange("p (n h x) -> p n h x", n=2, h=H)
        bkn = buf("bkn").rearrange("p (n c x) -> p n c x", n=2, c=NC)
        uv = buf("uv").rearrange("p (s h i) -> p s h i", s=3, h=H)
        inv, inv_t, y, xt = (blocks(x, 2 * NC) for x in ("inv", "inv_t", "y", "xt"))
        r_sb, state, o_t = blocks("r_sb", NC), blocks("state", NC), blocks("o_t", NC)
        n1, n2, mixed, sg = blocks("n1", NC), blocks("n2", NC), blocks("mixed", KD), blocks("sg", 2)
        an, bc, lng = buf("an"), blocks("bc", 4), blocks("lng", 4)
        x1, h2, h2_t = blocks("x1", 5), blocks("h2", 5), blocks("h2_t", KD)
        key_t, qp = blocks("key_t", 2), blocks("qp", 16)
        idx_u, idx_f, idx_s = buf("idx").bitcast(U32), buf("idx_f"), buf("idx_s").bitcast(U32)
        coef, coef_cols = blocks("coef", 5), buf("coef")
        coef_s, zero, gelu, eps = blocks("coef_s", NS), buf("zero"), buf("gelu"), buf("eps")
        gathered, diag = blocks("rows", RING), blocks("diag", RING)

        bank_full = [sem(f"bank_full{i}") for i in range(8)]
        bank_free = [sem(f"bank_free{i}") for i in range(8)]
        phase_end = sem("phase_end")
        vector_step, scalar_step, pool_step = sem("vector_step"), sem("scalar_step"), sem("pool_step")
        consts_in, x_in, c_in, par_in, shift_in = sem("consts_in"), sem("x_in"), sem("c_in"), sem("par_in"), sem("shift_in")
        ids_in, forget_in, logf_in = sem("ids_in"), sem("forget_in"), sem("logf_in")
        w_in_slot = [sem("w_in_slot0"), sem("w_in_slot1")]
        wf_in, lora_in = sem("wf_in"), sem("lora_in")
        w_used = [sem("w_used0"), sem("w_used1")]
        silu_ready, ada_ready, prefix_ready, tot_ready = sem("silu_ready"), sem("ada_ready"), sem("prefix_ready"), sem("tot_ready")
        prev_ready = sem("prev_ready")
        logf_ready = sem("logf_ready")
        krows_out, shift_stored = sem("krows_out"), sem("shift_stored")
        stored = sem("stored")
        page_loaded = [sem(f"page_loaded{j}") for j in range(RING)]
        page_free = [sem(f"page_free{j}") for j in range(RING)]
        page_seen = sem("page_seen")
        page_product, page_tick = sem("page_product"), sem("page_tick")
        snew_ready, max_ready, diag_ready, sum_ready, probs_ready = (
            sem("snew_ready"), sem("max_ready"), sem("diag_ready"), sem("sum_ready"), sem("probs_ready"))
        row_max, row_exp, row_prob = sem("row_max"), sem("row_exp"), sem("row_prob")
        proj_stored = sem("proj_stored")
        state_in = sem("state_in")
        heads_out = sem("heads_out")
        heads_in = sem("heads_in")
        wkv_ready = sem("wkv_ready")
        so_in = sem("so_in")
        wkv_stored = sem("wkv_stored")
        an_in = sem("an_in")
        key_in = sem("key_in")
        x2_in = sem("x2_in")
        lng_in = sem("lng_in")
        y_ready = sem("y_ready")
        idx_ready = sem("idx_ready")
        stage_tick = sem("stage_tick")
        stage_ready = sem("stage_ready")
        forget_sum = sem("forget_sum")
        lora_ready = sem("lora_ready")
        squares_ready = sem("squares_ready")
        rk_product = sem("rk_product")
        xt_ready = sem("xt_ready")
        state_ready = sem("state_ready")
        a_ready = sem("a_ready")
        dev_squares = sem("dev_squares")
        h2_ready = sem("h2_ready")
        zero_ready = sem("zero_ready")
        top_s_ready = sem("top_s_ready")
        coef_s_ready = sem("coef_s_ready")
        c_sigmoid = sem("c_sigmoid")
        f_abs = sem("f_abs")
        f_log = sem("f_log")
        shifted = sem("shifted")
        exps_ready = sem("exps_ready")
        norm_ready = sem("norm_ready")
        pre_acts = sem("pre_acts")
        logs_ready = sem("logs_ready")
        dev_ready = sem("dev_ready")
        var_ready = sem("var_ready")
        root_ready = sem("root_ready")
        top_done = sem("top_done")
        gate_ready = sem("gate_ready")
        gate_exps = sem("gate_exps")
        gelu_arg = sem("gelu_arg")
        gelu_tanh = sem("gelu_tanh")
        coef_ready = sem("coef_ready")
        dots_kept = sem("dots_kept")
        row_in = [sem(f"row_in{j}") for j in range(RING)]
        row_free = [sem(f"row_free{j}") for j in range(RING)]
        diag_made = [sem(f"diag_made{j}") for j in range(RING)]
        OUTPUTS = [0]

        wada = w_ada.rearrange("l (k p) n -> (l p) k n", p=P)
        win = w_in.rearrange("l (k p) n -> (l p) k n", p=P)
        WEIGHTS = [(f"ada{j}", [(wada[:, :, 512 * j:512 * (j + 1)], 0, 512)]) for j in range(4)]
        WEIGHTS += [("q", [(win[:, :, QCOL:QCOL + W], 0, 512)]), ("k", [(win[:, :, KCOL:KCOL + W], 0, 512)]),
                    ("v", [(win[:, :, VCOL:VCOL + W], 0, 512)])]
        WEIGHTS += [(f"z{j}", [(win[:, :, 512 * j:min(512 * (j + 1), SHIFT)], 0, min(512, SHIFT - 512 * j))])
                    for j in range(4)]
        for br, up in (("A", w_up_a), ("B", w_up_b)):
            wup = up.rearrange("l (k p) n -> (l p) k n", p=P)
            g0 = GCOL + (D if br == "B" else 0)
            WEIGHTS += [(f"{br}{j}", [(win[:, :, g0 + 256 * j:g0 + 256 * (j + 1)], 0, 256),
                                      (wup[:, :, 256 * j:256 * (j + 1)], 2048, 256)]) for j in range(4)]
        WEIGHTS += [(f"an{j}", [(wada[:, :, 2 * D + 512 * j:2 * D + 512 * (j + 1)], 0, 512)]) for j in range(8)]
        wov = w_o.rearrange("l (k p) n -> (l p) k n", p=P)
        WEIGHTS += [(f"wo{j}", [(wov[:, :, 512 * j:512 * (j + 1)], 0, 512)]) for j in range(2)]
        wqv = peer_wq.rearrange("l (k p) n -> (l p) k n", p=P)
        WEIGHTS += [(f"wq{j}", [(wqv[:, :, 512 * j:512 * (j + 1)], 0, 512)]) for j in range(4)]
        WJOB = {name: i for i, (name, _) in enumerate(WEIGHTS)}

        def arrivals(i):
            return 16 * sum(len(parts) for j, (_, parts) in enumerate(WEIGHTS[:i + 1]) if j % 2 == i % 2)

        def slot(i, at, k, n):
            return wring[i % 2][:, at:at + k * n].rearrange("p (k n) -> p k n", k=k)

        def full(e, job):
            bank, n = JOB[job]
            e.wait_ge(bank_full[bank], n + 1)

        def read(e, job):
            bank, n = JOB[job]
            e.wait_ge(bank_free[bank], n + 1)

        def bank(job):
            return bank_of[JOB[job][0]]

        def make_link(e, step):
            count = [0]

            def link(ins, job=None, signal=None, at=None):
                if job is not None:
                    ins.then_inc(bank_free[JOB[job][0]], 1)
                    e.wait_ge(bank_free[JOB[job][0]], JOB[job][1] + 1)
                elif signal is not None:
                    ins.then_inc(signal, 1)
                    e.wait_ge(signal, at)
                else:
                    count[0] += 1
                    ins.then_inc(step, 1)
                    e.wait_ge(step, count[0])

            return link

        def end_phase(e, phase):
            e.drain().then_inc(phase_end, 1)
            e.wait_ge(phase_end, 3 * (phase + 1))

        def col(name, n, i=0):
            return buf(name)[:, i:i + n]

        block = ctx.enter_context(nc.Block())

        last_use = {**{f"ada{j}": f"ada{j}" for j in range(4)}, "q": "q3", "k": "k3", "v": "v3",
                    **{f"z{j}": f"z{min(4 * j + 3, MS - 1)}" for j in range(4)},
                    **{f"{br}{j}": f"u{br}{2 * j + 1}" for br in "AB" for j in range(4)},
                    **{f"an{j}": f"an{j}" for j in range(8)}, **{f"wo{j}": f"wo{j}_{NT}" for j in range(2)},
                    **{f"wq{j}": f"pq{4 * j + 3}" for j in range(4)}}

        @block.sync
        def _(sp):
            def load(dst, src, signal):
                sp.dma_start(dst, src).then_inc(signal, 16)

            def store(dst, src):
                sp.dma_start(dst, src).then_inc(stored, 16)
                OUTPUTS[0] += 16

            def weights(*names):
                for name in names:
                    i = WJOB[name]
                    if i >= 2:
                        full(sp, last_use[WEIGHTS[i - 2][0]])
                    for src, at, n in WEIGHTS[i][1]:
                        load(slot(i, at, src.shape[1], n), src, w_in_slot[i % 2])

            load(buf("const"), consts[:, 0:CONST_B], consts_in)
            load(buf("const_b"), consts[:, CONST_B:CONST_C], consts_in)
            load(buf("c_rows")[0:8, 0:D], c_sample[:, :], c_in)
            load(buf("c_rows")[8:9, 0:D], c_prompt[:, :], c_in)
            load(buf("ids_col").bitcast(I32), page_table.rearrange("(t b) g -> (b g) t", t=2), ids_in)
            load(buf("ids_row")[0:1, :].bitcast(I32), page_table.rearrange("(o b) g -> o (b g)", o=1), ids_in)
            for name, src in (("mu_shift", mu_shift), ("w0", w0), ("a0", a0), ("k_k", k_k), ("k_a", k_a),
                              ("r_k", r_k.rearrange("l h n -> l (h n)")), ("ln_x_w", ln_x_w), ("ln_x_b", ln_x_b),
                              ("b_ada", b_ada[:, 0:2 * D])):
                at, n = PAR[name]
                load(buf("par_rows")[at:at + n, :], src.rearrange("l (m p) -> (l m) p", p=P), par_in)
            weights("ada0", "ada1")
            load(buf("x_rows").rearrange("p (t d) -> p t d", t=NT), x_prompt.rearrange("o (t p) d -> p (o t) d", p=P), x_in)
            load(buf("xs_rows")[0:8, :], x_sample.rearrange("b o d -> b (o d)"), x_in)
            load(buf("shift_rows")[0:8, :], state_shift.rearrange("l b n -> (l b) n"), shift_in)
            load(buf("bf")[0:8, 0:1], b_forget.rearrange("l h -> h l"), forget_in)
            load(buf("bf")[0:8, 8:16], b_forget.to_broadcast([8, H]), forget_in)
            load(buf("w_f").rearrange("p (k n) -> p k n", k=KD), win[:, :, FCOL:FCOL + H], wf_in)
            load(buf("lora")[0:64, 0:512], w2_decay.rearrange("l r n -> (l r) n"), lora_in)
            load(buf("lora")[64:128, 0:512], a2_iclr.rearrange("l r n -> (l r) n"), lora_in)
            load(buf("lora")[:, 512:1024], g2_gate.rearrange("l r n -> (l r) n"), lora_in)
            weights("ada2", "ada3", "q", "k", "v", "z0", "z1", "z2", "z3", "A0", "A1")
            for u in range(4):
                read(sp, f"shift{u}")
                n = min(4, MS - 4 * u) * P
                store(new_shift_sample.rearrange("l b n -> (l b) n")[:, 512 * u:512 * u + n], buf("shift_out")[0:8, 0:n])
                store(new_shift_prompt.rearrange("l b n -> (l b) n")[:, 512 * u:512 * u + n], buf("shift_out")[8:9, 0:n])
                sp.wait_ge(stored, OUTPUTS[0])
                sp.sem_inc(shift_stored, 1)
            nk = new_k_prompt.rearrange("l o (t p) h d -> p (l o t) (h d)", p=P)
            nv = new_v_prompt.rearrange("l o (t p) h d -> p (l o t) (h d)", p=P)
            for t in range(NT):
                read(sp, f"krows{t}")
                store(nk[:, t, :], buf("k_rows"))
                sp.wait_ge(stored, OUTPUTS[0])
                sp.sem_inc(krows_out, 1)
            store(nv, v_rows)
            read(sp, "logf")
            store(new_logf_prompt.rearrange("l o (t p) h -> p (l o t) h", p=P),
                  buf("logf_out").rearrange("p (t h) -> p t h", t=NT))
            store(new_k_sample.rearrange("l b o h d -> (l b o) (h d)"), buf("ks")[0:8, :])
            store(new_v_sample.rearrange("l b o h d -> (l b o) (h d)"), buf("vs")[0:8, :])
            store(new_logf_sample.rearrange("l b o h -> (l b o) h"), f[0:8, T:TT])
            sp.wait_ge(stored, OUTPUTS[0])
            sp.sem_inc(proj_stored, 1)
            sp.wait_ge(phase_end, 3 * (FOX + 1))
            load(buf("const_c"), consts[:, CONST_C:CONST_COLS], consts_in)
            sp.wait_ge(phase_end, 3 * (PRE + 1))
            load(buf("wkv"), state_wkv.rearrange("l b h (e i) j -> (l b h e) (i j)", e=2), state_in)
            for i in range(6):
                read(sp, f"svec{i}")
            load(scratch.rearrange("k b w -> b k w"), buf("snat")[0:8, :].rearrange("b (k w) -> b k w", k=6), heads_out)
            sp.wait_ge(heads_out, 16)
            heads = scratch.rearrange("k b (h n) -> (b h) k n", h=H)
            for e in range(2):
                load(buf("shead")[e:P:2, :].rearrange("p (k n) -> p k n", k=6), heads, heads_in)
            load(buf("svalue"), scratch[4, :, :].rearrange("b (h e n) -> (b h e) n", h=H, e=2), heads_in)
            sp.wait_ge(wkv_ready, 1)
            store(new_wkv_sample.rearrange("l b h (e i) j -> (l b h e) (i j)", e=2), buf("wkv"))
            sp.wait_ge(wkv_ready, 2)
            load(scratch_o.rearrange("b (h e n) -> (b h e) n", h=H, e=2), buf("so_col"), heads_out)
            sp.wait_ge(heads_out, 32)
            load(buf("so_rows")[0:8, :], scratch_o, so_in)
            sp.wait_ge(stored, OUTPUTS[0])
            sp.sem_inc(wkv_stored, 1)
            read(sp, "state")
            store(new_wkv_prompt.rearrange("l o h i j -> i (l o h) j"),
                  buf("y")[0:64, 0:512].rearrange("i (h j) -> i h j", h=H))
            sp.wait_ge(stored, OUTPUTS[0])
            sp.sem_inc(wkv_stored, 1)
            weights("A2", "A3", "B0", "B1", "B2", "B3", "an0", "an1")
            sp.wait_ge(phase_end, 3 * (MIX + 1))
            load(buf("an")[0:9, :], b_ada[:, 2 * D:6 * D].to_broadcast([9, 4 * D]), an_in)
            load(buf("key_rows")[:, 0:P], peer_keys1.rearrange("l n c -> (l n) c"), key_in)
            load(buf("key_rows")[:, P:2 * P], peer_keys2.rearrange("l n c -> (l n) c"), key_in)
            load(buf("x2").rearrange("p (t d) -> p t d", t=NT), x_prompt.rearrange("o (t p) d -> p (o t) d", p=P), x2_in)
            load(buf("xs2")[0:8, :], x_sample.rearrange("b o d -> b (o d)"), x2_in)
            for i, src in enumerate((ln1_g, ln1_b, ln2_g, ln2_b)):
                load(lng[:, i, :], src.to_broadcast([P, D]), lng_in)
            weights(*[f"an{j}" for j in range(2, 8)], "wo0", "wo1", "wq0", "wq1", "wq2", "wq3")
            for t in range(NT + 1):
                sp.wait_ge(y_ready, t + 1)
                if t < NT:
                    store(y_prompt.rearrange("o (t p) d -> p (o t) d", p=P)[:, t, :], h2[:, t, :])
                else:
                    store(y_sample.rearrange("b o d -> b (o d)"), h2[0:8, NT, :])
            sp.wait_ge(stored, OUTPUTS[0])

        @block.gpsimd
        def _(pool):
            pool.wait_ge(ids_in, 32)
            pages_logf = cache_logf.rearrange("l n s h -> (l n) (s h)")
            for t in range(2):
                nc.gpsimd.indirect_dma_start(buf("logf_rows")[:, t * D:(t + 1) * D], None, pages_logf[:, :],
                                             OFF(ap=buf("ids_col")[:, t:t + 1].bitcast(U32), axis=0)).then_inc(logf_in, 16)
            pool.wait_ge(phase_end, 3 * (LOAD + 1))
            ids = buf("ids_row")[0:1, :].bitcast(I32)
            for past, cache in enumerate((cache_k, cache_v)):
                rows_of = cache.rearrange("l n s h d -> (l n) s (h d)")
                with pool.Fori(0, NS) as b:
                    with pool.Fori(0, PAGES // RING) as g:
                        for j in range(RING):
                            page = pool.value_load(ids[:, ds(b * PAGES + g * RING + j, 1)], min_val=0, max_val=POOL - 1)
                            pool.wait_ge(page_free[j], b * 4 + g + (1 + 32 * past))
                            pool.sem_inc(page_seen, 1)
                            pool.dma_start(pages[:, j, :], rows_of[ds(page, 1), :, :].rearrange("o p d -> (o p) d"))\
                                .then_inc(page_loaded[j], 16)
            link = make_link(pool, pool_step)
            tables = (peer_u.rearrange("l e d -> (l e) d"), peer_v.rearrange("l e d -> (l e) d"))
            stage = buf("stage").bitcast(U32)
            pool.wait_ge(phase_end, 3 * (QUERY + 1))
            for t in range(NT):
                pool.wait_ge(idx_ready, t + 1)
                for kind in range(2):
                    use = 16 * (2 * t + kind)
                    with pool.Fori(0, SLOTS // (2 * RING)) as i:
                        for g in range(2):
                            for j in range(RING):
                                pool.wait_ge(row_free[j], i * 2 + (use + g + 1))
                            pool.sem_inc(stage_tick, 1)
                            nc.gpsimd.tensor_copy(stage[:, RING * g:RING * (g + 1)],
                                                  idx_u[:, ds(i * (2 * RING) + (t * SLOTS + g * RING), RING)])\
                                .then_inc(stage_ready, 1)
                            for j in range(RING):
                                pool.wait_ge(stage_ready, i * 2 + (use + g + 1))
                                pool.wait_ge(row_free[j], i * 2 + (use + g + 2))
                                pool.sem_inc(stage_tick, 1)
                                nc.gpsimd.indirect_dma_start(
                                    gathered[:, j, :], None, tables[kind][:, :],
                                    OFF(ap=stage[:, RING * g + j:RING * g + j + 1], axis=0)).then_inc(row_in[j], 16)
            pool.wait_ge(idx_ready, NT + 1)
            for kind in range(2):
                use = 16 * 2 * NT + kind
                for b in range(NS):
                    pool.wait_ge(row_free[b], use + 2)
                    nc.gpsimd.indirect_dma_start(gathered[:, b, :], None, tables[kind][:, :],
                                                 OFF(ap=idx_s[:, b:b + 1], axis=0)).then_inc(row_in[b], 16)

        @block.tensor
        def _(pe):
            mm = nc.tensor.matmul

            def begin(job):
                b, n = JOB[job]
                if n:
                    pe.wait_ge(bank_free[b], n)
                return bank_of[b]

            def end(ins, job):
                ins.then_inc(bank_full[JOB[job][0]], 1)

            def weight(name, k, n, at=0):
                i = WJOB[name]
                pe.wait_ge(w_in_slot[i % 2], arrivals(i))
                return slot(i, at, k, n)

            def product(out, pairs, **more):
                for i, (a, b) in enumerate(pairs):
                    ins = mm(out, a, b, start=i == 0, stop=i == len(pairs) - 1, **more)
                return ins

            def turn(out, in_):
                n = in_.shape[0]
                at = in_.start_partition if isinstance(in_.start_partition, int) else in_.start_partition()
                return nc.tensor.transpose(out, in_, ident[at:at + n, at:at + n])

            pe.wait_ge(consts_in, 32)
            pe.wait_ge(par_in, 16 * len(PAR))
            end(turn(begin("par")[:, 0:PAR_ROWS], buf("par_rows")[0:PAR_ROWS, :]), "par")
            pe.wait_ge(silu_ready, 1)
            o = begin("c_t")
            for k in range(KD):
                ins = turn(o[:, 9 * k:9 * k + 9], buf("c_rows")[0:9, P * k:P * (k + 1)])
            end(ins, "c_t")
            pe.wait_ge(shift_in, 16)
            o = begin("shift_t")
            for m in range(MS):
                ins = turn(o[:, NS * m:NS * (m + 1)], buf("shift_rows")[0:8, P * m:P * (m + 1)])
            end(ins, "shift_t")
            read(pe, "c_t")
            for j in range(4):
                o, w = begin(f"ada{j}"), weight(f"ada{j}", KD, 512)
                for m in range(4):
                    ins = product(o[:, 9 * m:9 * m + 9], [(w[:, k, P * m:P * (m + 1)], c_t[:, k, :]) for k in range(KD)])
                end(ins, f"ada{j}")
            pe.wait_ge(x_in, 32)
            for t in range(NT):
                for u in range(2):
                    o = begin(f"x{t}_{u}")
                    for k in range(4):
                        at = t * D + (4 * u + k) * P
                        ins = turn(o[:, P * k:P * (k + 1)], buf("x_rows")[:, at:at + P])
                    end(ins, f"x{t}_{u}")
            o = begin("xs")
            for k in range(KD):
                ins = turn(o[:, NS * k:NS * (k + 1)], buf("xs_rows")[0:8, P * k:P * (k + 1)])
            end(ins, "xs")
            pe.wait_ge(prefix_ready, 1)
            end(product(begin("suffix")[:, 0:16], [(const("suffix"), buf("page_tot")[:, 0:16])]), "suffix")
            pe.wait_ge(tot_ready, 1)
            for u in range(4):
                o = begin(f"bias{u}")
                for i in range(4):
                    at = (4 * u + i) * P
                    ins = turn(o[:, P * i:P * (i + 1)], buf("prefix")[:, at:at + P])
                end(ins, f"bias{u}")
            end_phase(pe, LOAD)

            hs = [h_t[:, k, T:TT] for k in range(KD)]
            hp = [h_t[:, k, 0:T] for k in range(KD)]

            def rows_s(job, w):
                end(product(begin(job)[0:8, 0:w.shape[2]], [(hs[k], w[:, k, :]) for k in range(KD)]), job)

            def columns(job, w, m):
                end(product(begin(job)[:, :], [(w[:, k, P * m:P * (m + 1)], hp[k]) for k in range(KD)]), job)

            w = weight("q", KD, W)
            rows_s("qs", w)
            for c in range(NC):
                columns(f"q{c}", w, c)
            read(pe, "qs")
            for b in range(NS):
                end(product(begin(f"qb{b}")[:, :], [(rows[0:8, b, :], buf("qs")[0:8, :])]), f"qb{b}")
            w = weight("k", KD, W)
            rows_s("ks", w)
            for c in range(NC):
                columns(f"k{c}", w, c)
            w = weight("v", KD, W)
            rows_s("vs", w)
            for t in range(NT):
                end(product(begin(f"v{t}")[:, :], [(h_t[:, k, P * t:P * (t + 1)], w[:, k, :]) for k in range(KD)]), f"v{t}")
            pe.wait_ge(wf_in, 16)
            w = blocks("w_f", KD)
            end(product(begin("f")[0:8, :], [(w[:, k, :], hp[k]) for k in range(KD)]), "f")
            rows_s("fs", w)
            zs = begin("zs")
            for m in range(MS):
                w = weight(f"z{m // 4}", KD, min(512, SHIFT - 512 * (m // 4)))
                a = P * (m % 4)
                product(zs[:, NS * m:NS * (m + 1)], [(w[:, k, a:a + P], hs[k]) for k in range(KD)])
                columns(f"z{m}", w, m % 4)
            pe.drain().then_inc(bank_full[7], 1)
            read(pe, "zs")
            for u in range(4):
                o = begin(f"shift{u}")
                for i in range(min(4, MS - 4 * u)):
                    ins = turn(o[0:9, P * i:P * (i + 1)], z9[:, 4 * u + i, :])
                end(ins, f"shift{u}")
            for t in range(NT):
                o = begin(f"krows{t}")
                for c in range(NC):
                    ins = turn(o[:, P * c:P * (c + 1)], k_t[:, c, P * t:P * (t + 1)])
                end(ins, f"krows{t}")
            pe.wait_ge(logf_ready, 1)
            o = begin("logf")
            for t in range(NT):
                ins = turn(o[:, H * t:H * (t + 1)], f[0:8, P * t:P * (t + 1)])
            end(ins, "logf")
            end_phase(pe, PROJ)

            pe.wait_ge(snew_ready, 1)
            end(product(begin("s_new")[:, 0:64], [(ones[0:8, :], sm(8, 72)[0:8, :])]), "s_new")
            pe.wait_ge(max_ready, 1)
            end(turn(begin("max_t")[0:64, 0:P], sm(136, 200)), "max_t")
            pe.wait_ge(diag_ready, 1)
            end(product(begin("max_b")[:, 0:64], [(ones[0:64, :], sm(201, 265)[0:64, :])]), "max_b")
            pe.wait_ge(sum_ready, 1)
            end(product(begin("sum_b")[:, 0:64], [(ones, sm(393, 457))]), "sum_b")
            end_phase(pe, SAMPLE)

            pe.wait_ge(forget_sum, 1)
            for i in range(NT * H + 2):
                if i < NT * H:
                    t, h = divmod(i, H)
                    n, a, c = P * (t + 1), HD * (h % 2), h // 2
                    o = begin(f"qk{i}")
                    mm(o[:, 0:n], q_t[a:a + HD, c, P * t:P * (t + 1)], k_t[a:a + HD, c, 0:n], start=True, stop=False)
                    mm(o[:, 0:n], rows[0:8, h, :], f2[0:8, 0:n], start=False, stop=False)
                    end(mm(o[:, n - P:n], ident, const("causal"), start=False, stop=True), f"qk{i}")
                if 1 <= i <= NT * H:
                    t = (i - 1) // H
                    pe.wait_ge(row_prob, i)
                    o = begin(f"pt{i - 1}")
                    for k in range(t + 1):
                        ins = turn(o[:, P * k:P * (k + 1)], probs[:, (i - 1) % 2, P * k:P * (k + 1)])
                    end(ins, f"pt{i - 1}")
                if i >= 2:
                    t, h = divmod(i - 2, H)
                    a, c = HD * (h % 2), h // 2
                    if h == 0:
                        o6 = begin(f"o{t}")
                    read(pe, f"pt{i - 2}")
                    ins = product(o6[a:a + HD, P * c:P * (c + 1)],
                                  [(v_rows[:, k, HD * h:HD * (h + 1)], probs_t[:, i % 2, P * k:P * (k + 1)])
                                   for k in range(t + 1)])
                    if h == H - 1:
                        end(ins, f"o{t}")
            end_phase(pe, FOX)

            lora = buf("lora")
            pe.wait_ge(lora_in, 48)
            pe.wait_ge(lora_ready, 2)
            kinds = [(lora[0:64, 0:512], mix[0:64, 12, :]), (lora[64:128, 0:512], mix[64:128, 12, :]),
                     (lora[:, 512:1024], mix[:, 13, :])]
            o = begin("lora_s")
            for i in (0, 2):
                w, x = kinds[i]
                for c in range(NC):
                    at = (NC * i + c) * NS
                    ins = mm(o[:, at:at + NS], w[:, P * c:P * (c + 1)], x[:, T:TT], start=True, stop=True)
            end(ins, "lora_s")
            o = begin("iclr_s")
            w, x = kinds[1]
            for c in range(NC):
                ins = mm(o[:, NS * c:NS * (c + 1)], w[:, P * c:P * (c + 1)], x[:, T:TT], start=True, stop=True)
            end(ins, "iclr_s")
            for name, (w, x) in zip(("dec", "iclr", "gate"), kinds):
                for c in range(NC):
                    end(mm(begin(f"{name}{c}")[:, :], w[:, P * c:P * (c + 1)], x[:, 0:T], start=True, stop=True), f"{name}{c}")
            pe.wait_ge(consts_in, 48)

            def head_sums(name, src):
                for c in range(NC):
                    end(mm(begin(f"{name}{c}")[:, :], const("headones"), src[:, c, 0:T], start=True, stop=True), f"{name}{c}")
                end(mm(begin(f"{name}_s")[:, 0:NC * NS], const("headones"), src[:, :, T:TT], start=True, stop=True), f"{name}_s")

            pe.wait_ge(squares_ready, 1)
            head_sums("norm", t1)
            pe.wait_ge(rk_product, 1)
            head_sums("bonus", buf("bk")[:, 0:NC * TT].rearrange("p (c t) -> p c t", c=NC))
            end_phase(pe, PRE)

            for i in range(6):
                o = begin(f"svec{i}")
                for c in range(NC):
                    ins = turn(o[0:8, P * c:P * (c + 1)], svec[:, i, c, :])
                end(ins, f"svec{i}")
            end_phase(pe, STATE)

            pe.wait_ge(so_in, 16)
            o = begin("so")
            for c in range(NC):
                ins = turn(o[:, NS * c:NS * (c + 1)], buf("so_rows")[0:8, P * c:P * (c + 1)])
            end(ins, "so")
            begin("vo")
            vflat = buf("mix")
            for gp in range(NG):
                chunks = (2 * gp, 2 * gp + 1)
                for n in chunks:
                    o = begin(f"bk{n}")
                    for c in range(NC):
                        ins = turn(o[:, P * c:P * (c + 1)], bk[:, c, n, :])
                    end(ins, f"bk{n}")
                    for u in range(2):
                        o = begin(f"gm{n}_{u}")
                        for i in range(4):
                            a = HD * u
                            ins = mm(o[:, P * i:P * (i + 1)], bk[a:a + HD, i, n, :], rk[a:a + HD, i, n, :],
                                     start=True, stop=True)
                        end(ins, f"gm{n}_{u}")
                for m in (range(0, 3) if gp == 0 else range(2 * gp + 1, 2 * gp + 3)):
                    o = begin(f"vw{m}")
                    for c in range(NC):
                        at = (8 + c) * TT + C * (m - 1)
                        ins = turn(o[:, P * c:P * (c + 1)], vflat[:, at:at + P])
                    end(ins, f"vw{m}")
                pairs = [(q, a) for q in range(2 * NC) for a in (0, C)]

                def small(job, lhs, rhs):
                    o = begin(job)
                    for q, a in pairs:
                        ins = mm(o[a:a + C, C * q:C * (q + 1)], lhs[a:a + C, q, :], rhs[a:a + C, q, :],
                                 start=True, stop=True)
                    end(ins, job)

                for lv in range(LEVELS):
                    pe.wait_ge(xt_ready, 2 * (gp * LEVELS + lv + 1))
                    small(f"iy{gp}_{lv}", xt, inv)
                    read(pe, f"iy{gp}_{lv}")
                    if lv < LEVELS - 1:
                        small(f"inv{gp}_{lv}", inv_t, y)
                    small(f"invt{gp}_{lv}", y, inv_t)
                read(pe, f"invt{gp}_{LEVELS - 1}")
                for n in chunks:
                    s, e2 = n % 3, n % 2
                    heads = [(2 * c + e, c, C * e) for c in range(NC) for e in range(2)]
                    pe.wait_ge(state_ready, n + 1)
                    o = begin(f"r{n}")
                    for h, c, a in heads:
                        mm(o[a:a + C, C * c:C * (c + 1)], rk[a:a + C, c, n, 0:C], state[a:a + C, c, :],
                           start=True, stop=False)
                        ins = mm(o[a:a + C, C * c:C * (c + 1)], g[:, e2, h, 0:C], uv[:, s, h, :], start=False, stop=True)
                    end(ins, f"r{n}")
                    read(pe, f"r{n}")
                    o = begin(f"u{n}")
                    for h, c, a in heads:
                        ins = mm(o[a:a + C, C * c:C * (c + 1)], inv_t[a:a + C, NC * e2 + c, :], r_sb[a:a + C, c, :],
                                 start=True, stop=True)
                    end(ins, f"u{n}")
                    read(pe, f"u{n}")
                    o = begin(f"oc{n}")
                    for h, c, a in heads:
                        mm(o[a:a + C, C * c:C * (c + 1)], state[a:a + C, c, :], rk[a:a + C, c, n, C:P],
                           start=True, stop=False)
                        ins = mm(o[a:a + C, C * c:C * (c + 1)], uv[:, s, h, :], g[:, e2, h, C:P], start=False, stop=True)
                    end(ins, f"oc{n}")
                    o = begin(f"st{n}")
                    for h, c, a in heads:
                        ins = mm(o[a:a + C, C * c:C * (c + 1)], bkn[:, e2, c, a:a + C], uv[:, s, h, :],
                                 start=True, stop=True)
                    end(ins, f"st{n}")
                    vo = bank_of[7]
                    for c in range(NC):
                        at = n * H + 2 * c
                        mm(vo[:, at:at + 2], buf("vs")[0:8, P * c:P * (c + 1)], pn_rows[0:8, n, 2 * c:2 * c + 2],
                           start=c == 0, stop=False, skip_group_check=True)
                    with pe.Fori(0, PAGES // RING) as gg:
                        for j in range(RING):
                            pe.wait_ge(page_loaded[j], gg * 16 + 16 * (32 + 4 * n + 1))
                            for c in range(NC):
                                at = n * H + 2 * c
                                ins = mm(vo[:, at:at + 2], pages[:, j, P * c:P * (c + 1)],
                                         scores[:, 2 * c:2 * c + 2, ds(gg * RING + (n * PAGES + j), 1)],
                                         start=False, stop=False, skip_group_check=True)
                            ins.then_inc(page_free[j], 1)
            pe.drain().then_inc(bank_full[7], 1)
            pe.wait_ge(state_ready, NCH + 1)
            o = begin("state")
            for c in range(NC):
                ins = turn(o[0:64, P * c:P * (c + 1)], state[:, c, :])
            end(ins, "state")
            end_phase(pe, CHAIN)

            head_sums("mean", o_t)
            pe.wait_ge(dev_squares, 1)
            head_sums("var", n2)
            for br, src in (("A", o_t), ("B", b_out)):
                if br == "A":
                    pe.wait_ge(a_ready, 1)
                gs, us = begin(f"gs{br}"), begin(f"us{br}")
                for m in range(KD):
                    wg, wu = weight(f"{br}{m // 2}", KD, 256), weight(f"{br}{m // 2}", NC, 256, 2048)
                    a = P * (m % 2)
                    product(gs[:, NS * m:NS * (m + 1)], [(wg[:, k, a:a + P], hs[k]) for k in range(KD)])
                    product(us[:, NS * m:NS * (m + 1)], [(wu[:, k, a:a + P], src[:, k, T:TT]) for k in range(NC)])
                    columns(f"g{br}{m}", wg, m % 2)
                    end(product(begin(f"u{br}{m}")[:, :], [(wu[:, k, a:a + P], src[:, k, 0:T]) for k in range(NC)]),
                        f"u{br}{m}")
                pe.drain().then_inc(bank_full[6], 1)
                pe.drain().then_inc(bank_full[7], 1)
            end_phase(pe, MIX)

            pe.wait_ge(key_in, 32)
            o = begin("keys")
            for i in range(2):
                ins = turn(o[:, P * i:P * (i + 1)], buf("key_rows")[:, P * i:P * (i + 1)])
            end(ins, "keys")
            for j in range(8):
                w = weight(f"an{j}", KD, 512)
                end(product(begin(f"an{j}")[0:9, :], [(c_t[:, k, :], w[:, k, :]) for k in range(KD)]), f"an{j}")
                read(pe, f"an{j}")
                end(mm(begin(f"ab{j}")[:, :], rows[0:9, NS, :], an[0:9, 512 * j:512 * (j + 1)], start=True, stop=True),
                    f"ab{j}")
            for u in range(2):
                w = weight(f"wo{u}", KD, 512)
                for t in range(NT + 1):
                    a, n = (P * t, P) if t < NT else (T, NS)
                    end(product(begin(f"wo{u}_{t}")[0:n, :], [(mixed[:, k, a:a + n], w[:, k, :]) for k in range(KD)]),
                        f"wo{u}_{t}")
            for t in range(NT):
                pe.wait_ge(h2_ready, t + 1)
                for u in range(2):
                    o = begin(f"h2{t}_{u}")
                    for k in range(4):
                        ins = turn(o[:, P * k:P * (k + 1)], h2[:, t, P * (4 * u + k):P * (4 * u + k + 1)])
                    end(ins, f"h2{t}_{u}")
            pe.wait_ge(h2_ready, NT + 1)
            o = begin("h2s")
            for k in range(KD):
                ins = turn(o[:, NS * k:NS * (k + 1)], h2[0:8, NT, P * k:P * (k + 1)])
            end(ins, "h2s")
            end_phase(pe, OUT)

            pqs = begin("pqs")
            for m in range(16):
                w = weight(f"wq{m // 4}", KD, 512)
                a = P * (m % 4)
                product(pqs[:, NS * m:NS * (m + 1)], [(w[:, k, a:a + P], h2_t[:, k, T:TT]) for k in range(KD)])
                end(product(begin(f"pq{m}")[:, :], [(w[:, k, a:a + P], h2_t[:, k, 0:T]) for k in range(KD)]), f"pq{m}")
            pe.drain().then_inc(bank_full[7], 1)
            end_phase(pe, QUERY)

            def key_scores(t):
                a, n = (P * t, P) if t < NT else (T, NS)
                for gg in range(4):
                    o = begin(f"s{t}_{gg}")
                    for i in range(4):
                        m = 4 * gg + i
                        ins = mm(o[0:n, P * i:P * (i + 1)], qp[:, m, a:a + n], key_t[:, m % 2, :], start=True, stop=True)
                    end(ins, f"s{t}_{gg}")

            key_scores(0)
            for t in range(NT):
                key_scores(t + 1)
                acc = [begin(f"y{t}_{u}") for u in range(2)]
                pe.wait_ge(zero_ready, 1)
                for u in range(2):
                    mm(acc[u][:, :], zero, bc[:, 0, 0:512], start=True, stop=False, skip_group_check=True)
                use = 16 * (2 * t + 1)
                with pe.Fori(0, SLOTS // RING) as i:
                    for j in range(RING):
                        pe.wait_ge(row_in[j], i * 16 + 16 * (use + 1))
                        pe.wait_ge(diag_made[j], i + (16 * t + 1))
                        for u in range(2):
                            ins = mm(acc[u][:, :], diag[:, j, :], gathered[:, j, 512 * u:512 * (u + 1)],
                                     start=False, stop=False, skip_group_check=True)
                        ins.then_inc(row_free[j], 1)
                pe.drain().then_inc(bank_full[6], 1)
                pe.drain().then_inc(bank_full[7], 1)
            pe.wait_ge(top_s_ready, 1)
            o = begin("tg")
            turn(o[:, 0:NS], idx_f[0:8, :])
            end(turn(o[:, NS:2 * NS], coef[0:8, NT, :]), "tg")
            for b in range(NS):
                for u in range(2):
                    end(mm(begin(f"hb{b}_{u}")[:, :], rows[0:8, b, :], h2[0:8, NT, 512 * u:512 * (u + 1)],
                           start=True, stop=True), f"hb{b}_{u}")
            acc = [begin(f"ys_{u}") for u in range(2)]
            pe.wait_ge(coef_s_ready, 1)
            for b in range(NS):
                pe.wait_ge(row_in[b], 16 * (16 * 2 * NT + 2))
                for u in range(2):
                    ins = mm(acc[u][0:8, :], coef_s[:, b, :], gathered[:, b, 512 * u:512 * (u + 1)],
                             start=b == 0, stop=b == NS - 1, skip_group_check=True)
            pe.drain().then_inc(bank_full[6], 1)
            pe.drain().then_inc(bank_full[7], 1)

        @block.scalar
        def _(act):
            link = make_link(act, scalar_step)
            fn = nc.scalar.activation

            def take(job, out, src, func=ACT.Copy, last=True, **more):
                full(act, job)
                link(fn(out, src, func, **more), job=job if last else None)

            act.wait_ge(c_in, 32)
            link(fn(buf("c_rows")[0:9, D:2 * D], buf("c_rows")[0:9, 0:D], ACT.Sigmoid), signal=c_sigmoid, at=1)
            take("par", par, bank("par")[:, 0:PAR_ROWS])
            take("c_t", buf("c_t"), bank("c_t")[:, 0:9 * KD])
            take("shift_t", buf("shift_t"), bank("shift_t")[:, 0:MS * NS])
            act.wait_ge(ada_ready, 1)
            for t in range(NT):
                for u in range(2):
                    for k in range(4):
                        m = 4 * u + k
                        take(f"x{t}_{u}", h_t[:, m, P * t:P * (t + 1)], bank(f"x{t}_{u}")[:, P * k:P * (k + 1)],
                             ACT.Identity, last=k == 3, scale=ada_t[:, 8 + m, 8:9], bias=ada_t[:, m, 8:9])
            bias = blocks("bias", H)
            for u in range(4):
                t, h = u // 2, 4 * (u % 2)
                take(f"bias{u}", bias[:, h:h + 4, P * t:P * (t + 1)],
                     bank(f"bias{u}")[:, :].rearrange("p (h s) -> p h s", h=4))
            end_phase(act, LOAD)

            take("qs", buf("qs")[0:8, :], bank("qs")[0:8, :])
            for c in range(NC):
                take(f"q{c}", q_t[:, c, :], bank(f"q{c}")[:, :], scale=SCALE)
            for b in range(NS):
                take(f"qb{b}", qb[:, b, :], bank(f"qb{b}")[:, :], scale=SCALE)
            take("ks", buf("ks")[0:8, :], bank("ks")[0:8, :])
            for c in range(NC):
                take(f"k{c}", k_t[:, c, :], bank(f"k{c}")[:, :])
            take("vs", buf("vs")[0:8, :], bank("vs")[0:8, :])
            for t in range(NT):
                take(f"v{t}", v_rows[:, t, :], bank(f"v{t}")[:, :])
            act.wait_ge(forget_in, 32)
            take("f", f[0:8, 0:T], bank("f")[0:8, :], ACT.Identity, bias=buf("bf")[0:8, 0:1])
            take("fs", f[0:8, T:TT], bank("fs")[0:8, 0:8])
            for m in range(MS):
                o = bank(f"z{m}")
                take(f"z{m}", mix[:, m, 0:T], o[:, :], last=False, scale=one_minus_mu[:, m:m + 1])
                take(f"z{m}", prev[:, m, 1:T], o[:, 0:T - 1], last=False, scale=param("mu_shift", m, m + 1))
                take(f"z{m}", z9[:, m, 8:9], o[:, T - 1:T])
            take("zs", z9[:, :, 0:8], bank("zs")[:, 0:MS * NS].rearrange("p (m b) -> p m b", m=MS))
            for u in range(4):
                n = min(4, MS - 4 * u) * P
                if u:
                    act.wait_ge(shift_stored, u)
                take(f"shift{u}", buf("shift_out")[0:9, 0:n], bank(f"shift{u}")[0:9, 0:n])
            for t in range(NT):
                if t:
                    act.wait_ge(krows_out, t)
                take(f"krows{t}", buf("k_rows"), bank(f"krows{t}")[:, :])
            act.wait_ge(f_abs, 1)
            link(fn(f2[0:8, 0:TT], f2[0:8, 0:TT], ACT.Exp))
            link(fn(f2[0:8, 0:TT], f2[0:8, 0:TT], ACT.Ln, bias=1.0), signal=f_log, at=1)
            take("logf", buf("logf_out"), bank("logf")[:, 0:NT * H])
            end_phase(act, PROJ)

            act.wait_ge(shifted, 1)
            link(fn(buf("scores"), buf("scores"), ACT.Exp))
            link(fn(sm(329, 393), sm(329, 393), ACT.Exp), signal=exps_ready, at=1)
            act.wait_ge(proj_stored, 1)
            end_phase(act, SAMPLE)

            stat = buf("rowstat")
            for i in range(NT * H + 2):
                if i < NT * H:
                    n = P * (i // H + 1)
                    act.wait_ge(row_max, i + 1)
                    if i >= 2:
                        full(act, f"pt{i - 2}")
                    take(f"qk{i}", probs[:, i % 2, 0:n], bank(f"qk{i}")[:, 0:n], ACT.Exp, bias=stat[:, i:i + 1],
                         accum_out=stat[:, NT * H + i:NT * H + i + 1])
                if 1 <= i <= NT * H:
                    n = P * ((i - 1) // H + 1)
                    take(f"pt{i - 1}", probs_t[:, (i - 1) % 2, 0:n], bank(f"pt{i - 1}")[:, 0:n])
                if i >= 2 and (i - 2) % H == H - 1:
                    t = (i - 2) // H
                    take(f"o{t}", b_out[:, :, P * t:P * (t + 1)], bank(f"o{t}")[:, :].rearrange("p (c q) -> p c q", c=NC))
            end_phase(act, FOX)

            link(fn(mix[0:64, 12, :], mix[0:64, 12, :], ACT.Tanh), signal=lora_ready, at=1)
            link(fn(mix[:, 13, :], mix[:, 13, :], ACT.Sigmoid), signal=lora_ready, at=2)
            lo = bank("lora_s")
            for c in range(NC):
                take("lora_s", sig[:, c, T:TT], lo[:, NS * c:NS * (c + 1)], ACT.Sigmoid, last=False,
                     bias=param("w0", c, c + 1))
            for c in range(NC):
                take("iclr_s", iclr[:, c, T:TT], bank("iclr_s")[:, NS * c:NS * (c + 1)], ACT.Sigmoid, last=c == NC - 1,
                     bias=param("a0", c, c + 1))
            take("lora_s", gate[:, :, T:TT], lo[:, 2 * NC * NS:3 * NC * NS].rearrange("p (c b) -> p c b", c=NC))
            for c in range(NC):
                take(f"dec{c}", sig[:, c, 0:T], bank(f"dec{c}")[:, :], ACT.Sigmoid, bias=param("w0", c, c + 1))
            for c in range(NC):
                take(f"iclr{c}", iclr[:, c, 0:T], bank(f"iclr{c}")[:, :], ACT.Sigmoid, bias=param("a0", c, c + 1))
            for c in range(NC):
                take(f"gate{c}", gate[:, c, 0:T], bank(f"gate{c}")[:, :])
            act.wait_ge(norm_ready, 1)
            link(fn(buf("t1"), buf("t1"), ACT.Sqrt), signal=pre_acts, at=1)
            act.wait_ge(logs_ready, 1)
            link(fn(buf("sig"), buf("sig"), ACT.Exp, scale=-DECAY), signal=pre_acts, at=2)
            act.wait_ge(logs_ready, 2)
            link(fn(buf("sig"), buf("iclr"), ACT.Exp, scale=-DECAY))
            link(fn(buf("iclr"), buf("iclr"), ACT.Exp, scale=DECAY), signal=pre_acts, at=3)
            end_phase(act, PRE)

            for i in range(6):
                take(f"svec{i}", buf("snat")[0:8, W * i:W * (i + 1)], bank(f"svec{i}")[0:8, :])
            end_phase(act, STATE)

            take("so", o_t[:, :, T:TT], bank("so")[:, 0:NC * NS].rearrange("p (c b) -> p c b", c=NC))
            for gp in range(NG):
                chunks = (2 * gp, 2 * gp + 1)
                for n in chunks:
                    take(f"bk{n}", bkn[:, n % 2, :, :], bank(f"bk{n}")[:, :].rearrange("p (c x) -> p c x", c=NC))
                for m in (range(0, 3) if gp == 0 else range(2 * gp + 1, 2 * gp + 3)):
                    o = bank(f"vw{m}")[:, :].rearrange("p (c e i) -> p c e i", c=NC, e=2)
                    pairs = uv.rearrange("p s (c e) i -> p s c e i", e=2)
                    if m < NCH:
                        take(f"vw{m}", pairs[C:P, m % 3, :, 0, :], o[C:P, :, 0, :], last=m == 0)
                    if m:
                        take(f"vw{m}", pairs[0:C, (m - 1) % 3, :, 1, :], o[0:C, :, 1, :])
                for lv in range(LEVELS):
                    take(f"iy{gp}_{lv}", buf("y"), bank(f"iy{gp}_{lv}")[:, :])
                for n in chunks:
                    take(f"r{n}", buf("r_sb"), bank(f"r{n}")[:, 0:NC * C])
                    take(f"oc{n}", o_t[:, :, C * n:C * (n + 1)], bank(f"oc{n}")[:, 0:NC * C].rearrange("p (c t) -> p c t", c=NC))
            vo = bank("vo")[:, 0:NS * H].rearrange("p (b c e) -> p c e b", b=NS, e=2)
            for e in range(2):
                take("vo", b_out[C * e:C * (e + 1), :, T:TT], vo[C * e:C * (e + 1), :, e, :], last=e == 1)
            act.wait_ge(wkv_stored, 1)
            take("state", buf("y")[0:64, 0:512], bank("state")[0:64, :])
            act.wait_ge(wkv_stored, 2)
            end_phase(act, CHAIN)

            act.wait_ge(dev_ready, 1)
            link(fn(buf("n2"), buf("n1"), ACT.Square), signal=dev_squares, at=1)
            for c in range(NC):
                take(f"var{c}", n2[:, c, 0:T], bank(f"var{c}")[:, :], ACT.Sqrt, scale=1.0 / HD, bias=eps[:, 1:2])
            take("var_s", n2[:, :, T:TT], bank("var_s")[:, 0:NC * NS].rearrange("p (c b) -> p c b", c=NC),
                 ACT.Sqrt, scale=1.0 / HD, bias=eps[:, 1:2])
            sgs = buf("sgs")
            for i, br in enumerate("AB"):
                for m in range(KD):
                    if m >= 2:
                        read(act, f"u{br}{m - 2}")
                    elif br == "B":
                        read(act, f"uA{KD - 2 + m}")
                    take(f"g{br}{m}", sg[:, m % 2, 0:T], bank(f"g{br}{m}")[:, :], ACT.Sigmoid)
                if br == "B":
                    read(act, "usA")
                take(f"gs{br}", sgs, bank(f"gs{br}")[:, 0:KD * NS], ACT.Sigmoid)
            end_phase(act, MIX)

            take("keys", buf("key_t"), bank("keys")[:, 0:2 * P])
            for j in range(8):
                take(f"ab{j}", bc[:, j // 2, 512 * (j % 2):512 * (j % 2 + 1)], bank(f"ab{j}")[:, :])

            def root(n, count):
                act.wait_ge(var_ready, count)
                link(fn(stats[0:n, 14:15], stats[0:n, 13:14], ACT.Sqrt, bias=eps[0:n, 0:1]), signal=root_ready, at=count)

            for t in range(NT + 1):
                root(P if t < NT else NS, t + 1)
            for t in range(NT):
                for u in range(2):
                    take(f"h2{t}_{u}", h2_t[:, 4 * u:4 * u + 4, P * t:P * (t + 1)],
                         bank(f"h2{t}_{u}")[:, :].rearrange("p (k x) -> p k x", k=4))
            take("h2s", h2_t[:, :, T:TT], bank("h2s")[:, 0:KD * NS].rearrange("p (k b) -> p k b", k=KD))
            end_phase(act, OUT)

            for m in range(16):
                take(f"pq{m}", qp[:, m, 0:T], bank(f"pq{m}")[:, :])
            take("pqs", qp[:, :, T:TT], bank("pqs")[:, 0:16 * NS].rearrange("p (m b) -> p m b", m=16))
            end_phase(act, QUERY)

            def key_scores(t):
                n = P if t < NT else NS
                if t:
                    act.wait_ge(top_done, t)
                for gg in range(4):
                    take(f"s{t}_{gg}", buf("ta")[0:n, 512 * gg:512 * (gg + 1)], bank(f"s{t}_{gg}")[0:n, :])

            def gate_exp(t):
                n = P if t < NT else NS
                act.wait_ge(gate_ready, t + 1)
                link(fn(coef[0:n, t, :], coef[0:n, t, :], ACT.Exp), signal=gate_exps, at=t + 1)

            key_scores(0)
            gate_exp(0)
            for t in range(NT):
                key_scores(t + 1)
                act.wait_ge(gelu_arg, t + 1)
                link(fn(gelu[:, 0:SLOTS], gelu[:, 0:SLOTS], ACT.Tanh, scale=0.7978845608028654), signal=gelu_tanh, at=t + 1)
                gate_exp(t + 1)
                act.wait_ge(coef_ready, t + 1)
                use = 16 * (2 * t + 1)
                with act.Fori(0, SLOTS // RING) as i:
                    for j in range(RING):
                        act.wait_ge(row_free[j], i + (use + 2))
                        link_free = fn(diag[:, j, :], ident, ACT.Copy, scale=coef_cols[:, ds(i * RING + (t * SLOTS + j), 1)])
                        link_free.then_inc(diag_made[j], 1)
                root(P, NT + 1 + t + 1)
            act.wait_ge(gelu_arg, NT + 1)
            link(fn(gelu[:, 0:NS], gelu[:, 0:NS], ACT.Tanh, scale=0.7978845608028654), signal=gelu_tanh, at=NT + 1)
            root(NS, 2 * NT + 2)

        @block.vector
        def _(dve):
            link = make_link(dve, vector_step)
            tt, ts, stt = nc.vector.tensor_tensor, nc.vector.tensor_scalar, nc.vector.scalar_tensor_tensor
            red = nc.vector.tensor_reduce
            MUL, ADD, SUB, MAX, MIN = ALU.mult, ALU.add, ALU.subtract, ALU.max, ALU.min

            def along(x, shape, *axes):
                for a in axes:
                    x = x.unsqueeze(a)
                return x.to_broadcast(shape)

            link(nc.vector.memset(eps[:, 0:1], LN_EPS))
            link(nc.vector.memset(eps[:, 1:2], GN_EPS))
            dve.wait_ge(c_sigmoid, 1)
            link(tt(buf("c_rows")[0:9, 0:D], buf("c_rows")[0:9, 0:D], buf("c_rows")[0:9, D:2 * D], MUL),
                 signal=silu_ready, at=1)
            read(dve, "par")
            link(ts(one_minus_mu, param("mu_shift"), -1.0, 1.0, MUL, ADD))
            link(ts(one_minus_ka, param("k_a"), -1.0, 1.0, MUL, ADD))
            for j in range(4):
                full(dve, f"ada{j}")
                link(tt(ada_t[:, 4 * j:4 * j + 4, :], bank(f"ada{j}")[:, 0:36].rearrange("p (m b) -> p m b", m=4),
                        along(param("b_ada", 4 * j, 4 * j + 4), [P, 4, 9], 2), ADD), job=f"ada{j}")
            link(nc.vector.tensor_scalar_add(ada_t[:, 8:16, :], ada_t[:, 8:16, :], 1.0), signal=ada_ready, at=1)
            full(dve, "xs")
            link(tt(h_t[:, :, T:TT], bank("xs")[:, 0:KD * NS].rearrange("p (k b) -> p k b", k=KD), ada_t[:, 8:16, 0:8], MUL),
                 job="xs")
            link(tt(h_t[:, :, T:TT], h_t[:, :, T:TT], ada_t[:, 0:8, 0:8], ADD))
            dve.wait_ge(logf_in, 32)
            dve.wait_ge(consts_in, 32)
            prefix = blocks("prefix", 2 * H)
            for t in range(2):
                past = buf("logf_rows")[:, t * D:(t + 1) * D].rearrange("p (s h) -> p h s", h=H)
                for h in range(H):
                    link(nc.vector.tensor_tensor_scan(prefix[:, t * H + h, :], ones, past[:, h, :], 0.0, MUL, ADD))
            tot = buf("page_tot")
            link(nc.vector.tensor_copy(tot[:, 0:16], prefix[:, :, P - 1]), signal=prefix_ready, at=1)
            full(dve, "suffix")
            link(tt(tot[:, 16:32], bank("suffix")[:, 0:16], tot[:, 0:16], ADD), job="suffix")
            link(tt(prefix, along(tot[:, 16:32], [P, 2 * H, P], 2), prefix, SUB), signal=tot_ready, at=1)
            end_phase(dve, LOAD)

            for j in range(RING):
                dve.sem_inc(page_free[j], 1)
            read(dve, f"qb{NS - 1}")
            qflat = buf("qb")
            with dve.Fori(0, NS) as b:
                with dve.Fori(0, PAGES // RING) as gg:

                    def page_dot(j):
                        dve.wait_ge(page_loaded[j], b * 64 + gg * 16 + 16)
                        tt(pages[:, j, :], pages[:, j, :], qflat[:, ds(b * W, W)], MUL).then_inc(page_product, 1)

                    def page_sum(j):
                        dve.wait_ge(page_product, b * PAGES + gg * RING + (j + 1))
                        red(scores[:, :, ds(b * PAGES + gg * RING + j, 1)].rearrange("p h o -> p (h o)"),
                            pages[:, j, :].rearrange("p (h d) -> p h d", h=H), AX.X, ADD).then_inc(page_free[j], 1)

                    page_dot(0)
                    for j in range(1, RING):
                        page_dot(j)
                        page_sum(j - 1)
                    page_sum(RING - 1)
            for j in range(RING):
                dve.wait_ge(page_free[j], 33)
            read(dve, "fs")
            link(tt(f[0:8, T:TT], f[0:8, T:TT], buf("bf")[0:8, 8:16], ADD))
            link(stt(f2[0:8, 0:TT], f[0:8, 0:TT], -1.0, f[0:8, 0:TT], MUL, MIN), signal=f_abs, at=1)
            dve.wait_ge(f_log, 1)
            link(stt(f[0:8, 0:TT], f[0:8, 0:TT], 0.0, f2[0:8, 0:TT], MIN, SUB), signal=logf_ready, at=1)
            read(dve, "zs")
            link(nc.vector.memset(prev[:, :, 0:1], 0.0))
            link(tt(prev[:, :, T:TT], blocks("shift_t", MS), along(param("mu_shift"), [P, MS, NS], 2), MUL))
            link(tt(mix[:, :, T:TT], z9[:, :, 0:8], along(one_minus_mu, [P, MS, NS], 2), MUL))
            link(tt(buf("mix"), buf("mix"), buf("prev"), ADD))
            end_phase(dve, PROJ)

            s8 = buf("small")[0:8, :]
            link(tt(buf("qs")[0:8, :], buf("qs")[0:8, :], buf("ks")[0:8, :], MUL))
            link(red(s8[:, 0:8], buf("qs")[0:8, :].rearrange("p (h d) -> p h d", h=H), AX.X, ADD))
            link(stt(s8[:, 0:8], s8[:, 0:8], SCALE, f[0:8, T:TT], MUL, SUB))
            link(tt(s8[:, 8:72].rearrange("p (h b) -> p h b", h=H), along(s8[:, 0:8], [8, H, NS], 2),
                    along(ident[0:8, 0:8], [8, H, NS], 1), MUL), signal=snew_ready, at=1)
            full(dve, "s_new")
            link(nc.vector.tensor_copy(sm(72, 136), bank("s_new")[:, 0:64]), job="s_new")
            link(tt(buf("scores"), buf("scores"), buf("bias"), ADD))
            by_pair = buf("scores").rearrange("p (x g) -> p x g", g=PAGES)
            link(red(sm(136, 200), by_pair, AX.X, MAX))
            link(tt(sm(136, 200), sm(136, 200), sm(72, 136), MAX), signal=max_ready, at=1)
            full(dve, "max_t")
            link(red(sm(200, 201)[0:64, :], bank("max_t")[0:64, 0:P], AX.X, MAX), job="max_t")
            link(ts(sm(201, 265)[0:64, :], ident[0:64, 0:64], sm(200, 201)[0:64, :], None, MUL), signal=diag_ready, at=1)
            full(dve, "max_b")
            link(nc.vector.tensor_copy(sm(265, 329), bank("max_b")[:, 0:64]), job="max_b")
            link(tt(sm(329, 393), sm(72, 136), sm(265, 329), SUB))
            link(tt(by_pair, by_pair, along(sm(265, 329), [P, 64, PAGES], 2), SUB), signal=shifted, at=1)
            dve.wait_ge(exps_ready, 1)
            link(red(sm(393, 457), by_pair, AX.X, ADD), signal=sum_ready, at=1)
            full(dve, "sum_b")
            link(tt(sm(457, 521), bank("sum_b")[:, 0:64], sm(329, 393), ADD), job="sum_b")
            link(nc.vector.reciprocal(sm(457, 521), sm(457, 521)))
            link(tt(by_pair, by_pair, along(sm(457, 521), [P, 64, PAGES], 2), MUL))
            link(tt(sm(521, 585), sm(329, 393), sm(457, 521), MUL))
            link(tt(pn_rows[0:8], s8[:, 521:585].rearrange("p (h b) -> p b h", h=H), along(ident[0:8, 0:8], [8, NS, H], 2),
                    MUL))
            link(nc.vector.tensor_tensor_scan(f2[0:8, 0:T], ones[0:8, 0:1].to_broadcast([8, T]), f[0:8, 0:T], 0.0, MUL, ADD))
            link(ts(f2[0:8, 0:T], f2[0:8, 0:T], -1.0, None, MUL), signal=forget_sum, at=1)
            end_phase(dve, SAMPLE)

            stat = buf("rowstat")
            NR = NT * H
            for i in range(NR + 1):
                if i < NR:
                    full(dve, f"qk{i}")
                    link(red(stat[:, i:i + 1], bank(f"qk{i}")[:, 0:P * (i // H + 1)], AX.X, MAX, negate=True),
                         signal=row_max, at=i + 1)
                if i:
                    k, n = i - 1, P * ((i - 1) // H + 1)
                    read(dve, f"qk{k}")
                    link(nc.vector.reciprocal(stat[:, 2 * NR + k:2 * NR + k + 1], stat[:, NR + k:NR + k + 1]))
                    link(ts(probs[:, k % 2, 0:n], probs[:, k % 2, 0:n], stat[:, 2 * NR + k:2 * NR + k + 1], None, MUL),
                         signal=row_prob, at=i)
            end_phase(dve, FOX)

            R, K, V = mix[:, 0:NC, :], mix[:, NC:2 * NC, :], mix[:, 2 * NC:3 * NC, :]
            whole = [P, NC, TT]
            link(tt(kk, K, along(param("k_k"), whole, 2), MUL))
            link(tt(t1, kk, kk, MUL), signal=squares_ready, at=1)
            for c in range(NC):
                full(dve, f"norm{c}")
                link(ts(t1[:, c, 0:T], bank(f"norm{c}")[:, :], 1e-24, None, MAX), job=f"norm{c}")
            full(dve, "norm_s")
            link(ts(t1[:, :, T:TT], bank("norm_s")[:, 0:NC * NS].rearrange("p (c b) -> p c b", c=NC), 1e-24, None, MAX),
                 job="norm_s")
            read(dve, "gate3")
            link(nc.vector.tensor_copy(svec[:, 4, :, :], V[:, :, T:TT]), signal=norm_ready, at=1)
            dve.wait_ge(pre_acts, 1)
            link(nc.vector.reciprocal(t1, t1))
            link(tt(kk, kk, t1, MUL))
            link(tt(t1, kk, iclr, MUL))
            for c in range(NC):
                link(ts(iclr[:, c, :], iclr[:, c, :], param("k_a", c, c + 1), one_minus_ka[:, c:c + 1], MUL, ADD))
            link(tt(K, K, iclr, MUL))
            rkp = buf("bk")[:, 0:NC * TT].rearrange("p (c t) -> p c t", c=NC)
            link(tt(rkp, R, K, MUL))
            link(tt(rkp, rkp, along(param("r_k"), whole, 2), MUL), signal=rk_product, at=1)
            dve.wait_ge(consts_in, 48)
            for c in range(NC):
                link(nc.vector.tensor_tensor_scan(iclr[:, c, 0:T], const("reset"), sig[:, c, 0:T], 0.0, MUL, ADD))
            link(nc.vector.tensor_copy(iclr[:, :, T:TT], sig[:, :, T:TT]))
            link(tt(sig, iclr, sig, SUB), signal=logs_ready, at=1)
            dve.wait_ge(pre_acts, 2)

            def chunked(x, a=0, b=P):
                return x[a:b, :, 0:T].rearrange("p c (n t) -> p c n t", n=NCH)

            link(nc.vector.tensor_copy(svec[:, 1, :, :], kk[:, :, T:TT]))
            link(tt(rk[:, :, :, 0:C], chunked(kk), chunked(sig), MUL), signal=logs_ready, at=2)
            dve.wait_ge(pre_acts, 3)
            link(nc.vector.tensor_copy(svec[:, 0, :, :], sig[:, :, T:TT]))
            link(nc.vector.tensor_copy(svec[:, 2, :, :], t1[:, :, T:TT]))
            link(nc.vector.tensor_copy(svec[:, 3, :, :], K[:, :, T:TT]))
            link(nc.vector.tensor_copy(svec[:, 5, :, :], R[:, :, T:TT]))
            link(nc.vector.tensor_copy(lam, chunked(sig)[:, :, :, C - 1]))
            link(tt(rk[:, :, :, C:P], chunked(R), chunked(sig), MUL))
            full(dve, "bonus_s")
            for a, first, second in ((0, t1, K), (C, K, t1)):
                link(tt(bk[a:a + C, :, :, 0:C], chunked(first, a, a + C), chunked(iclr, a, a + C), MUL))
                link(tt(bk[a:a + C, :, :, C:P], chunked(second, a, a + C), chunked(iclr, a, a + C), MUL))
            for c in range(NC):
                full(dve, f"bonus{c}")
                link(tt(R[:, c, 0:T], bank(f"bonus{c}")[:, :], V[:, c, 0:T], MUL), job=f"bonus{c}")
            link(tt(R[:, :, T:TT], bank("bonus_s")[:, 0:NC * NS].rearrange("p (c b) -> p c b", c=NC), V[:, :, T:TT], MUL),
                 job="bonus_s")
            end_phase(dve, PRE)

            dve.wait_ge(state_in, 16)
            dve.wait_ge(heads_in, 48)
            S = buf("wkv").rearrange("p (i j) -> p i j", j=HD)
            X = buf("wkv_tmp").rearrange("p (i j) -> p i j", j=HD)
            sh = blocks("shead", 6)
            sv, half = buf("svalue"), [P, 32, HD]
            link(tt(X, S, along(sh[:, 1, :], half, 1), MUL))
            link(red(buf("so_col"), X, AX.X, ADD))
            link(tt(S, S, along(sh[:, 0, :], half, 1), MUL))
            link(tt(X, along(buf("so_col"), half, 2), along(sh[:, 2, :], half, 1), MUL))
            link(tt(S, S, X, SUB))
            link(tt(X, along(sv, half, 2), along(sh[:, 3, :], half, 1), MUL))
            link(tt(S, S, X, ADD), signal=wkv_ready, at=1)
            link(tt(X, S, along(sh[:, 5, :], half, 1), MUL))
            link(red(buf("so_col"), X, AX.X, ADD), signal=wkv_ready, at=2)
            dve.wait_ge(heads_out, 32)
            end_phase(dve, STATE)

            dve.wait_ge(wkv_stored, 1)
            removed = uv.rearrange("p s (c e) i -> p s c e i", e=2)
            for a in (0, C):
                link(nc.vector.memset(removed[a:a + C, :, :, a // C, :], 0.0))
            link(nc.vector.memset(buf("state"), 0.0), signal=state_ready, at=1)
            gmask = const("gmask")
            levels = const("levels").rearrange("p (l t) -> p l t", l=LEVELS)
            for gp in range(NG):
                chunks = (2 * gp, 2 * gp + 1)
                for n in chunks:
                    for u in range(2):
                        full(dve, f"gm{n}_{u}")
                        link(tt(g[:, n % 2, u:H:2, :], bank(f"gm{n}_{u}")[:, :].rearrange("p (h x) -> p h x", h=4),
                                along(gmask, [P, 4, P], 1), MUL), job=f"gm{n}_{u}")
                for x in (inv, inv_t):
                    for a in (0, C):
                        link(nc.vector.tensor_copy(x[a:a + C], along(ident[a:a + C, a:a + C], [C, 2 * NC, C], 1)))
                for lv in range(LEVELS):
                    if lv:
                        full(dve, f"iy{gp}_{lv - 1}")
                    for a in (0, C):
                        mats = g[a:a + C].rearrange("p n (c e) x -> p (n c) e x", e=2)[:, :, a // C, 0:C]
                        link(tt(xt[a:a + C], mats, along(levels[a:a + C, lv, :], [C, 2 * NC, C], 1), MUL),
                             signal=xt_ready, at=2 * (gp * LEVELS + lv) + 1 + a // C)
                    if lv < LEVELS - 1:
                        full(dve, f"inv{gp}_{lv}")
                        link(tt(buf("inv"), buf("inv"), bank(f"inv{gp}_{lv}")[:, :], SUB), job=f"inv{gp}_{lv}")
                    full(dve, f"invt{gp}_{lv}")
                    link(tt(buf("inv_t"), buf("inv_t"), bank(f"invt{gp}_{lv}")[:, :], SUB), job=f"invt{gp}_{lv}")
                for n in chunks:
                    full(dve, f"u{n}")
                    o = bank(f"u{n}")[:, 0:NC * C].rearrange("p (c i) -> p c i", c=NC)
                    pairs = uv.rearrange("p s (c e) i -> p s c e i", e=2)
                    link(ts(pairs[0:C, n % 3, :, 0, :], o[0:C], -1.0, None, MUL))
                    link(ts(pairs[C:P, n % 3, :, 1, :], o[C:P], -1.0, None, MUL), job=f"u{n}")
                    full(dve, f"st{n}")
                    link(tt(buf("state"), buf("state"), bank(f"st{n}")[:, 0:NC * C], ADD), job=f"st{n}")
                    if n + 3 < NCH:
                        for a in (0, C):
                            link(nc.vector.memset(removed[a:a + C, n % 3, :, a // C, :], 0.0))
                    link(tt(state, state, along(lam[:, :, n], [P, NC, C], 2), MUL), signal=state_ready, at=n + 2)
            end_phase(dve, CHAIN)

            for c in range(NC):
                full(dve, f"mean{c}")
                link(stt(n1[:, c, 0:T], bank(f"mean{c}")[:, :], -1.0 / HD, o_t[:, c, 0:T], MUL, ADD), job=f"mean{c}")
            full(dve, "mean_s")
            link(stt(n1[:, :, T:TT], bank("mean_s")[:, 0:NC * NS].rearrange("p (c b) -> p c b", c=NC), -1.0 / HD,
                     o_t[:, :, T:TT], MUL, ADD), job="mean_s")
            dve.sem_inc(dev_ready, 1)
            read(dve, "var_s")
            link(nc.vector.reciprocal(n2, n2))
            link(tt(n1, n1, n2, MUL))
            for c in range(NC):
                link(ts(n1[:, c, :], n1[:, c, :], param("ln_x_w", c, c + 1), param("ln_x_b", c, c + 1), MUL, ADD))
            link(tt(n1, n1, R, ADD))
            link(tt(o_t, n1, gate, MUL), signal=a_ready, at=1)
            for br in "AB":
                for m in range(KD):
                    read(dve, f"g{br}{m}")
                    full(dve, f"u{br}{m}")
                    o = bank(f"u{br}{m}")[:, :]
                    if br == "A":
                        link(tt(mixed[:, m, 0:T], sg[:, m % 2, 0:T], o, MUL), job=f"uA{m}")
                    else:
                        link(tt(sg[:, m % 2, 0:T], sg[:, m % 2, 0:T], o, MUL))
                        link(tt(mixed[:, m, 0:T], mixed[:, m, 0:T], sg[:, m % 2, 0:T], ADD), job=f"uB{m}")
                read(dve, f"gs{br}")
                full(dve, f"us{br}")
                sgs = blocks("sgs", KD)
                o = bank(f"us{br}")[:, 0:KD * NS].rearrange("p (k b) -> p k b", k=KD)
                if br == "A":
                    link(tt(mixed[:, :, T:TT], sgs, o, MUL), job="usA")
                else:
                    link(tt(sgs, sgs, o, MUL))
                    link(tt(mixed[:, :, T:TT], mixed[:, :, T:TT], sgs, ADD), job="usB")
            end_phase(dve, MIX)

            dve.wait_ge(an_in, 16)
            for j in range(8):
                full(dve, f"an{j}")
                part = an[0:9, 512 * j:512 * (j + 1)]
                if j // 2 == 2:
                    link(tt(part, part, bank(f"an{j}")[0:9, :], ADD))
                    link(nc.vector.tensor_scalar_add(part, part, 1.0), job=f"an{j}")
                else:
                    link(tt(part, part, bank(f"an{j}")[0:9, :], ADD), job=f"an{j}")
            link(nc.vector.tensor_copy(buf("g2s")[0:8, :], an[0:8, 3 * D:4 * D]))
            dve.wait_ge(x2_in, 32)
            dve.wait_ge(lng_in, 64)
            norms = [0]

            def layer_norm(x, n, i):
                norms[0] += 1
                for u in range(2):
                    link(nc.vector.bn_stats(stats[0:n, 6 * u:6 * u + 6], x[:, 512 * u:512 * (u + 1)]))
                link(nc.vector.bn_aggr(stats[0:n, 12:14], stats[0:n, 0:12]), signal=var_ready, at=norms[0])
                dve.wait_ge(root_ready, norms[0])
                link(nc.vector.reciprocal(stats[0:n, 15:16], stats[0:n, 14:15]))
                link(ts(x, x, stats[0:n, 12:13], stats[0:n, 15:16], SUB, MUL))
                link(tt(x, x, lng[0:n, i, :], MUL))
                return tt(x, x, lng[0:n, i + 1, :], ADD)

            def mod(i, t, n):
                return bc[:, i, :] if t < NT else an[0:8, i * D:(i + 1) * D]

            read(dve, "ab7")
            for u in range(2):
                for t in range(NT + 1):
                    n = P if t < NT else NS
                    full(dve, f"wo{u}_{t}")
                    part = slice(512 * u, 512 * (u + 1))
                    link(tt(x1[0:n, t, part], bank(f"wo{u}_{t}")[0:n, :], mod(0, t, n)[:, part], MUL), job=f"wo{u}_{t}")
            for t in range(NT + 1):
                n = P if t < NT else NS
                x0 = buf("x2")[:, t * D:(t + 1) * D] if t < NT else buf("xs2")[0:8, :]
                link(stt(x1[0:n, t, :], x0, ALPHA, x1[0:n, t, :], MUL, ADD))
                link(layer_norm(x1[0:n, t, :], n, 0))
                link(tt(h2[0:n, t, :], x1[0:n, t, :], mod(2, t, n), MUL))
                link(tt(h2[0:n, t, :], h2[0:n, t, :], mod(1, t, n), ADD), signal=h2_ready, at=t + 1)
            end_phase(dve, OUT)
            end_phase(dve, QUERY)

            for j in range(RING):
                dve.sem_inc(row_free[j], 2)
            dve.sem_inc(dots_kept, 1)
            link(nc.vector.memset(zero, 0.0), signal=zero_ready, at=1)
            top = buf("top")
            t1v = top[:, 0:256].rearrange("p (m k) -> p m k", m=16)
            ti = top[:, 256:512].bitcast(U32).rearrange("p (m k) -> p m k", m=16)
            tif = top[:, 512:768].rearrange("p (h e k) -> p h e k", h=PH, e=2)
            cv = top[:, 768:896].rearrange("p (h k) -> p h k", h=PH)
            cp = top[:, 896:1024].bitcast(U32).rearrange("p (h k) -> p h k", h=PH)
            pos = [top[:, 1024 + 128 * i:1152 + 128 * i] for i in range(2)]
            posf = [top[:, 1280 + 128 * i:1408 + 128 * i] for i in range(2)]
            ssum, smax = top[:, 1536:1544], top[:, 1544:1552]

            def top16(n, values, indices, src, spare):
                num = src.shape[1]
                for i in range(num):
                    link(nc.vector.max(values[0:n, i, 0:8], src[:, i, :]))
                for i in range(num):
                    link(nc.vector.max_index(indices[0:n, i, 0:8], values[0:n, i, 0:8], src[:, i, :]))
                for i in range(num):
                    link(nc.vector.match_replace(spare[:, i, :], values[0:n, i, 0:8], src[:, i, :], LOW))
                for i in range(num):
                    link(nc.vector.max(values[0:n, i, 8:16], spare[:, i, :]))
                for i in range(num):
                    link(nc.vector.max_index(indices[0:n, i, 8:16], values[0:n, i, 8:16], spare[:, i, :]))

            def choose(t):
                n = P if t < NT else NS
                read(dve, f"s{t}_3")
                ta = buf("ta")[0:n, :]
                tb = buf("tb")[0:n, :]
                top16(n, t1v, ti, ta.rearrange("p (m k) -> p m k", m=16), tb.rearrange("p (m k) -> p m k", m=16))
                pair = t1v[0:n].rearrange("p (h e) k -> p h e k", e=2)
                grid = [n, PH, TOP, TOP]
                link(tt(ta.rearrange("p (h i j) -> p h i j", h=PH, i=TOP), along(pair[:, :, 0, :], grid, 3),
                        along(pair[:, :, 1, :], grid, 2), ADD))
                top16(n, cv, cp, ta.rearrange("p (h x) -> p h x", h=PH), tb.rearrange("p (h x) -> p h x", h=PH))
                cpf = top[0:n, 896:1024].bitcast(U32)
                link(ts(pos[0][0:n].bitcast(U32), cpf, 4, None, ALU.logical_shift_right))
                link(ts(pos[1][0:n].bitcast(U32), cpf, TOP - 1, None, ALU.bitwise_and))
                link(nc.vector.tensor_copy(top[0:n, 512:768], top[0:n, 256:512].bitcast(U32)))
                for e in range(2):
                    link(nc.vector.tensor_copy(posf[e][0:n], pos[e][0:n].bitcast(U32)))
                    hit = tb.rearrange("p (x i) -> p x i", i=TOP)
                    link(tt(hit, along(posf[e][0:n], [n, SLOTS, TOP], 2), along(iota[0:n], [n, SLOTS, TOP], 1), ALU.is_equal))
                    hit4 = tb.rearrange("p (h x i) -> p h x i", h=PH, x=TOP)
                    link(tt(hit4, hit4, along(tif[0:n, :, e, :], grid, 2), MUL))
                    link(red(posf[e][0:n], hit, AX.X, ADD))
                link(stt(idx_f[0:n], posf[0][0:n], float(KEYS), posf[1][0:n], MUL, ADD))
                link(nc.vector.tensor_copy(idx_u[0:n, t * SLOTS:(t + 1) * SLOTS], idx_f[0:n]))
                gate_t = coef[0:n, t, :].rearrange("p (h k) -> p h k", h=PH)
                link(nc.vector.tensor_copy(smax[0:n], cv[0:n, :, 0]), signal=top_done, at=t + 1)
                link(tt(gate_t, cv[0:n], along(smax[0:n], [n, PH, TOP], 2), SUB), signal=gate_ready, at=t + 1)
                dve.wait_ge(gate_exps, t + 1)
                link(red(ssum[0:n], gate_t, AX.X, ADD))
                link(nc.vector.reciprocal(ssum[0:n], ssum[0:n]))
                link(tt(gate_t, gate_t, along(ssum[0:n], [n, PH, TOP], 2), MUL),
                     signal=idx_ready if t < NT else top_s_ready, at=t + 1 if t < NT else 1)

            def gelu_times_gate(x, y, gate_x, count):
                link(tt(y, x, x, MUL))
                link(ts(y, y, 0.044715, 1.0, MUL, ADD))
                link(tt(y, y, x, MUL), signal=gelu_arg, at=count)
                dve.wait_ge(gelu_tanh, count)
                link(stt(y, y, 1.0, x, ADD, MUL))
                return lambda out: stt(out, y, 0.5, gate_x, MUL, MUL)

            def output(t, n):
                for u in range(2):
                    part = slice(512 * u, 512 * (u + 1))
                    job = f"y{t}_{u}" if t < NT else f"ys_{u}"
                    full(dve, job)
                    g2 = bc[:, 3, part] if t < NT else buf("g2s")[0:8, part]
                    link(tt(h2[0:n, t, part], bank(job)[0:n, :], g2, MUL), job=job)
                link(stt(h2[0:n, t, :], x1[0:n, t, :], ALPHA, h2[0:n, t, :], MUL, ADD))
                link(layer_norm(h2[0:n, t, :], n, 2), signal=y_ready, at=t + 1)

            choose(0)
            dot = gelu[:, 2 * SLOTS:2 * SLOTS + 2 * RING]
            for t in range(NT):
                use = 16 * 2 * t
                with dve.Fori(0, SLOTS // (2 * RING)) as i:
                    for gg in range(2):
                        for j in range(RING):
                            dve.wait_ge(row_in[j], i * 32 + 16 * (use + gg + 1))
                            if gg == 0 and j == 0:
                                dve.wait_ge(dots_kept, i + (8 * t + 1))
                            at = RING * gg + j
                            nc.vector.tensor_tensor_reduce(
                                out=gathered[:, j, :], in0=gathered[:, j, :], in1=h2[:, t, :], scale=1.0, scalar=0.0,
                                op0=MUL, op1=ADD, accum_out=dot[:, at:at + 1]).then_inc(row_free[j], 1)
                    for j in range(RING):
                        dve.wait_ge(row_free[j], i * 2 + (use + 4))
                    nc.vector.tensor_copy(gelu[:, ds(i * (2 * RING) + SLOTS, 2 * RING)], dot).then_inc(dots_kept, 1)
                dve.wait_ge(dots_kept, 8 * (t + 1) + 1)
                done = gelu_times_gate(gelu[:, SLOTS:2 * SLOTS], gelu[:, 0:SLOTS], coef[:, t, :], t + 1)
                link(done(coef[:, t, :]), signal=coef_ready, at=t + 1)
                choose(t + 1)
                if t == NT - 1:
                    full(dve, "tg")
                    link(nc.vector.tensor_copy(idx_s, bank("tg")[:, 0:NS]), signal=idx_ready, at=NT + 1)
                output(t, P)
            link(nc.vector.tensor_copy(gelu[:, 16:24], bank("tg")[:, NS:2 * NS]), job="tg")
            use = 16 * 2 * NT
            for b in range(NS):
                dve.wait_ge(row_in[b], 16 * (use + 1))
                for u in range(2):
                    full(dve, f"hb{b}_{u}")
                    part = slice(512 * u, 512 * (u + 1))
                    at = 24 + 2 * b + u
                    link(nc.vector.tensor_tensor_reduce(
                        out=bc[:, 0, part], in0=gathered[:, b, part], in1=bank(f"hb{b}_{u}")[:, :], scale=1.0,
                        scalar=0.0, op0=MUL, op1=ADD, accum_out=gelu[:, at:at + 1]), job=f"hb{b}_{u}")
                dve.sem_inc(row_free[b], 1)
            pairs = gelu[:, 24:40].rearrange("p (b u) -> p b u", u=2)
            link(tt(gelu[:, 8:16], pairs[:, :, 0], pairs[:, :, 1], ADD))
            done = gelu_times_gate(gelu[:, 8:16], gelu[:, 0:8], gelu[:, 16:24], NT + 1)
            link(done(gelu[:, 16:24]))
            link(tt(coef_s, along(gelu[:, 16:24], [P, NS, NS], 2), eye, MUL),
                 signal=coef_s_ready, at=1)
            output(NT, NS)


INPUTS = ["x_prompt", "x_sample", "cache_k", "cache_v", "cache_logf", "state_wkv", "state_shift", "page_table",
          "c_prompt", "c_sample", "w_ada", "b_ada", "w_in", "mu_shift", "w0", "w2_decay", "a0", "a2_iclr", "g2_gate",
          "k_k", "k_a", "r_k", "ln_x_w", "ln_x_b", "b_forget", "w_up_a", "w_up_b", "w_o", "ln1_g", "ln1_b",
          "peer_wq", "peer_keys1", "peer_keys2", "peer_u", "peer_v", "ln2_g", "ln2_b"]
OUTPUT_SHAPES = [(1, T, D), (NS, 1, D), (1, 1, T, H, HD), (1, 1, T, H, HD), (1, 1, T, H), (1, 1, H, HD, HD),
                 (1, 1, SHIFT), (1, NS, 1, H, HD), (1, NS, 1, H, HD), (1, NS, 1, H), (1, NS, H, HD, HD), (1, NS, SHIFT)]


def kernel(**inputs):
    import concourse.bacc as bacc
    from concourse.bass_utils import run_bass_kernel_spmd

    nc = bacc.Bacc("TRN2", target_bir_lowering=False, num_devices=1)
    arrays, args = {}, []
    for name in INPUTS:
        a = np.ascontiguousarray(inputs[name])
        arrays[f"in_{name}"] = a
        args.append(nc.dram_tensor(f"in_{name}", a.shape, mybir.dt.from_np(a.dtype), kind="ExternalInput").ap())
    arrays["in_constants"] = constants()
    args.append(nc.dram_tensor("in_constants", (P, CONST_COLS), mybir.dt.float32, kind="ExternalInput").ap())
    args.append(nc.dram_tensor("scratch_heads", (6, NS, W), mybir.dt.float32, kind="Internal").ap())
    args.append(nc.dram_tensor("scratch_out", (NS, W), mybir.dt.float32, kind="Internal").ap())
    for i, shape in enumerate(OUTPUT_SHAPES):
        args.append(nc.dram_tensor(f"out_{i}", shape, mybir.dt.float32, kind="ExternalOutput").ap())
    hybrid_step(nc, *args)
    r = run_bass_kernel_spmd(nc, [arrays], core_ids=[0])
    return tuple(r.results[0][f"out_{i}"] for i in range(len(OUTPUT_SHAPES)))
```

```python
from contextlib import ExitStack

import numpy as np

import concourse.bass as bass
from concourse import mybir

P = 128
D = 1024
KD = D // P
T = 512
NT = T // P
NS = 8
TT = T + NS
H = 8
HD = 64
W = H * HD
NC = W // P
SHIFT = 3 * W + 64 + 64 + 128
MS = SHIFT // P
QCOL, KCOL, VCOL, FCOL = SHIFT, SHIFT + W, SHIFT + 2 * W, SHIFT + 3 * W
GCOL = FCOL + H
IN_COLS = GCOL + 2 * D
PAGES = 32
PAGE = 128
POOL = 320
RING = 8
C = 64
NCH = T // C
NG = NCH // 2
LEVELS = 6
PH = 8
KEYS = 128
TOP = 16
SLOTS = PH * TOP
ALPHA = 2.0 ** 0.25
LN_EPS = 1e-5
GN_EPS = 64e-5
DECAY = float(np.exp(-0.5))
SCALE = HD ** -0.5
NEG = -1.0e30
LOW = -3.0e38

CONST = {}
_at = 0
for _name, _n in [("ident", P), ("ones", P), ("rows", (NS + 1) * P), ("iota", TOP), ("eye", NS * NS),
                  ("causal", P), ("suffix", P),
                  ("headones", P), ("gmask", P), ("levels", LEVELS * C), ("reset", T)]:
    CONST[_name] = (_at, _n)
    _at += _n
CONST_COLS = _at
CONST_B = CONST["causal"][0]
CONST_C = CONST["headones"][0]

PAR = {}
_at = 0
for _name, _n in [("mu_shift", MS), ("w0", NC), ("a0", NC), ("k_k", NC), ("k_a", NC), ("r_k", NC),
                  ("ln_x_w", NC), ("ln_x_b", NC), ("b_ada", 16)]:
    PAR[_name] = (_at, _n)
    _at += _n
PAR_ROWS = _at


def constants():
    c = np.zeros((P, CONST_COLS), np.float32)
    p = np.arange(P)

    def put(name, value):
        at, n = CONST[name]
        c[:value.shape[0], at:at + n] = value

    put("ident", np.eye(P))
    put("headones", (p[:, None] // HD == p[None, :] // HD) * 1.0)
    put("ones", np.ones((P, P)))
    put("causal", np.where(p[None, :] <= p[:, None], 0.0, NEG))
    s, t = (p % C)[:, None], np.arange(C)[None, :]
    put("gmask", np.concatenate([s < t, s <= t], 1) * 1.0)
    put("suffix", ((p[:, None] // PAGES == p[None, :] // PAGES) & (p[:, None] > p[None, :])) * 1.0)
    lv = []
    for n in range(LEVELS):
        b = 2 ** n
        lv.append((s // (2 * b) == t // (2 * b)) & (s % (2 * b) < b) & (t % (2 * b) >= b))
    put("levels", np.concatenate(lv, 1) * 1.0)
    put("reset", np.broadcast_to((np.arange(T) % C != 0) * 1.0, (P, T)))
    rows = np.zeros((NS + 1, NS + 1, P))
    for n in range(NS + 1):
        rows[n, n] = 1.0
    put("rows", rows.reshape(NS + 1, (NS + 1) * P))
    put("eye", np.broadcast_to(np.eye(NS).reshape(1, NS * NS), (P, NS * NS)))
    put("iota", np.broadcast_to(np.arange(TOP) * 1.0, (P, TOP)))
    return c


(LOAD, PROJ, SAMPLE, FOX, PRE, STATE, CHAIN, MIX, OUT, QUERY, PEER) = range(11)


def place_buffers(buffers, limit):
    placed = {}
    for name, n, a, b in sorted(buffers, key=lambda x: -(x[1] + 1200 * (x[3] - x[2]) + 2000 * (x[2] <= PRE <= x[3]))):
        at, moved = 0, True
        while moved:
            moved = False
            for o, (oat, on, oa, ob) in placed.items():
                if not (b < oa or ob < a) and at < oat + on and oat < at + n:
                    at, moved = oat + on, True
        placed[name] = (at, n, a, b)
        assert at + n <= limit, (name, at + n, limit)
    return placed


BUFFERS = [
    ("const", CONST_B, LOAD, PEER), ("const_b", CONST_C - CONST_B, LOAD, FOX),
    ("const_c", CONST_COLS - CONST_C, PRE, MIX), ("par", PAR_ROWS + 24, LOAD, MIX), ("c_t", KD * 9, LOAD, PRE),
    ("stats", 16, LOAD, PEER), ("eps", 2, LOAD, PEER),
    ("x_rows", NT * D, LOAD, LOAD), ("xs_rows", D, LOAD, LOAD), ("c_rows", 2 * D, LOAD, LOAD),
    ("par_rows", P, LOAD, LOAD), ("shift_rows", SHIFT, LOAD, LOAD), ("shift_t", MS * NS, LOAD, PROJ),
    ("logf_rows", 2 * D, LOAD, LOAD), ("prefix", 2 * D, LOAD, LOAD), ("page_tot", 64, LOAD, LOAD),
    ("ada_t", 16 * 9, LOAD, PROJ), ("ada_rows", 2 * 512, LOAD, LOAD), ("h_t", KD * TT, LOAD, MIX), ("w_f", KD * H, LOAD, PROJ),
    ("wring0", 4096, LOAD, QUERY), ("wring1", 4096, LOAD, QUERY),
    ("mix", MS * TT, PROJ, MIX), ("prev", MS * TT, PROJ, PROJ), ("z9", MS * 9, PROJ, PROJ),
    ("shift_out", 512, PROJ, SAMPLE),
    ("q_t", NC * T, PROJ, FOX), ("k_t", NC * T, PROJ, FOX), ("v_rows", NT * W, PROJ, FOX),
    ("k_rows", W, PROJ, SAMPLE), ("f", TT, PROJ, FOX), ("f2", TT, PROJ, FOX), ("logf_out", NT * H, PROJ, SAMPLE),
    ("qs", W, PROJ, SAMPLE), ("ks", W, PROJ, SAMPLE), ("vs", W, PROJ, CHAIN), ("bf", 16, LOAD, PROJ),
    ("qb", NS * W, PROJ, SAMPLE), ("pages", RING * W, PROJ, CHAIN), ("scores", H * 256, PROJ, CHAIN),
    ("bias", H * 256, LOAD, SAMPLE), ("small", 649, SAMPLE, CHAIN),
    ("probs", 2 * T, FOX, FOX), ("probs_t", 2 * T, FOX, FOX), ("rowstat", 3 * NT * H, FOX, FOX),
    ("b_out", NC * TT, FOX, MIX),
    ("lora", 512 * 2, LOAD, PRE),
    ("bk", NC * NCH * P, PRE, CHAIN), ("rk", NC * NCH * P, PRE, CHAIN), ("kk", NC * TT, PRE, PRE),
    ("sig", NC * TT, PRE, PRE), ("iclr", NC * TT, PRE, PRE), ("t1", NC * TT, PRE, PRE),
    ("svec", 6 * NC * NS, PRE, STATE), ("snat", 6 * W, STATE, STATE), ("shead", 6 * HD, STATE, STATE),
    ("wkv", 2048, STATE, STATE), ("wkv_tmp", 2048, STATE, STATE), ("gate", NC * TT, PRE, MIX), ("lam", NC * NCH, PRE, CHAIN),
    ("so_rows", W, STATE, MIX), ("vm", 2 * W, CHAIN, CHAIN),
    ("g", 2 * H * P, CHAIN, CHAIN), ("bkn", 2 * NC * P, CHAIN, CHAIN), ("uv", 3 * W, CHAIN, CHAIN),
    ("inv", 2 * NC * C, CHAIN, CHAIN), ("inv_t", 2 * NC * C, CHAIN, CHAIN), ("y", 2 * NC * C, CHAIN, CHAIN),
    ("xt", 2 * NC * C, CHAIN, CHAIN), ("r_sb", NC * C, CHAIN, CHAIN), ("state", NC * C, CHAIN, CHAIN),
    ("o_t", NC * TT, CHAIN, MIX),
    ("n1", NC * TT, MIX, MIX), ("n2", NC * TT, MIX, MIX), ("mixed", KD * TT, MIX, OUT), ("sg", 2 * TT, MIX, MIX),
    ("sgs", KD * NS, MIX, MIX),
    ("x2", NT * D, OUT, OUT), ("xs2", D, OUT, OUT), ("an", 4 * D, MIX, OUT), ("bc", 4 * D, MIX, PEER),
    ("bb", 4 * D, MIX, MIX), ("an_rows", 2 * 512, PRE, PRE),
    ("lng", 4 * D, OUT, PEER), ("x1", 5 * D, OUT, PEER), ("h2", 5 * D, OUT, PEER), ("g2s", D, OUT, PEER),
    ("h2_t", KD * TT, OUT, QUERY), ("key_t", 2 * P, OUT, PEER), ("key_rows", 2 * P, OUT, OUT),
    ("qp", 16 * TT, QUERY, PEER), ("ta", 2048, QUERY, PEER), ("tb", 2048, QUERY, PEER),
    ("idx", 5 * SLOTS, QUERY, PEER), ("coef", 5 * SLOTS, QUERY, PEER), ("top", 1552, QUERY, PEER),
    ("rows", RING * D, PEER, PEER), ("diag", RING * P, PEER, PEER), ("stage", 4 * RING, PEER, PEER),
    ("ids_row", NS * PAGES, LOAD, CHAIN), ("ids_col", 2, LOAD, LOAD), ("svalue", 32, STATE, STATE),
    ("so_col", 32, STATE, STATE), ("idx_f", SLOTS, QUERY, PEER), ("idx_s", NS, PEER, PEER),
    ("coef_s", NS * NS, PEER, PEER), ("zero", P, PEER, PEER), ("gelu", 288, PEER, PEER),
]


def psum_jobs():
    jobs = []

    def ring(*names):
        jobs.extend((n, None) for n in names)

    def fixed(bank, name):
        jobs.append((name, bank))

    ring("c_t", "ada0", "par", "ada1", "adat0", "ada2", "adat1", "ada3", "adat2", "adat3")
    ring(*[f"x{t}_{u}" for t in range(NT) for u in range(2)], "xs", "shift_t", "suffix", *[f"bias{u}" for u in range(4)])
    ring("qs", *[f"q{c}" for c in range(NC)], *[f"qb{b}" for b in range(NS)])
    ring("ks", *[f"k{c}" for c in range(NC)], "vs", *[f"v{t}" for t in range(NT)], "f", "fs")
    ring(*[f"z{m}" for m in range(MS)])
    fixed(7, "zs")
    ring(*[f"shift{u}" for u in range(4)], *[f"krows{t}" for t in range(NT)], "logf")
    ring("s_new", "max_t", "max_b", "sum_b")
    for i in range(NT * H + 2):
        if i < NT * H:
            ring(f"qk{i}")
        if 1 <= i <= NT * H:
            ring(f"pt{i - 1}")
        if i >= 2 and (i - 2) % H == 0:
            fixed(6, f"o{(i - 2) // H}")
    fixed(7, "lora_s")
    fixed(6, "iclr_s")
    ring(*[f"{x}{c}" for x in ("dec", "iclr", "gate") for c in range(NC)])
    ring(*[f"norm{c}" for c in range(NC)], "norm_s", *[f"an{j}" for j in range(8)])
    ring(*[f"bonus{c}" for c in range(NC)], "bonus_s")
    ring(*[f"svec{i}" for i in range(6)], "so")
    for gp in range(NG):
        for n in (2 * gp, 2 * gp + 1):
            ring(f"bk{n}", f"gm{n}_0", f"gm{n}_1")
        for m in (range(0, 3) if gp == 0 else range(2 * gp + 1, 2 * gp + 3)):
            ring(f"vw{m}")
        if gp:
            ring(f"vt{gp - 1}")
        fixed(6, f"vo{2 * gp}")
        fixed(7, f"vo{2 * gp + 1}")
        for lv in range(LEVELS):
            ring(f"iy{gp}_{lv}", *([f"inv{gp}_{lv}"] if lv < LEVELS - 1 else []), f"invt{gp}_{lv}")
        for n in (2 * gp, 2 * gp + 1):
            ring(f"r{n}", f"u{n}", f"oc{n}", f"st{n}")
    ring("state", f"vt{NG - 1}")
    ring(*[f"mean{c}" for c in range(NC)], "mean_s", *[f"var{c}" for c in range(NC)], "var_s")
    for br in "AB":
        fixed(6, f"gs{br}")
        fixed(7, f"us{br}")
        ring(*[f"{x}{br}{m}" for m in range(KD) for x in ("g", "u")])
    ring("keys")
    ring(*[f"wo{u}_{t}" for u in range(2) for t in range(NT + 1)])
    ring(*[f"h2{t}_{u}" for t in range(NT) for u in range(2)], "h2s")
    fixed(7, "pqs")
    for m in range(16):
        ring(f"pq{m}")
        if m in (4, 8, 12, 15):
            ring(f"s0_{(m - 1) // 4}")
    for t in range(1, NT + 1):
        ring(*[f"s{t}_{g}" for g in range(4)])
    for t in range(NT):
        fixed(6, f"y{t}_0")
        fixed(7, f"y{t}_1")
    ring("tg", *[f"hb{b}_{u}" for b in range(NS) for u in range(2)])
    fixed(6, "ys_0")
    fixed(7, "ys_1")
    place, used, r = {}, [0] * 8, 0
    for name, bank in jobs:
        if bank is None:
            bank, r = r, (r + 1) % 6
        place[name] = (bank, used[bank])
        used[bank] += 1
    return place


def hybrid_step(nc, x_prompt, x_sample, cache_k, cache_v, cache_logf, state_wkv, state_shift, page_table,
                c_prompt, c_sample, w_ada, b_ada, w_in, mu_shift, w0, w2_decay, a0, a2_iclr, g2_gate,
                k_k, k_a, r_k, ln_x_w, ln_x_b, b_forget, w_up_a, w_up_b, w_o, ln1_g, ln1_b,
                peer_wq, peer_keys1, peer_keys2, peer_u, peer_v, ln2_g, ln2_b, consts, scratch, scratch_o, scratch_m,
                y_prompt, y_sample, new_k_prompt, new_v_prompt, new_logf_prompt, new_wkv_prompt, new_shift_prompt,
                new_k_sample, new_v_sample, new_logf_sample, new_wkv_sample, new_shift_sample):
    F32 = mybir.dt.float32
    I32 = mybir.dt.int32
    U32 = mybir.dt.uint32
    ALU = mybir.AluOpType
    ACT = mybir.ActivationFunctionType
    AX = mybir.AxisListType
    OFF = bass.IndirectOffsetOnAxis
    ds = bass.ds
    JOB = psum_jobs()
    limit = (nc.sbuf_usable_end - nc.sbuf_base - 64) // 4
    PLACE = place_buffers(BUFFERS, limit)

    ctx = ExitStack()
    with ctx:
        ctx.enter_context(nc.allow_non_contiguous_dma(reason="a page's index a partition"))
        arena = ctx.enter_context(nc.sbuf_tensor("arena", [P, limit], F32))
        bank_of = [ctx.enter_context(nc.psum_tensor(f"bank{i}", [P, 512], F32)) for i in range(8)]

        def sem(name):
            return ctx.enter_context(nc.semaphore(name))

        def buf(name):
            at, n, _, _ = PLACE[name]
            return arena[:, at:at + n]

        def const(name):
            at, n = CONST[name]
            part, base = ("const", 0) if at < CONST_B else ("const_b", CONST_B) if at < CONST_C else ("const_c", CONST_C)
            return buf(part)[:, at - base:at - base + n]

        ident, ones, iota = const("ident"), const("ones"), const("iota")
        rows = const("rows").rearrange("p (n q) -> p n q", n=NS + 1)
        eye = const("eye").rearrange("p (b t) -> p b t", b=NS)
        stats = buf("stats")
        par = buf("par")[:, 0:PAR_ROWS]
        par_more = buf("par")[:, PAR_ROWS:PAR_ROWS + 24]
        one_minus_mu, one_minus_ka = par_more[:, 0:MS], par_more[:, MS:MS + NC]

        def param(name, a=0, b=None):
            at, n = PAR[name]
            return par[:, at + a:at + (n if b is None else b)]

        def blocks(name, n):
            return buf(name).rearrange("p (n x) -> p n x", n=n)

        h_t = blocks("h_t", KD)
        c_t = blocks("c_t", KD)
        ada_t = blocks("ada_t", 16)
        mix = blocks("mix", MS)
        prev = blocks("prev", MS)
        z9 = blocks("z9", MS)
        q_t, k_t, v_rows = blocks("q_t", NC), blocks("k_t", NC), blocks("v_rows", NT)
        f, f2 = buf("f"), buf("f2")
        qb, pages = blocks("qb", NS), blocks("pages", RING)
        scores = blocks("scores", H)
        b_out = blocks("b_out", NC)
        wring = [buf("wring0"), buf("wring1")]

        def sm(a, b):
            return buf("small")[:, a:b]

        pn_rows = sm(585, 649).rearrange("p (b h) -> p b h", b=NS)
        probs, probs_t = blocks("probs", 2), blocks("probs_t", 2)
        kk, sig, iclr, t1, gate = (blocks(x, NC) for x in ("kk", "sig", "iclr", "t1", "gate"))
        bk = buf("bk").rearrange("p (c n x) -> p c n x", c=NC, n=NCH)
        rk = buf("rk").rearrange("p (c n x) -> p c n x", c=NC, n=NCH)
        lam = blocks("lam", NC)
        svec = buf("svec").rearrange("p (i c b) -> p i c b", i=6, c=NC)
        g = buf("g").rearrange("p (n h x) -> p n h x", n=2, h=H)
        bkn = buf("bkn").rearrange("p (n c x) -> p n c x", n=2, c=NC)
        uv = buf("uv").rearrange("p (s h i) -> p s h i", s=3, h=H)
        inv, inv_t, y, xt = (blocks(x, 2 * NC) for x in ("inv", "inv_t", "y", "xt"))
        r_sb, state, o_t = blocks("r_sb", NC), blocks("state", NC), blocks("o_t", NC)
        n1, n2, mixed, sg = blocks("n1", NC), blocks("n2", NC), blocks("mixed", KD), blocks("sg", 2)
        an, bc, lng = buf("an"), blocks("bc", 4), blocks("lng", 4)
        x1, h2, h2_t = blocks("x1", 5), blocks("h2", 5), blocks("h2_t", KD)
        key_t, qp = blocks("key_t", 2), blocks("qp", 16)
        idx_u, idx_f, idx_s = buf("idx").bitcast(U32), buf("idx_f"), buf("idx_s").bitcast(U32)
        coef, coef_cols = blocks("coef", 5), buf("coef")
        coef_s, zero, gelu, eps = blocks("coef_s", NS), buf("zero"), buf("gelu"), buf("eps")
        gathered, diag = blocks("rows", RING), blocks("diag", RING)

        bank_full = [sem(f"bank_full{i}") for i in range(8)]
        bank_free = [sem(f"bank_free{i}") for i in range(8)]
        phase_end = sem("phase_end")
        vector_step, scalar_step, pool_step = sem("vector_step"), sem("scalar_step"), sem("pool_step")
        consts_in, masks_in, x_in, c_in, par_in, shift_in = sem("consts_in"), sem("masks_in"), sem("x_in"), sem("c_in"), sem("par_in"), sem("shift_in")
        ids_in, forget_in, logf_in = sem("ids_in"), sem("forget_in"), sem("logf_in")
        w_in_slot = [sem("w_in_slot0"), sem("w_in_slot1")]
        wf_in, lora_in = sem("wf_in"), sem("lora_in")
        silu_ready, ada_ready, prefix_ready, tot_ready = sem("silu_ready"), sem("ada_ready"), sem("prefix_ready"), sem("tot_ready")
        prev_ready = sem("prev_ready")
        logf_ready = sem("logf_ready")
        krows_out, shift_stored = sem("krows_out"), sem("shift_stored")
        stored = sem("stored")
        page_loaded = [sem(f"page_loaded{j}") for j in range(RING)]
        page_free = [sem(f"page_free{j}") for j in range(RING)]
        page_seen = sem("page_seen")
        page_product = sem("page_product")
        snew_ready, max_ready, diag_ready, sum_ready, probs_ready = (
            sem("snew_ready"), sem("max_ready"), sem("diag_ready"), sem("sum_ready"), sem("probs_ready"))
        row_max, row_exp, row_prob = sem("row_max"), sem("row_exp"), sem("row_prob")
        proj_stored = sem("proj_stored")
        state_in = sem("state_in")
        heads_out = sem("heads_out")
        heads_in = sem("heads_in")
        wkv_ready = sem("wkv_ready")
        so_in = sem("so_in")
        wkv_stored = sem("wkv_stored")
        an_in = sem("an_in")
        mod_out = [sem("mod_out0"), sem("mod_out1")]
        key_in = sem("key_in")
        x2_in = sem("x2_in")
        lng_in = sem("lng_in")
        y_ready = sem("y_ready")
        idx_ready = sem("idx_ready")
        stage_tick = sem("stage_tick")
        stage_ready = sem("stage_ready")
        sort_tick = sem("sort_tick")
        forget_sum = sem("forget_sum")
        lora_ready = sem("lora_ready")
        squares_ready = sem("squares_ready")
        rk_product = sem("rk_product")
        xt_ready = sem("xt_ready")
        state_ready = sem("state_ready")
        a_ready = sem("a_ready")
        dev_squares = sem("dev_squares")
        h2_ready = sem("h2_ready")
        zero_ready = sem("zero_ready")
        top_s_ready = sem("top_s_ready")
        coef_s_ready = sem("coef_s_ready")
        c_sigmoid = sem("c_sigmoid")
        f_abs = sem("f_abs")
        f_log = sem("f_log")
        shifted = sem("shifted")
        exps_ready = sem("exps_ready")
        norm_ready = sem("norm_ready")
        pre_acts = sem("pre_acts")
        logs_ready = sem("logs_ready")
        dev_ready = sem("dev_ready")
        var_ready = sem("var_ready")
        root_ready = sem("root_ready")
        top_done = sem("top_done")
        gate_ready = sem("gate_ready")
        gate_exps = sem("gate_exps")
        gelu_arg = sem("gelu_arg")
        gelu_tanh = sem("gelu_tanh")
        coef_ready = sem("coef_ready")
        dots_kept = sem("dots_kept")
        row_in = [sem(f"row_in{j}") for j in range(RING)]
        row_free = [sem(f"row_free{j}") for j in range(RING)]
        diag_made = [sem(f"diag_made{j}") for j in range(RING)]
        OUTPUTS = [0]
        TURN = {-1: 0}
        for t in range(NT):
            TURN[t] = 16 + 32 * t
        TURN[NT] = TURN[NT - 1] + 16

        wada = w_ada.rearrange("l (k p) n -> (l p) k n", p=P)
        win = w_in.rearrange("l (k p) n -> (l p) k n", p=P)
        WEIGHTS = [(f"ada{j}", [(wada[:, :, 512 * j:512 * (j + 1)], 0, 512)]) for j in range(4)]
        WEIGHTS += [("q", [(win[:, :, QCOL:QCOL + W], 0, 512)]), ("k", [(win[:, :, KCOL:KCOL + W], 0, 512)]),
                    ("v", [(win[:, :, VCOL:VCOL + W], 0, 512)])]
        WEIGHTS += [(f"z{j}", [(win[:, :, 512 * j:min(512 * (j + 1), SHIFT)], 0, min(512, SHIFT - 512 * j))])
                    for j in range(4)]
        WEIGHTS += [(f"an{j}", [(wada[:, :, 2 * D + 512 * j:2 * D + 512 * (j + 1)], 0, 512)]) for j in range(8)]
        for br, up in (("A", w_up_a), ("B", w_up_b)):
            wup = up.rearrange("l (k p) n -> (l p) k n", p=P)
            g0 = GCOL + (D if br == "B" else 0)
            WEIGHTS += [(f"{br}{j}", [(win[:, :, g0 + 256 * j:g0 + 256 * (j + 1)], 0, 256),
                                      (wup[:, :, 256 * j:256 * (j + 1)], 2048, 256)]) for j in range(4)]
        wov = w_o.rearrange("l (k p) n -> (l p) k n", p=P)
        WEIGHTS += [(f"wo{j}", [(wov[:, :, 512 * j:512 * (j + 1)], 0, 512)]) for j in range(2)]
        wqv = peer_wq.rearrange("l (k p) n -> (l p) k n", p=P)
        WEIGHTS += [(f"wq{j}", [(wqv[:, :, 512 * j:512 * (j + 1)], 0, 512)]) for j in range(4)]
        WJOB = {name: i for i, (name, _) in enumerate(WEIGHTS)}

        def arrivals(i):
            return 16 * sum(len(parts) for j, (_, parts) in enumerate(WEIGHTS[:i + 1]) if j % 2 == i % 2)

        def slot(i, at, k, n):
            return wring[i % 2][:, at:at + k * n].rearrange("p (k n) -> p k n", k=k)

        def full(e, job):
            bank, n = JOB[job]
            e.wait_ge(bank_full[bank], n + 1)

        def read(e, job):
            bank, n = JOB[job]
            e.wait_ge(bank_free[bank], n + 1)

        def bank(job):
            return bank_of[JOB[job][0]]

        def make_link(e, step):
            count = [0]

            def link(ins, job=None, signal=None, at=None):
                if job is not None:
                    ins.then_inc(bank_free[JOB[job][0]], 1)
                    e.wait_ge(bank_free[JOB[job][0]], JOB[job][1] + 1)
                elif signal is not None:
                    ins.then_inc(signal, 1)
                    e.wait_ge(signal, at)
                else:
                    count[0] += 1
                    ins.then_inc(step, 1)
                    e.wait_ge(step, count[0])

            def in_loop(i, turns, per):
                first, k = count[0], [0]
                count[0] += turns * per

                def link_in_loop(ins, wait=True):
                    k[0] += 1
                    assert k[0] <= per
                    ins.then_inc(step, 1)
                    if wait:
                        e.wait_ge(step, i * per + (first + k[0]))

                return link_in_loop

            link.in_loop = in_loop
            return link

        def end_phase(e, phase):
            e.drain().then_inc(phase_end, 1)
            e.wait_ge(phase_end, 3 * (phase + 1))

        def col(name, n, i=0):
            return buf(name)[:, i:i + n]

        block = ctx.enter_context(nc.Block())

        last_use = {**{f"ada{j}": f"ada{j}" for j in range(4)}, "q": "q3", "k": "k3", "v": "v3",
                    **{f"z{j}": f"z{min(4 * j + 3, MS - 1)}" for j in range(4)},
                    **{f"{br}{j}": f"u{br}{2 * j + 1}" for br in "AB" for j in range(4)},
                    **{f"an{j}": f"an{j}" for j in range(8)}, **{f"wo{j}": f"wo{j}_{NT}" for j in range(2)},
                    **{f"wq{j}": f"pq{4 * j + 3}" for j in range(4)}}

        @block.sync
        def _(sp):
            def load(dst, src, signal):
                sp.dma_start(dst, src).then_inc(signal, 16)

            def store(dst, src):
                sp.dma_start(dst, src).then_inc(stored, 16)
                OUTPUTS[0] += 16

            def weights(*names):
                for name in names:
                    i = WJOB[name]
                    if i >= 2:
                        full(sp, last_use[WEIGHTS[i - 2][0]])
                    for src, at, n in WEIGHTS[i][1]:
                        load(slot(i, at, src.shape[1], n), src, w_in_slot[i % 2])

            load(buf("c_rows")[0:8, 0:D], c_sample[:, :], c_in)
            load(buf("c_rows")[8:9, 0:D], c_prompt[:, :], c_in)
            load(buf("ids_col").bitcast(I32), page_table.rearrange("(t b) g -> (b g) t", t=2), ids_in)
            load(buf("ids_row")[0:1, :].bitcast(I32), page_table.rearrange("(o b) g -> o (b g)", o=1), ids_in)
            load(buf("const"), consts[:, 0:CONST_B], consts_in)
            weights("ada0")
            load(buf("const_b"), consts[:, CONST_B:CONST_C], masks_in)
            for name, src in (("mu_shift", mu_shift), ("w0", w0), ("a0", a0), ("k_k", k_k), ("k_a", k_a),
                              ("r_k", r_k.rearrange("l h n -> l (h n)")), ("ln_x_w", ln_x_w), ("ln_x_b", ln_x_b),
                              ("b_ada", b_ada[:, 0:2 * D])):
                at, n = PAR[name]
                load(buf("par_rows")[at:at + n, :], src.rearrange("l (m p) -> (l m) p", p=P), par_in)
            weights("ada1")
            load(buf("x_rows").rearrange("p (t d) -> p t d", t=NT), x_prompt.rearrange("o (t p) d -> p (o t) d", p=P), x_in)
            load(buf("xs_rows")[0:8, :], x_sample.rearrange("b o d -> b (o d)"), x_in)
            load(buf("shift_rows")[0:8, :], state_shift.rearrange("l b n -> (l b) n"), shift_in)
            load(buf("bf")[0:8, 0:1], b_forget.rearrange("l h -> h l"), forget_in)
            load(buf("bf")[0:8, 8:16], b_forget.to_broadcast([8, H]), forget_in)
            load(buf("w_f").rearrange("p (k n) -> p k n", k=KD), win[:, :, FCOL:FCOL + H], wf_in)
            load(buf("lora")[0:64, 0:512], w2_decay.rearrange("l r n -> (l r) n"), lora_in)
            load(buf("lora")[64:128, 0:512], a2_iclr.rearrange("l r n -> (l r) n"), lora_in)
            load(buf("lora")[:, 512:1024], g2_gate.rearrange("l r n -> (l r) n"), lora_in)
            weights("ada2", "ada3", "q", "k", "v", "z0", "z1", "z2", "z3", "an0", "an1")
            for u in range(4):
                read(sp, f"shift{u}")
                n = min(4, MS - 4 * u) * P
                store(new_shift_sample.rearrange("l b n -> (l b) n")[:, 512 * u:512 * u + n], buf("shift_out")[0:8, 0:n])
                store(new_shift_prompt.rearrange("l b n -> (l b) n")[:, 512 * u:512 * u + n], buf("shift_out")[8:9, 0:n])
                sp.wait_ge(stored, OUTPUTS[0])
                sp.sem_inc(shift_stored, 1)
            nk = new_k_prompt.rearrange("l o (t p) h d -> p (l o t) (h d)", p=P)
            nv = new_v_prompt.rearrange("l o (t p) h d -> p (l o t) (h d)", p=P)
            for t in range(NT):
                read(sp, f"krows{t}")
                store(nk[:, t, :], buf("k_rows"))
                sp.wait_ge(stored, OUTPUTS[0])
                sp.sem_inc(krows_out, 1)
            store(nv, v_rows)
            read(sp, "logf")
            store(new_logf_prompt.rearrange("l o (t p) h -> p (l o t) h", p=P),
                  buf("logf_out").rearrange("p (t h) -> p t h", t=NT))
            store(new_k_sample.rearrange("l b o h d -> (l b o) (h d)"), buf("ks")[0:8, :])
            store(new_v_sample.rearrange("l b o h d -> (l b o) (h d)"), buf("vs")[0:8, :])
            store(new_logf_sample.rearrange("l b o h -> (l b o) h"), f[0:8, T:TT])
            sp.wait_ge(stored, OUTPUTS[0])
            sp.sem_inc(proj_stored, 1)
            sp.wait_ge(phase_end, 3 * (FOX + 1))
            load(buf("const_c"), consts[:, CONST_C:CONST_COLS], masks_in)
            for j in range(8):
                read(sp, f"an{j}")
                load(scratch_m[:, 512 * j:512 * (j + 1)], buf("an_rows")[0:9, 512 * (j % 2):512 * (j % 2 + 1)], mod_out[j % 2])
                weights(f"an{j + 2}" if j < 6 else f"A{j - 6}")
            sp.wait_ge(phase_end, 3 * (PRE + 1))
            load(buf("wkv"), state_wkv.rearrange("l b h (e i) j -> (l b h e) (i j)", e=2), state_in)
            for i in range(6):
                read(sp, f"svec{i}")
            load(scratch.rearrange("k b w -> b k w"), buf("snat")[0:8, :].rearrange("b (k w) -> b k w", k=6), heads_out)
            sp.wait_ge(heads_out, 16)
            heads = scratch.rearrange("k b (h n) -> (b h) k n", h=H)
            for e in range(2):
                load(buf("shead")[e:P:2, :].rearrange("p (k n) -> p k n", k=6), heads, heads_in)
            load(buf("svalue"), scratch[4, :, :].rearrange("b (h e n) -> (b h e) n", h=H, e=2), heads_in)
            sp.wait_ge(wkv_ready, 1)
            store(new_wkv_sample.rearrange("l b h (e i) j -> (l b h e) (i j)", e=2), buf("wkv"))
            sp.wait_ge(wkv_ready, 2)
            load(scratch_o.rearrange("b (h e n) -> (b h e) n", h=H, e=2), buf("so_col"), heads_out)
            sp.wait_ge(heads_out, 32)
            load(buf("so_rows")[0:8, :], scratch_o, so_in)
            sp.wait_ge(stored, OUTPUTS[0])
            sp.sem_inc(wkv_stored, 1)
            read(sp, "state")
            store(new_wkv_prompt.rearrange("l o h i j -> i (l o h) j"),
                  buf("y")[0:64, 0:512].rearrange("i (h j) -> i h j", h=H))
            sp.wait_ge(stored, OUTPUTS[0])
            sp.sem_inc(wkv_stored, 1)
            sp.wait_ge(phase_end, 3 * (CHAIN + 1))
            sp.wait_ge(mod_out[0], 4 * 16)
            sp.wait_ge(mod_out[1], 4 * 16)
            load(buf("bb"), b_ada[:, 2 * D:6 * D].to_broadcast([P, 4 * D]), an_in)
            load(buf("bc"), scratch_m[8:9, :].to_broadcast([P, 4 * D]), an_in)
            load(buf("an")[0:8, :], scratch_m[0:8, :], an_in)
            weights("A2", "A3", "B0", "B1", "B2", "B3", "wo0", "wo1")
            sp.wait_ge(phase_end, 3 * (MIX + 1))
            load(buf("key_rows")[:, 0:P], peer_keys1.rearrange("l n c -> (l n) c"), key_in)
            load(buf("key_rows")[:, P:2 * P], peer_keys2.rearrange("l n c -> (l n) c"), key_in)
            load(buf("x2").rearrange("p (t d) -> p t d", t=NT), x_prompt.rearrange("o (t p) d -> p (o t) d", p=P), x2_in)
            load(buf("xs2")[0:8, :], x_sample.rearrange("b o d -> b (o d)"), x2_in)
            for i, src in enumerate((ln1_g, ln1_b, ln2_g, ln2_b)):
                load(lng[:, i, :], src.to_broadcast([P, D]), lng_in)
            weights("wq0", "wq1", "wq2", "wq3")
            for t in range(NT + 1):
                sp.wait_ge(y_ready, t + 1)
                if t < NT:
                    store(y_prompt.rearrange("o (t p) d -> p (o t) d", p=P)[:, t, :], h2[:, t, :])
                else:
                    store(y_sample.rearrange("b o d -> b (o d)"), h2[0:8, NT, :])
            sp.wait_ge(stored, OUTPUTS[0])

        @block.gpsimd
        def _(pool):
            pool.wait_ge(ids_in, 32)
            pages_logf = cache_logf.rearrange("l n s h -> (l n) (s h)")
            for t in range(2):
                nc.gpsimd.indirect_dma_start(buf("logf_rows")[:, t * D:(t + 1) * D], None, pages_logf[:, :],
                                             OFF(ap=buf("ids_col")[:, t:t + 1].bitcast(U32), axis=0)).then_inc(logf_in, 16)
            pool.wait_ge(phase_end, 3 * (LOAD + 1))
            ids = buf("ids_row")[0:1, :].bitcast(I32)
            for past, cache in enumerate((cache_k, cache_v)):
                rows_of = cache.rearrange("l n s h d -> (l n) s (h d)")
                with pool.Fori(0, NS) as b:
                    with pool.Fori(0, PAGES // RING) as g:
                        for j in range(RING):
                            page = pool.value_load(ids[:, ds(b * PAGES + g * RING + j, 1)], min_val=0, max_val=POOL - 1)
                            pool.wait_ge(page_free[j], b * 4 + g + (1 + 32 * past))
                            pool.sem_inc(page_seen, 1)
                            pool.dma_start(pages[:, j, :], rows_of[ds(page, 1), :, :].rearrange("o p d -> (o p) d"))\
                                .then_inc(page_loaded[j], 16)
            link = make_link(pool, pool_step)
            tables = (peer_u.rearrange("l e d -> (l e) d"), peer_v.rearrange("l e d -> (l e) d"))
            stage = buf("stage").bitcast(U32)
            pool.wait_ge(phase_end, 3 * (QUERY + 1))
            staged = [0]

            def experts(first, passes):
                n = len(passes)
                with pool.Fori(0, SLOTS // TOP) as i:
                    for half in range(2):
                        for k, (t, kind) in enumerate(passes):
                            nc.gpsimd.tensor_copy(
                                stage[:, 2 * RING * half + k:2 * RING * half + k + (RING - 1) * n + 1:n],
                                idx_u[:, ds(i * TOP + (t * SLOTS + half * RING), RING)]).then_inc(stage_ready, 1)
                        pool.wait_ge(stage_ready, i * (2 * n) + (staged[0] + n * (half + 1)))
                        for x in range(RING * n):
                            pool.wait_ge(row_free[x % RING], i * (2 * n) + (first + n * half + x // RING + 2))
                            pool.sem_inc(stage_tick, 1)
                            nc.gpsimd.indirect_dma_start(
                                gathered[:, x % RING, :], None, tables[passes[x % n][1]][:, :],
                                OFF(ap=stage[:, 2 * RING * half + x:2 * RING * half + x + 1], axis=0))\
                                .then_inc(row_in[x % RING], 16)
                staged[0] += 2 * n * (SLOTS // TOP)

            pool.wait_ge(idx_ready, 1)
            experts(TURN[-1], [(0, 0)])
            for t in range(NT - 1):
                pool.wait_ge(idx_ready, t + 2)
                experts(TURN[t], [(t + 1, 0), (t, 1)])
            experts(TURN[NT - 1], [(NT - 1, 1)])
            pool.wait_ge(idx_ready, NT + 1)
            for kind in range(2):
                use = TURN[NT] + kind
                for b in range(NS):
                    pool.wait_ge(row_free[b], use + 2)
                    nc.gpsimd.indirect_dma_start(gathered[:, b, :], None, tables[kind][:, :],
                                                 OFF(ap=idx_s[:, b:b + 1], axis=0)).then_inc(row_in[b], 16)

        @block.tensor
        def _(pe):
            mm = nc.tensor.matmul

            def begin(job):
                b, n = JOB[job]
                if n:
                    pe.wait_ge(bank_free[b], n)
                return bank_of[b]

            def end(ins, job):
                ins.then_inc(bank_full[JOB[job][0]], 1)

            def weight(name, k, n, at=0):
                i = WJOB[name]
                pe.wait_ge(w_in_slot[i % 2], arrivals(i))
                return slot(i, at, k, n)

            def product(out, pairs, **more):
                for i, (a, b) in enumerate(pairs):
                    ins = mm(out, a, b, start=i == 0, stop=i == len(pairs) - 1, **more)
                return ins

            def turn(out, in_):
                n = in_.shape[0]
                at = in_.start_partition if isinstance(in_.start_partition, int) else in_.start_partition()
                return nc.tensor.transpose(out, in_, ident[at:at + n, at:at + n])

            pe.wait_ge(consts_in, 16)
            pe.wait_ge(silu_ready, 1)
            o = begin("c_t")
            for k in range(KD):
                ins = turn(o[:, 9 * k:9 * k + 9], buf("c_rows")[0:9, P * k:P * (k + 1)])
            end(ins, "c_t")
            read(pe, "c_t")

            def turn_ada(j):
                read(pe, f"ada{j}")
                o = begin(f"adat{j}")
                for m in range(4):
                    ins = turn(o[:, 9 * m:9 * m + 9], buf("ada_rows")[0:9, 512 * (j % 2) + P * m:512 * (j % 2) + P * (m + 1)])
                end(ins, f"adat{j}")

            for j in range(4):
                w = weight(f"ada{j}", KD, 512)
                end(product(begin(f"ada{j}")[0:9, :], [(c_t[:, k, :], w[:, k, :]) for k in range(KD)]), f"ada{j}")
                if j:
                    turn_ada(j - 1)
                else:
                    pe.wait_ge(par_in, 16 * len(PAR))
                    end(turn(begin("par")[:, 0:PAR_ROWS], buf("par_rows")[0:PAR_ROWS, :]), "par")
            turn_ada(3)
            pe.wait_ge(x_in, 32)
            for t in range(NT):
                for u in range(2):
                    o = begin(f"x{t}_{u}")
                    for k in range(4):
                        at = t * D + (4 * u + k) * P
                        ins = turn(o[:, P * k:P * (k + 1)], buf("x_rows")[:, at:at + P])
                    end(ins, f"x{t}_{u}")
            o = begin("xs")
            for k in range(KD):
                ins = turn(o[:, NS * k:NS * (k + 1)], buf("xs_rows")[0:8, P * k:P * (k + 1)])
            end(ins, "xs")
            pe.wait_ge(shift_in, 16)
            o = begin("shift_t")
            for m in range(MS):
                ins = turn(o[:, NS * m:NS * (m + 1)], buf("shift_rows")[0:8, P * m:P * (m + 1)])
            end(ins, "shift_t")
            pe.wait_ge(masks_in, 16)
            pe.wait_ge(prefix_ready, 1)
            end(product(begin("suffix")[:, 0:16], [(const("suffix"), buf("page_tot")[:, 0:16])]), "suffix")
            pe.wait_ge(tot_ready, 1)
            for u in range(4):
                o = begin(f"bias{u}")
                for i in range(4):
                    at = (4 * u + i) * P
                    ins = turn(o[:, P * i:P * (i + 1)], buf("prefix")[:, at:at + P])
                end(ins, f"bias{u}")
            end_phase(pe, LOAD)

            hs = [h_t[:, k, T:TT] for k in range(KD)]
            hp = [h_t[:, k, 0:T] for k in range(KD)]

            def rows_s(job, w):
                end(product(begin(job)[0:8, 0:w.shape[2]], [(hs[k], w[:, k, :]) for k in range(KD)]), job)

            def columns(job, w, m):
                end(product(begin(job)[:, :], [(w[:, k, P * m:P * (m + 1)], hp[k]) for k in range(KD)]), job)

            w = weight("q", KD, W)
            rows_s("qs", w)
            for c in range(NC):
                columns(f"q{c}", w, c)
            read(pe, "qs")
            for b in range(NS):
                end(product(begin(f"qb{b}")[:, :], [(rows[0:8, b, :], buf("qs")[0:8, :])]), f"qb{b}")
            w = weight("k", KD, W)
            rows_s("ks", w)
            for c in range(NC):
                columns(f"k{c}", w, c)
            w = weight("v", KD, W)
            rows_s("vs", w)
            for t in range(NT):
                end(product(begin(f"v{t}")[:, :], [(h_t[:, k, P * t:P * (t + 1)], w[:, k, :]) for k in range(KD)]), f"v{t}")
            pe.wait_ge(wf_in, 16)
            w = blocks("w_f", KD)
            end(product(begin("f")[0:8, :], [(w[:, k, :], hp[k]) for k in range(KD)]), "f")
            rows_s("fs", w)
            zs = begin("zs")
            for m in range(MS):
                w = weight(f"z{m // 4}", KD, min(512, SHIFT - 512 * (m // 4)))
                a = P * (m % 4)
                product(zs[:, NS * m:NS * (m + 1)], [(w[:, k, a:a + P], hs[k]) for k in range(KD)])
                columns(f"z{m}", w, m % 4)
            pe.drain().then_inc(bank_full[7], 1)
            read(pe, "zs")
            for u in range(4):
                o = begin(f"shift{u}")
                for i in range(min(4, MS - 4 * u)):
                    ins = turn(o[0:9, P * i:P * (i + 1)], z9[:, 4 * u + i, :])
                end(ins, f"shift{u}")
            for t in range(NT):
                o = begin(f"krows{t}")
                for c in range(NC):
                    ins = turn(o[:, P * c:P * (c + 1)], k_t[:, c, P * t:P * (t + 1)])
                end(ins, f"krows{t}")
            pe.wait_ge(logf_ready, 1)
            o = begin("logf")
            for t in range(NT):
                ins = turn(o[:, H * t:H * (t + 1)], f[0:8, P * t:P * (t + 1)])
            end(ins, "logf")
            end_phase(pe, PROJ)

            pe.wait_ge(snew_ready, 1)
            end(product(begin("s_new")[:, 0:64], [(ones[0:8, :], sm(8, 72)[0:8, :])]), "s_new")
            pe.wait_ge(max_ready, 1)
            end(turn(begin("max_t")[0:64, 0:P], sm(136, 200)), "max_t")
            pe.wait_ge(diag_ready, 1)
            end(product(begin("max_b")[:, 0:64], [(ones[0:64, :], sm(201, 265)[0:64, :])]), "max_b")
            pe.wait_ge(sum_ready, 1)
            end(product(begin("sum_b")[:, 0:64], [(ones, sm(393, 457))]), "sum_b")
            end_phase(pe, SAMPLE)

            pe.wait_ge(forget_sum, 1)
            for i in range(NT * H + 2):
                if i < NT * H:
                    t, h = divmod(i, H)
                    n, a, c = P * (t + 1), HD * (h % 2), h // 2
                    o = begin(f"qk{i}")
                    mm(o[:, 0:n], q_t[a:a + HD, c, P * t:P * (t + 1)], k_t[a:a + HD, c, 0:n], start=True, stop=False)
                    mm(o[:, 0:n], rows[0:8, h, :], f2[0:8, 0:n], start=False, stop=False)
                    end(mm(o[:, n - P:n], ident, const("causal"), start=False, stop=True), f"qk{i}")
                if 1 <= i <= NT * H:
                    t = (i - 1) // H
                    pe.wait_ge(row_prob, i)
                    o = begin(f"pt{i - 1}")
                    for k in range(t + 1):
                        ins = turn(o[:, P * k:P * (k + 1)], probs[:, (i - 1) % 2, P * k:P * (k + 1)])
                    end(ins, f"pt{i - 1}")
                if i >= 2:
                    t, h = divmod(i - 2, H)
                    a, c = HD * (h % 2), h // 2
                    if h == 0:
                        o6 = begin(f"o{t}")
                    read(pe, f"pt{i - 2}")
                    ins = product(o6[a:a + HD, P * c:P * (c + 1)],
                                  [(v_rows[:, k, HD * h:HD * (h + 1)], probs_t[:, i % 2, P * k:P * (k + 1)])
                                   for k in range(t + 1)])
                    if h == H - 1:
                        end(ins, f"o{t}")
            end_phase(pe, FOX)

            lora = buf("lora")
            pe.wait_ge(lora_in, 48)
            pe.wait_ge(lora_ready, 2)
            kinds = [(lora[0:64, 0:512], mix[0:64, 12, :]), (lora[64:128, 0:512], mix[64:128, 12, :]),
                     (lora[:, 512:1024], mix[:, 13, :])]
            o = begin("lora_s")
            for i in (0, 2):
                w, x = kinds[i]
                for c in range(NC):
                    at = (NC * i + c) * NS
                    ins = mm(o[:, at:at + NS], w[:, P * c:P * (c + 1)], x[:, T:TT], start=True, stop=True)
            end(ins, "lora_s")
            o = begin("iclr_s")
            w, x = kinds[1]
            for c in range(NC):
                ins = mm(o[:, NS * c:NS * (c + 1)], w[:, P * c:P * (c + 1)], x[:, T:TT], start=True, stop=True)
            end(ins, "iclr_s")
            for name, (w, x) in zip(("dec", "iclr", "gate"), kinds):
                for c in range(NC):
                    end(mm(begin(f"{name}{c}")[:, :], w[:, P * c:P * (c + 1)], x[:, 0:T], start=True, stop=True), f"{name}{c}")
            pe.wait_ge(masks_in, 32)

            def head_sums(name, src):
                for c in range(NC):
                    end(mm(begin(f"{name}{c}")[:, :], const("headones"), src[:, c, 0:T], start=True, stop=True), f"{name}{c}")
                end(mm(begin(f"{name}_s")[:, 0:NC * NS], const("headones"), src[:, :, T:TT], start=True, stop=True), f"{name}_s")

            pe.wait_ge(squares_ready, 1)
            head_sums("norm", t1)
            for j in range(8):
                w = weight(f"an{j}", KD, 512)
                end(product(begin(f"an{j}")[0:9, :], [(c_t[:, k, :], w[:, k, :]) for k in range(KD)]), f"an{j}")
            pe.wait_ge(rk_product, 1)
            head_sums("bonus", buf("bk")[:, 0:NC * TT].rearrange("p (c t) -> p c t", c=NC))
            end_phase(pe, PRE)

            for i in range(6):
                o = begin(f"svec{i}")
                for c in range(NC):
                    ins = turn(o[0:8, P * c:P * (c + 1)], svec[:, i, c, :])
                end(ins, f"svec{i}")
            end_phase(pe, STATE)

            pe.wait_ge(so_in, 16)
            o = begin("so")
            for c in range(NC):
                ins = turn(o[:, NS * c:NS * (c + 1)], buf("so_rows")[0:8, P * c:P * (c + 1)])
            end(ins, "so")
            vflat = buf("mix")

            def channels(gp):
                o = begin(f"vt{gp}")
                for n in (2 * gp, 2 * gp + 1):
                    read(pe, f"vo{n}")
                    for c in range(NC):
                        at = 2 * ((n % 2) * NC + c)
                        ins = mm(o[:, at:at + 2], buf("vm")[0:8, W * (n % 2) + P * c:W * (n % 2) + P * (c + 1)],
                                 ident[0:8, 2 * c:2 * c + 2], start=True, stop=True)
                end(ins, f"vt{gp}")

            def page_values(gp, point, points):
                for k in range(2 * PAGES * point // points, 2 * PAGES * (point + 1) // points):
                    n, pg = 2 * gp + k // PAGES, k % PAGES
                    if pg == 0:
                        begin(f"vo{n}")
                    vo = bank(f"vo{n}")[0:8, :]
                    if pg == 0:
                        mm(vo, pn_rows[0:8, n, :], buf("vs")[0:8, :], start=True, stop=False)
                    j = pg % RING
                    pe.wait_ge(page_loaded[j], 16 * (32 + 4 * n + pg // RING + 1))
                    mm(vo, scores[:, :, n * PAGES + pg], pages[:, j, :],
                       start=False, stop=pg == PAGES - 1).then_inc(page_free[j], 1)
                    if pg == PAGES - 1:
                        pe.drain().then_inc(bank_full[JOB[f"vo{n}"][0]], 1)

            for gp in range(NG):
                chunks = (2 * gp, 2 * gp + 1)
                for n in chunks:
                    o = begin(f"bk{n}")
                    for c in range(NC):
                        ins = turn(o[:, P * c:P * (c + 1)], bk[:, c, n, :])
                    end(ins, f"bk{n}")
                    for u in range(2):
                        o = begin(f"gm{n}_{u}")
                        for i in range(4):
                            a = HD * u
                            ins = mm(o[:, P * i:P * (i + 1)], bk[a:a + HD, i, n, :], rk[a:a + HD, i, n, :],
                                     start=True, stop=True)
                        end(ins, f"gm{n}_{u}")
                for m in (range(0, 3) if gp == 0 else range(2 * gp + 1, 2 * gp + 3)):
                    o = begin(f"vw{m}")
                    for c in range(NC):
                        at = (8 + c) * TT + C * (m - 1)
                        ins = turn(o[:, P * c:P * (c + 1)], vflat[:, at:at + P])
                    end(ins, f"vw{m}")
                if gp:
                    channels(gp - 1)
                pairs = [(q, a) for q in range(2 * NC) for a in (0, C)]
                points = 3 * LEVELS + 6

                def small(job, lhs, rhs):
                    o = begin(job)
                    for q, a in pairs:
                        ins = mm(o[a:a + C, C * q:C * (q + 1)], lhs[a:a + C, q, :], rhs[a:a + C, q, :],
                                 start=True, stop=True)
                    end(ins, job)

                for lv in range(LEVELS):
                    pe.wait_ge(xt_ready, 2 * (gp * LEVELS + lv + 1))
                    small(f"iy{gp}_{lv}", xt, inv)
                    page_values(gp, 3 * lv, points)
                    read(pe, f"iy{gp}_{lv}")
                    if lv < LEVELS - 1:
                        small(f"inv{gp}_{lv}", inv_t, y)
                    page_values(gp, 3 * lv + 1, points)
                    small(f"invt{gp}_{lv}", y, inv_t)
                    page_values(gp, 3 * lv + 2, points)
                read(pe, f"invt{gp}_{LEVELS - 1}")
                for n in chunks:
                    s, e2 = n % 3, n % 2
                    heads = [(2 * c + e, c, C * e) for c in range(NC) for e in range(2)]
                    pe.wait_ge(state_ready, n + 1)
                    o = begin(f"r{n}")
                    for h, c, a in heads:
                        mm(o[a:a + C, C * c:C * (c + 1)], rk[a:a + C, c, n, 0:C], state[a:a + C, c, :],
                           start=True, stop=False)
                        ins = mm(o[a:a + C, C * c:C * (c + 1)], g[:, e2, h, 0:C], uv[:, s, h, :], start=False, stop=True)
                    end(ins, f"r{n}")
                    page_values(gp, 3 * LEVELS + 3 * e2, points)
                    read(pe, f"r{n}")
                    o = begin(f"u{n}")
                    for h, c, a in heads:
                        ins = mm(o[a:a + C, C * c:C * (c + 1)], inv_t[a:a + C, NC * e2 + c, :], r_sb[a:a + C, c, :],
                                 start=True, stop=True)
                    end(ins, f"u{n}")
                    page_values(gp, 3 * LEVELS + 3 * e2 + 1, points)
                    read(pe, f"u{n}")
                    o = begin(f"oc{n}")
                    for h, c, a in heads:
                        mm(o[a:a + C, C * c:C * (c + 1)], state[a:a + C, c, :], rk[a:a + C, c, n, C:P],
                           start=True, stop=False)
                        ins = mm(o[a:a + C, C * c:C * (c + 1)], uv[:, s, h, :], g[:, e2, h, C:P], start=False, stop=True)
                    end(ins, f"oc{n}")
                    o = begin(f"st{n}")
                    for h, c, a in heads:
                        ins = mm(o[a:a + C, C * c:C * (c + 1)], bkn[:, e2, c, a:a + C], uv[:, s, h, :],
                                 start=True, stop=True)
                    end(ins, f"st{n}")
                    page_values(gp, 3 * LEVELS + 3 * e2 + 2, points)
            pe.wait_ge(state_ready, NCH + 1)
            o = begin("state")
            for c in range(NC):
                ins = turn(o[0:64, P * c:P * (c + 1)], state[:, c, :])
            end(ins, "state")
            channels(NG - 1)
            end_phase(pe, CHAIN)

            head_sums("mean", o_t)
            pe.wait_ge(dev_squares, 1)
            head_sums("var", n2)
            for br, src in (("A", o_t), ("B", b_out)):
                if br == "A":
                    pe.wait_ge(a_ready, 1)
                gs, us = begin(f"gs{br}"), begin(f"us{br}")
                for m in range(KD):
                    wg, wu = weight(f"{br}{m // 2}", KD, 256), weight(f"{br}{m // 2}", NC, 256, 2048)
                    a = P * (m % 2)
                    product(gs[:, NS * m:NS * (m + 1)], [(wg[:, k, a:a + P], hs[k]) for k in range(KD)])
                    product(us[:, NS * m:NS * (m + 1)], [(wu[:, k, a:a + P], src[:, k, T:TT]) for k in range(NC)])
                    columns(f"g{br}{m}", wg, m % 2)
                    end(product(begin(f"u{br}{m}")[:, :], [(wu[:, k, a:a + P], src[:, k, 0:T]) for k in range(NC)]),
                        f"u{br}{m}")
                pe.drain().then_inc(bank_full[6], 1)
                pe.drain().then_inc(bank_full[7], 1)
            end_phase(pe, MIX)

            pe.wait_ge(key_in, 32)
            o = begin("keys")
            for i in range(2):
                ins = turn(o[:, P * i:P * (i + 1)], buf("key_rows")[:, P * i:P * (i + 1)])
            end(ins, "keys")
            for u in range(2):
                w = weight(f"wo{u}", KD, 512)
                for t in range(NT + 1):
                    a, n = (P * t, P) if t < NT else (T, NS)
                    end(product(begin(f"wo{u}_{t}")[0:n, :], [(mixed[:, k, a:a + n], w[:, k, :]) for k in range(KD)]),
                        f"wo{u}_{t}")
            for t in range(NT):
                pe.wait_ge(h2_ready, t + 1)
                for u in range(2):
                    o = begin(f"h2{t}_{u}")
                    for k in range(4):
                        ins = turn(o[:, P * k:P * (k + 1)], h2[:, t, P * (4 * u + k):P * (4 * u + k + 1)])
                    end(ins, f"h2{t}_{u}")
            pe.wait_ge(h2_ready, NT + 1)
            o = begin("h2s")
            for k in range(KD):
                ins = turn(o[:, NS * k:NS * (k + 1)], h2[0:8, NT, P * k:P * (k + 1)])
            end(ins, "h2s")
            end_phase(pe, OUT)

            def key_scores(t, groups=range(4)):
                a, n = (P * t, P) if t < NT else (T, NS)
                for gg in groups:
                    o = begin(f"s{t}_{gg}")
                    for i in range(4):
                        m = 4 * gg + i
                        ins = mm(o[0:n, P * i:P * (i + 1)], qp[:, m, a:a + n], key_t[:, m % 2, :], start=True, stop=True)
                    end(ins, f"s{t}_{gg}")

            pqs = begin("pqs")
            for m in range(16):
                w = weight(f"wq{m // 4}", KD, 512)
                a = P * (m % 4)
                product(pqs[:, NS * m:NS * (m + 1)], [(w[:, k, a:a + P], h2_t[:, k, T:TT]) for k in range(KD)])
                end(product(begin(f"pq{m}")[:, :], [(w[:, k, a:a + P], h2_t[:, k, 0:T]) for k in range(KD)]), f"pq{m}")
                if m in (4, 8, 12, 15):
                    gg = (m - 1) // 4
                    read(pe, f"pq{4 * gg + 3}")
                    key_scores(0, [gg])
            pe.drain().then_inc(bank_full[7], 1)
            end_phase(pe, QUERY)

            for t in (1, 2):
                key_scores(t)
            for t in range(NT):
                if t + 3 < NT + 1:
                    key_scores(t + 3)
                acc = [begin(f"y{t}_{u}") for u in range(2)]
                pe.wait_ge(zero_ready, 1)
                for u in range(2):
                    mm(acc[u][:, :], zero, bc[:, 0, 0:512], start=True, stop=False, skip_group_check=True)
                n = 2 if t < NT - 1 else 1
                with pe.Fori(0, SLOTS // TOP) as i:
                    for x in range(TOP):
                        j, d = (n * x + n - 1) % RING, x % RING
                        pe.wait_ge(row_in[j], i * (32 * n) + 16 * (TURN[t] + n * x // RING + 1))
                        pe.wait_ge(diag_made[d], i * 2 + (16 * t + x // RING + 1))
                        for u in range(2):
                            ins = mm(acc[u][:, :], diag[:, d, :], gathered[:, j, 512 * u:512 * (u + 1)],
                                     start=False, stop=False, skip_group_check=True)
                        ins.then_inc(row_free[j], 1)
                pe.drain().then_inc(bank_full[6], 1)
                pe.drain().then_inc(bank_full[7], 1)
            pe.wait_ge(top_s_ready, 1)
            o = begin("tg")
            turn(o[:, 0:NS], idx_f[0:8, :])
            end(turn(o[:, NS:2 * NS], coef[0:8, NT, :]), "tg")
            for b in range(NS):
                for u in range(2):
                    end(mm(begin(f"hb{b}_{u}")[:, :], rows[0:8, b, :], h2[0:8, NT, 512 * u:512 * (u + 1)],
                           start=True, stop=True), f"hb{b}_{u}")
            acc = [begin(f"ys_{u}") for u in range(2)]
            pe.wait_ge(coef_s_ready, 1)
            for b in range(NS):
                pe.wait_ge(row_in[b], 16 * (TURN[NT] + 2))
                for u in range(2):
                    ins = mm(acc[u][0:8, :], coef_s[:, b, :], gathered[:, b, 512 * u:512 * (u + 1)],
                             start=b == 0, stop=b == NS - 1, skip_group_check=True)
            pe.drain().then_inc(bank_full[6], 1)
            pe.drain().then_inc(bank_full[7], 1)

        @block.scalar
        def _(act):
            link = make_link(act, scalar_step)
            fn = nc.scalar.activation

            def take(job, out, src, func=ACT.Copy, last=True, **more):
                full(act, job)
                link(fn(out, src, func, **more), job=job if last else None)

            act.wait_ge(c_in, 32)
            link(fn(buf("c_rows")[0:9, D:2 * D], buf("c_rows")[0:9, 0:D], ACT.Sigmoid), signal=c_sigmoid, at=1)
            take("c_t", buf("c_t"), bank("c_t")[:, 0:9 * KD])
            for j in range(4):
                if j >= 2:
                    full(act, f"adat{j - 2}")
                take(f"ada{j}", buf("ada_rows")[0:9, 512 * (j % 2):512 * (j % 2 + 1)], bank(f"ada{j}")[0:9, :])
                if j == 0:
                    take("par", par, bank("par")[:, 0:PAR_ROWS])
            act.wait_ge(ada_ready, 1)
            for t in range(NT):
                for k in range(4):
                    take(f"x{t}_0", h_t[:, k, P * t:P * (t + 1)], bank(f"x{t}_0")[:, P * k:P * (k + 1)],
                         ACT.Identity, last=k == 3, scale=ada_t[:, 8 + k, 8:9], bias=ada_t[:, k, 8:9])
            take("shift_t", buf("shift_t"), bank("shift_t")[:, 0:MS * NS])
            bias = blocks("bias", H)
            for u in range(4):
                t, h = u // 2, 4 * (u % 2)
                take(f"bias{u}", bias[:, h:h + 4, P * t:P * (t + 1)],
                     bank(f"bias{u}")[:, :].rearrange("p (h s) -> p h s", h=4))
            end_phase(act, LOAD)

            take("qs", buf("qs")[0:8, :], bank("qs")[0:8, :])
            for c in range(NC):
                take(f"q{c}", q_t[:, c, :], bank(f"q{c}")[:, :], scale=SCALE)
            for b in range(NS):
                take(f"qb{b}", qb[:, b, :], bank(f"qb{b}")[:, :], scale=SCALE)
            take("ks", buf("ks")[0:8, :], bank("ks")[0:8, :])
            for c in range(NC):
                take(f"k{c}", k_t[:, c, :], bank(f"k{c}")[:, :])
            take("vs", buf("vs")[0:8, :], bank("vs")[0:8, :])
            for t in range(NT):
                take(f"v{t}", v_rows[:, t, :], bank(f"v{t}")[:, :])
            act.wait_ge(forget_in, 32)
            take("f", f[0:8, 0:T], bank("f")[0:8, :], ACT.Identity, bias=buf("bf")[0:8, 0:1])
            take("fs", f[0:8, T:TT], bank("fs")[0:8, 0:8])
            for m in range(MS):
                o = bank(f"z{m}")
                take(f"z{m}", mix[:, m, 0:T], o[:, :], last=False, scale=one_minus_mu[:, m:m + 1])
                take(f"z{m}", prev[:, m, 1:T], o[:, 0:T - 1], last=False, scale=param("mu_shift", m, m + 1))
                take(f"z{m}", z9[:, m, 8:9], o[:, T - 1:T])
            take("zs", z9[:, :, 0:8], bank("zs")[:, 0:MS * NS].rearrange("p (m b) -> p m b", m=MS))
            for u in range(4):
                n = min(4, MS - 4 * u) * P
                if u:
                    act.wait_ge(shift_stored, u)
                take(f"shift{u}", buf("shift_out")[0:9, 0:n], bank(f"shift{u}")[0:9, 0:n])
            for t in range(NT):
                if t:
                    act.wait_ge(krows_out, t)
                take(f"krows{t}", buf("k_rows"), bank(f"krows{t}")[:, :])
            act.wait_ge(f_abs, 1)
            link(fn(f2[0:8, 0:TT], f2[0:8, 0:TT], ACT.Exp))
            link(fn(f2[0:8, 0:TT], f2[0:8, 0:TT], ACT.Ln, bias=1.0), signal=f_log, at=1)
            take("logf", buf("logf_out"), bank("logf")[:, 0:NT * H])
            end_phase(act, PROJ)

            act.wait_ge(shifted, 1)
            link(fn(buf("scores"), buf("scores"), ACT.Exp))
            link(fn(sm(329, 393), sm(329, 393), ACT.Exp), signal=exps_ready, at=1)
            act.wait_ge(proj_stored, 1)
            end_phase(act, SAMPLE)

            stat = buf("rowstat")
            for i in range(NT * H + 2):
                if i < NT * H:
                    n = P * (i // H + 1)
                    act.wait_ge(row_max, i + 1)
                    if i >= 2:
                        full(act, f"pt{i - 2}")
                    take(f"qk{i}", probs[:, i % 2, 0:n], bank(f"qk{i}")[:, 0:n], ACT.Exp, bias=stat[:, i:i + 1],
                         accum_out=stat[:, NT * H + i:NT * H + i + 1])
                if 1 <= i <= NT * H:
                    n = P * ((i - 1) // H + 1)
                    take(f"pt{i - 1}", probs_t[:, (i - 1) % 2, 0:n], bank(f"pt{i - 1}")[:, 0:n])
                if i >= 2 and (i - 2) % H == H - 1:
                    t = (i - 2) // H
                    take(f"o{t}", b_out[:, :, P * t:P * (t + 1)], bank(f"o{t}")[:, :].rearrange("p (c q) -> p c q", c=NC))
            end_phase(act, FOX)

            link(fn(mix[0:64, 12, :], mix[0:64, 12, :], ACT.Tanh), signal=lora_ready, at=1)
            link(fn(mix[:, 13, :], mix[:, 13, :], ACT.Sigmoid), signal=lora_ready, at=2)
            lo = bank("lora_s")
            for c in range(NC):
                take("lora_s", sig[:, c, T:TT], lo[:, NS * c:NS * (c + 1)], ACT.Sigmoid, last=False,
                     bias=param("w0", c, c + 1))
            for c in range(NC):
                take("iclr_s", iclr[:, c, T:TT], bank("iclr_s")[:, NS * c:NS * (c + 1)], ACT.Sigmoid, last=c == NC - 1,
                     bias=param("a0", c, c + 1))
            take("lora_s", gate[:, :, T:TT], lo[:, 2 * NC * NS:3 * NC * NS].rearrange("p (c b) -> p c b", c=NC))
            for c in range(NC):
                take(f"dec{c}", sig[:, c, 0:T], bank(f"dec{c}")[:, :], ACT.Sigmoid, bias=param("w0", c, c + 1))
            for c in range(NC):
                take(f"iclr{c}", iclr[:, c, 0:T], bank(f"iclr{c}")[:, :], ACT.Sigmoid, bias=param("a0", c, c + 1))
            for c in range(NC):
                take(f"gate{c}", gate[:, c, 0:T], bank(f"gate{c}")[:, :])

            def modulations(js):
                for j in js:
                    if j >= 2:
                        act.wait_ge(mod_out[j % 2], 16 * (j // 2))
                    take(f"an{j}", buf("an_rows")[0:9, 512 * (j % 2):512 * (j % 2 + 1)], bank(f"an{j}")[0:9, :])

            act.wait_ge(norm_ready, 1)
            link(fn(buf("t1"), buf("t1"), ACT.Sqrt), signal=pre_acts, at=1)
            modulations(range(5))
            act.wait_ge(logs_ready, 1)
            link(fn(buf("sig"), buf("sig"), ACT.Exp, scale=-DECAY), signal=pre_acts, at=2)
            act.wait_ge(logs_ready, 2)
            link(fn(buf("sig"), buf("iclr"), ACT.Exp, scale=-DECAY))
            link(fn(buf("iclr"), buf("iclr"), ACT.Exp, scale=DECAY), signal=pre_acts, at=3)
            modulations(range(5, 8))
            act.wait_ge(mod_out[0], 4 * 16)
            act.wait_ge(mod_out[1], 4 * 16)
            end_phase(act, PRE)

            for i in range(6):
                take(f"svec{i}", buf("snat")[0:8, W * i:W * (i + 1)], bank(f"svec{i}")[0:8, :])
            end_phase(act, STATE)

            take("so", o_t[:, :, T:TT], bank("so")[:, 0:NC * NS].rearrange("p (c b) -> p c b", c=NC))

            def channels(gp):
                o = bank(f"vt{gp}")[:, 0:4 * NC].rearrange("p (b c e) -> p e c b", b=2, e=2)
                for e in range(2):
                    part = slice(C * e, C * (e + 1))
                    take(f"vt{gp}", b_out[part, :, T + 2 * gp:T + 2 * gp + 2], o[part, e, :, :], last=e == 1)

            for gp in range(NG):
                chunks = (2 * gp, 2 * gp + 1)
                for n in chunks:
                    take(f"bk{n}", bkn[:, n % 2, :, :], bank(f"bk{n}")[:, :].rearrange("p (c x) -> p c x", c=NC))
                for m in (range(0, 3) if gp == 0 else range(2 * gp + 1, 2 * gp + 3)):
                    o = bank(f"vw{m}")[:, :].rearrange("p (c e i) -> p c e i", c=NC, e=2)
                    pairs = uv.rearrange("p s (c e) i -> p s c e i", e=2)
                    if m < NCH:
                        take(f"vw{m}", pairs[C:P, m % 3, :, 0, :], o[C:P, :, 0, :], last=m == 0)
                    if m:
                        take(f"vw{m}", pairs[0:C, (m - 1) % 3, :, 1, :], o[0:C, :, 1, :])
                if gp:
                    channels(gp - 1)
                for lv in range(LEVELS):
                    take(f"iy{gp}_{lv}", buf("y"), bank(f"iy{gp}_{lv}")[:, :])
                for n in chunks:
                    take(f"r{n}", buf("r_sb"), bank(f"r{n}")[:, 0:NC * C])
                    take(f"oc{n}", o_t[:, :, C * n:C * (n + 1)], bank(f"oc{n}")[:, 0:NC * C].rearrange("p (c t) -> p c t", c=NC))
                for n in chunks:
                    take(f"vo{n}", buf("vm")[0:8, W * (n % 2):W * (n % 2 + 1)], bank(f"vo{n}")[0:8, :])
            act.wait_ge(wkv_stored, 1)
            take("state", buf("y")[0:64, 0:512], bank("state")[0:64, :])
            channels(NG - 1)
            act.wait_ge(wkv_stored, 2)
            end_phase(act, CHAIN)

            act.wait_ge(dev_ready, 1)
            link(fn(buf("n2"), buf("n1"), ACT.Square), signal=dev_squares, at=1)
            for c in range(NC):
                take(f"var{c}", n2[:, c, 0:T], bank(f"var{c}")[:, :], ACT.Sqrt, scale=1.0 / HD, bias=eps[:, 1:2])
            take("var_s", n2[:, :, T:TT], bank("var_s")[:, 0:NC * NS].rearrange("p (c b) -> p c b", c=NC),
                 ACT.Sqrt, scale=1.0 / HD, bias=eps[:, 1:2])
            sgs = buf("sgs")
            for i, br in enumerate("AB"):
                for m in range(KD):
                    if m >= 2:
                        read(act, f"u{br}{m - 2}")
                    elif br == "B":
                        read(act, f"uA{KD - 2 + m}")
                    take(f"g{br}{m}", sg[:, m % 2, 0:T], bank(f"g{br}{m}")[:, :], ACT.Sigmoid)
                if br == "B":
                    read(act, "usA")
                take(f"gs{br}", sgs, bank(f"gs{br}")[:, 0:KD * NS], ACT.Sigmoid)
            end_phase(act, MIX)

            take("keys", buf("key_t"), bank("keys")[:, 0:2 * P])

            def root(n, count):
                act.wait_ge(var_ready, count)
                link(fn(stats[0:n, 14:15], stats[0:n, 13:14], ACT.Sqrt, bias=eps[0:n, 0:1]), signal=root_ready, at=count)

            for t in range(NT + 1):
                root(P if t < NT else NS, t + 1)
            for t in range(NT):
                for u in range(2):
                    take(f"h2{t}_{u}", h2_t[:, 4 * u:4 * u + 4, P * t:P * (t + 1)],
                         bank(f"h2{t}_{u}")[:, :].rearrange("p (k x) -> p k x", k=4))
            take("h2s", h2_t[:, :, T:TT], bank("h2s")[:, 0:KD * NS].rearrange("p (k b) -> p k b", k=KD))
            end_phase(act, OUT)

            def key_scores(t, groups=range(4)):
                n = P if t < NT else NS
                if t >= 2:
                    act.wait_ge(top_done, t - 1)
                for gg in groups:
                    take(f"s{t}_{gg}", buf("ta" if t % 2 == 0 else "tb")[0:n, 512 * gg:512 * (gg + 1)],
                         bank(f"s{t}_{gg}")[0:n, :])

            def gate_exp(t):
                n = P if t < NT else NS
                act.wait_ge(gate_ready, t + 1)
                link(fn(coef[0:n, t, :], coef[0:n, t, :], ACT.Exp), signal=gate_exps, at=t + 1)

            def gelu_exp(t):
                act.wait_ge(gelu_arg, t + 1)
                link(fn(gelu[:, 0:SLOTS], gelu[:, 0:SLOTS], ACT.Tanh, scale=0.7978845608028654), signal=gelu_tanh, at=t + 1)

            for m in range(16):
                take(f"pq{m}", qp[:, m, 0:T], bank(f"pq{m}")[:, :])
                if m in (4, 8, 12, 15):
                    key_scores(0, [(m - 1) // 4])
            take("pqs", qp[:, :, T:TT], bank("pqs")[:, 0:16 * NS].rearrange("p (m b) -> p m b", m=16))
            gate_exp(0)
            end_phase(act, QUERY)

            key_scores(1)
            key_scores(2)
            gelu_exp(0)
            gate_exp(1)
            for t in range(NT):
                if t + 3 < NT + 1:
                    key_scores(t + 3)
                act.wait_ge(coef_ready, t + 1)
                n = 2 if t < NT - 1 else 1
                if n == 1:
                    for j in range(1, RING, 2):
                        act.wait_ge(row_free[j], TURN[t] + 2)
                with act.Fori(0, SLOTS // TOP) as i:
                    for x in range(TOP):
                        j, d = (n * x + n - 1) % RING, x % RING
                        act.wait_ge(row_free[j], i * (2 * n) + (TURN[t] + n * x // RING - n + 3))
                        fn(diag[:, d, :], ident, ACT.Copy, scale=coef_cols[:, ds(i * TOP + (t * SLOTS + x), 1)])\
                            .then_inc(diag_made[d], 1)
                if t < NT - 1:
                    gelu_exp(t + 1)
                    gate_exp(t + 2)
                root(P, NT + 1 + t + 1)
            act.wait_ge(gelu_arg, NT + 1)
            link(fn(gelu[:, 0:NS], gelu[:, 0:NS], ACT.Tanh, scale=0.7978845608028654), signal=gelu_tanh, at=NT + 1)
            root(NS, 2 * NT + 2)

        @block.vector
        def _(dve):
            link = make_link(dve, vector_step)
            tt, ts, stt = nc.vector.tensor_tensor, nc.vector.tensor_scalar, nc.vector.scalar_tensor_tensor
            red = nc.vector.tensor_reduce
            MUL, ADD, SUB, MAX, MIN = ALU.mult, ALU.add, ALU.subtract, ALU.max, ALU.min

            def along(x, shape, *axes):
                for a in axes:
                    x = x.unsqueeze(a)
                return x.to_broadcast(shape)

            link(nc.vector.memset(eps[:, 0:1], LN_EPS))
            link(nc.vector.memset(eps[:, 1:2], GN_EPS))
            dve.wait_ge(c_sigmoid, 1)
            link(tt(buf("c_rows")[0:9, 0:D], buf("c_rows")[0:9, 0:D], buf("c_rows")[0:9, D:2 * D], MUL),
                 signal=silu_ready, at=1)
            dve.wait_ge(logf_in, 32)
            dve.wait_ge(consts_in, 16)
            prefix = blocks("prefix", 2 * H)
            for t in range(2):
                past = buf("logf_rows")[:, t * D:(t + 1) * D].rearrange("p (s h) -> p h s", h=H)
                for h in range(H):
                    link(nc.vector.tensor_tensor_scan(prefix[:, t * H + h, :], ones, past[:, h, :], 0.0, MUL, ADD))
            tot = buf("page_tot")
            link(nc.vector.tensor_copy(tot[:, 0:16], prefix[:, :, P - 1]), signal=prefix_ready, at=1)
            read(dve, "par")
            link(ts(one_minus_mu, param("mu_shift"), -1.0, 1.0, MUL, ADD))
            link(ts(one_minus_ka, param("k_a"), -1.0, 1.0, MUL, ADD))
            for j in range(4):
                full(dve, f"adat{j}")
                link(tt(ada_t[:, 4 * j:4 * j + 4, :], bank(f"adat{j}")[:, 0:36].rearrange("p (m b) -> p m b", m=4),
                        along(param("b_ada", 4 * j, 4 * j + 4), [P, 4, 9], 2), ADD), job=f"adat{j}")
            link(nc.vector.tensor_scalar_add(ada_t[:, 8:16, :], ada_t[:, 8:16, :], 1.0), signal=ada_ready, at=1)
            for t in range(NT):
                full(dve, f"x{t}_1")
                for k in range(4, KD):
                    link(ts(h_t[:, k, P * t:P * (t + 1)], bank(f"x{t}_1")[:, P * (k - 4):P * (k - 3)],
                            ada_t[:, 8 + k, 8:9], ada_t[:, k, 8:9], MUL, ADD), job=f"x{t}_1" if k == KD - 1 else None)
            full(dve, "xs")
            link(tt(h_t[:, :, T:TT], bank("xs")[:, 0:KD * NS].rearrange("p (k b) -> p k b", k=KD), ada_t[:, 8:16, 0:8], MUL),
                 job="xs")
            link(tt(h_t[:, :, T:TT], h_t[:, :, T:TT], ada_t[:, 0:8, 0:8], ADD))
            full(dve, "suffix")
            link(tt(tot[:, 16:32], bank("suffix")[:, 0:16], tot[:, 0:16], ADD), job="suffix")
            link(tt(prefix, along(tot[:, 16:32], [P, 2 * H, P], 2), prefix, SUB), signal=tot_ready, at=1)
            end_phase(dve, LOAD)

            for j in range(RING):
                dve.sem_inc(page_free[j], 1)
            read(dve, f"qb{NS - 1}")
            qflat = buf("qb")
            with dve.Fori(0, NS) as b:
                with dve.Fori(0, PAGES // RING) as gg:

                    def page_dot(j):
                        dve.wait_ge(page_loaded[j], b * 64 + gg * 16 + 16)
                        tt(pages[:, j, :], pages[:, j, :], qflat[:, ds(b * W, W)], MUL).then_inc(page_product, 1)

                    def page_sum(j):
                        dve.wait_ge(page_product, b * PAGES + gg * RING + (j + 1))
                        red(scores[:, :, ds(b * PAGES + gg * RING + j, 1)].rearrange("p h o -> p (h o)"),
                            pages[:, j, :].rearrange("p (h d) -> p h d", h=H), AX.X, ADD).then_inc(page_free[j], 1)

                    page_dot(0)
                    for j in range(1, RING):
                        page_dot(j)
                        page_sum(j - 1)
                    page_sum(RING - 1)
            for j in range(RING):
                dve.wait_ge(page_free[j], 33)
            read(dve, "fs")
            link(tt(f[0:8, T:TT], f[0:8, T:TT], buf("bf")[0:8, 8:16], ADD))
            link(stt(f2[0:8, 0:TT], f[0:8, 0:TT], -1.0, f[0:8, 0:TT], MUL, MIN), signal=f_abs, at=1)
            dve.wait_ge(f_log, 1)
            link(stt(f[0:8, 0:TT], f[0:8, 0:TT], 0.0, f2[0:8, 0:TT], MIN, SUB), signal=logf_ready, at=1)
            read(dve, "zs")
            link(nc.vector.memset(prev[:, :, 0:1], 0.0))
            link(tt(prev[:, :, T:TT], blocks("shift_t", MS), along(param("mu_shift"), [P, MS, NS], 2), MUL))
            link(tt(mix[:, :, T:TT], z9[:, :, 0:8], along(one_minus_mu, [P, MS, NS], 2), MUL))
            link(tt(buf("mix"), buf("mix"), buf("prev"), ADD))
            end_phase(dve, PROJ)

            s8 = buf("small")[0:8, :]
            link(tt(buf("qs")[0:8, :], buf("qs")[0:8, :], buf("ks")[0:8, :], MUL))
            link(red(s8[:, 0:8], buf("qs")[0:8, :].rearrange("p (h d) -> p h d", h=H), AX.X, ADD))
            link(stt(s8[:, 0:8], s8[:, 0:8], SCALE, f[0:8, T:TT], MUL, SUB))
            link(tt(s8[:, 8:72].rearrange("p (h b) -> p h b", h=H), along(s8[:, 0:8], [8, H, NS], 2),
                    along(ident[0:8, 0:8], [8, H, NS], 1), MUL), signal=snew_ready, at=1)
            full(dve, "s_new")
            link(nc.vector.tensor_copy(sm(72, 136), bank("s_new")[:, 0:64]), job="s_new")
            link(tt(buf("scores"), buf("scores"), buf("bias"), ADD))
            by_pair = buf("scores").rearrange("p (x g) -> p x g", g=PAGES)
            link(red(sm(136, 200), by_pair, AX.X, MAX))
            link(tt(sm(136, 200), sm(136, 200), sm(72, 136), MAX), signal=max_ready, at=1)
            full(dve, "max_t")
            link(red(sm(200, 201)[0:64, :], bank("max_t")[0:64, 0:P], AX.X, MAX), job="max_t")
            link(ts(sm(201, 265)[0:64, :], ident[0:64, 0:64], sm(200, 201)[0:64, :], None, MUL), signal=diag_ready, at=1)
            full(dve, "max_b")
            link(nc.vector.tensor_copy(sm(265, 329), bank("max_b")[:, 0:64]), job="max_b")
            link(tt(sm(329, 393), sm(72, 136), sm(265, 329), SUB))
            link(tt(by_pair, by_pair, along(sm(265, 329), [P, 64, PAGES], 2), SUB), signal=shifted, at=1)
            dve.wait_ge(exps_ready, 1)
            link(red(sm(393, 457), by_pair, AX.X, ADD), signal=sum_ready, at=1)
            full(dve, "sum_b")
            link(tt(sm(457, 521), bank("sum_b")[:, 0:64], sm(329, 393), ADD), job="sum_b")
            link(nc.vector.reciprocal(sm(457, 521), sm(457, 521)))
            link(tt(by_pair, by_pair, along(sm(457, 521), [P, 64, PAGES], 2), MUL))
            link(tt(sm(521, 585), sm(329, 393), sm(457, 521), MUL))
            link(tt(pn_rows[0:8], s8[:, 521:585].rearrange("p (h b) -> p b h", h=H), along(ident[0:8, 0:8], [8, NS, H], 2),
                    MUL))
            link(nc.vector.tensor_tensor_scan(f2[0:8, 0:T], ones[0:8, 0:1].to_broadcast([8, T]), f[0:8, 0:T], 0.0, MUL, ADD))
            link(ts(f2[0:8, 0:T], f2[0:8, 0:T], -1.0, None, MUL), signal=forget_sum, at=1)
            end_phase(dve, SAMPLE)

            stat = buf("rowstat")
            NR = NT * H
            for i in range(NR + 1):
                if i < NR:
                    full(dve, f"qk{i}")
                    link(red(stat[:, i:i + 1], bank(f"qk{i}")[:, 0:P * (i // H + 1)], AX.X, MAX, negate=True),
                         signal=row_max, at=i + 1)
                if i:
                    k, n = i - 1, P * ((i - 1) // H + 1)
                    read(dve, f"qk{k}")
                    link(nc.vector.reciprocal(stat[:, 2 * NR + k:2 * NR + k + 1], stat[:, NR + k:NR + k + 1]))
                    link(ts(probs[:, k % 2, 0:n], probs[:, k % 2, 0:n], stat[:, 2 * NR + k:2 * NR + k + 1], None, MUL),
                         signal=row_prob, at=i)
            end_phase(dve, FOX)

            R, K, V = mix[:, 0:NC, :], mix[:, NC:2 * NC, :], mix[:, 2 * NC:3 * NC, :]
            whole = [P, NC, TT]
            link(tt(kk, K, along(param("k_k"), whole, 2), MUL))
            link(tt(t1, kk, kk, MUL), signal=squares_ready, at=1)
            for c in range(NC):
                full(dve, f"norm{c}")
                link(ts(t1[:, c, 0:T], bank(f"norm{c}")[:, :], 1e-24, None, MAX), job=f"norm{c}")
            full(dve, "norm_s")
            link(ts(t1[:, :, T:TT], bank("norm_s")[:, 0:NC * NS].rearrange("p (c b) -> p c b", c=NC), 1e-24, None, MAX),
                 job="norm_s")
            read(dve, "gate3")
            link(nc.vector.tensor_copy(svec[:, 4, :, :], V[:, :, T:TT]), signal=norm_ready, at=1)
            dve.wait_ge(pre_acts, 1)
            link(nc.vector.reciprocal(t1, t1))
            link(tt(kk, kk, t1, MUL))
            link(tt(t1, kk, iclr, MUL))
            for c in range(NC):
                link(ts(iclr[:, c, :], iclr[:, c, :], param("k_a", c, c + 1), one_minus_ka[:, c:c + 1], MUL, ADD))
            link(tt(K, K, iclr, MUL))
            rkp = buf("bk")[:, 0:NC * TT].rearrange("p (c t) -> p c t", c=NC)
            link(tt(rkp, R, K, MUL))
            link(tt(rkp, rkp, along(param("r_k"), whole, 2), MUL), signal=rk_product, at=1)
            dve.wait_ge(masks_in, 32)
            for c in range(NC):
                link(nc.vector.tensor_tensor_scan(iclr[:, c, 0:T], const("reset"), sig[:, c, 0:T], 0.0, MUL, ADD))
            link(nc.vector.tensor_copy(iclr[:, :, T:TT], sig[:, :, T:TT]))
            link(tt(sig, iclr, sig, SUB), signal=logs_ready, at=1)
            dve.wait_ge(pre_acts, 2)

            def chunked(x, a=0, b=P):
                return x[a:b, :, 0:T].rearrange("p c (n t) -> p c n t", n=NCH)

            link(nc.vector.tensor_copy(svec[:, 1, :, :], kk[:, :, T:TT]))
            link(tt(rk[:, :, :, 0:C], chunked(kk), chunked(sig), MUL), signal=logs_ready, at=2)
            dve.wait_ge(pre_acts, 3)
            link(nc.vector.tensor_copy(svec[:, 0, :, :], sig[:, :, T:TT]))
            link(nc.vector.tensor_copy(svec[:, 2, :, :], t1[:, :, T:TT]))
            link(nc.vector.tensor_copy(svec[:, 3, :, :], K[:, :, T:TT]))
            link(nc.vector.tensor_copy(svec[:, 5, :, :], R[:, :, T:TT]))
            link(nc.vector.tensor_copy(lam, chunked(sig)[:, :, :, C - 1]))
            link(tt(rk[:, :, :, C:P], chunked(R), chunked(sig), MUL))
            full(dve, "bonus_s")
            for a, first, second in ((0, t1, K), (C, K, t1)):
                link(tt(bk[a:a + C, :, :, 0:C], chunked(first, a, a + C), chunked(iclr, a, a + C), MUL))
                link(tt(bk[a:a + C, :, :, C:P], chunked(second, a, a + C), chunked(iclr, a, a + C), MUL))
            for c in range(NC):
                full(dve, f"bonus{c}")
                link(tt(R[:, c, 0:T], bank(f"bonus{c}")[:, :], V[:, c, 0:T], MUL), job=f"bonus{c}")
            link(tt(R[:, :, T:TT], bank("bonus_s")[:, 0:NC * NS].rearrange("p (c b) -> p c b", c=NC), V[:, :, T:TT], MUL),
                 job="bonus_s")
            end_phase(dve, PRE)

            dve.wait_ge(state_in, 16)
            dve.wait_ge(heads_in, 48)
            S = buf("wkv").rearrange("p (i j) -> p i j", j=HD)
            X = buf("wkv_tmp").rearrange("p (i j) -> p i j", j=HD)
            sh = blocks("shead", 6)
            sv, half = buf("svalue"), [P, 32, HD]
            link(tt(X, S, along(sh[:, 1, :], half, 1), MUL))
            link(red(buf("so_col"), X, AX.X, ADD))
            link(tt(S, S, along(sh[:, 0, :], half, 1), MUL))
            link(tt(X, along(buf("so_col"), half, 2), along(sh[:, 2, :], half, 1), MUL))
            link(tt(S, S, X, SUB))
            link(tt(X, along(sv, half, 2), along(sh[:, 3, :], half, 1), MUL))
            link(tt(S, S, X, ADD), signal=wkv_ready, at=1)
            link(tt(X, S, along(sh[:, 5, :], half, 1), MUL))
            link(red(buf("so_col"), X, AX.X, ADD), signal=wkv_ready, at=2)
            dve.wait_ge(heads_out, 32)
            end_phase(dve, STATE)

            dve.wait_ge(wkv_stored, 1)
            removed = uv.rearrange("p s (c e) i -> p s c e i", e=2)
            for a in (0, C):
                link(nc.vector.memset(removed[a:a + C, :, :, a // C, :], 0.0))
            link(nc.vector.memset(buf("state"), 0.0), signal=state_ready, at=1)

            gmask = const("gmask")
            levels = const("levels").rearrange("p (l t) -> p l t", l=LEVELS)
            for gp in range(NG):
                chunks = (2 * gp, 2 * gp + 1)
                for n in chunks:
                    for u in range(2):
                        full(dve, f"gm{n}_{u}")
                        link(tt(g[:, n % 2, u:H:2, :], bank(f"gm{n}_{u}")[:, :].rearrange("p (h x) -> p h x", h=4),
                                along(gmask, [P, 4, P], 1), MUL), job=f"gm{n}_{u}")
                for x in (inv, inv_t):
                    for a in (0, C):
                        link(nc.vector.tensor_copy(x[a:a + C], along(ident[a:a + C, a:a + C], [C, 2 * NC, C], 1)))
                for lv in range(LEVELS):
                    if lv:
                        full(dve, f"iy{gp}_{lv - 1}")
                    for a in (0, C):
                        mats = g[a:a + C].rearrange("p n (c e) x -> p (n c) e x", e=2)[:, :, a // C, 0:C]
                        link(tt(xt[a:a + C], mats, along(levels[a:a + C, lv, :], [C, 2 * NC, C], 1), MUL),
                             signal=xt_ready, at=2 * (gp * LEVELS + lv) + 1 + a // C)
                    if lv < LEVELS - 1:
                        full(dve, f"inv{gp}_{lv}")
                        link(tt(buf("inv"), buf("inv"), bank(f"inv{gp}_{lv}")[:, :], SUB), job=f"inv{gp}_{lv}")
                    full(dve, f"invt{gp}_{lv}")
                    link(tt(buf("inv_t"), buf("inv_t"), bank(f"invt{gp}_{lv}")[:, :], SUB), job=f"invt{gp}_{lv}")
                for n in chunks:
                    full(dve, f"u{n}")
                    o = bank(f"u{n}")[:, 0:NC * C].rearrange("p (c i) -> p c i", c=NC)
                    pairs = uv.rearrange("p s (c e) i -> p s c e i", e=2)
                    link(ts(pairs[0:C, n % 3, :, 0, :], o[0:C], -1.0, None, MUL))
                    link(ts(pairs[C:P, n % 3, :, 1, :], o[C:P], -1.0, None, MUL), job=f"u{n}")
                    full(dve, f"st{n}")
                    link(tt(buf("state"), buf("state"), bank(f"st{n}")[:, 0:NC * C], ADD), job=f"st{n}")
                    if n + 3 < NCH:
                        for a in (0, C):
                            link(nc.vector.memset(removed[a:a + C, n % 3, :, a // C, :], 0.0))
                    link(tt(state, state, along(lam[:, :, n], [P, NC, C], 2), MUL), signal=state_ready, at=n + 2)
            end_phase(dve, CHAIN)

            for c in range(NC):
                full(dve, f"mean{c}")
                link(stt(n1[:, c, 0:T], bank(f"mean{c}")[:, :], -1.0 / HD, o_t[:, c, 0:T], MUL, ADD), job=f"mean{c}")
            full(dve, "mean_s")
            link(stt(n1[:, :, T:TT], bank("mean_s")[:, 0:NC * NS].rearrange("p (c b) -> p c b", c=NC), -1.0 / HD,
                     o_t[:, :, T:TT], MUL, ADD), job="mean_s")
            dve.sem_inc(dev_ready, 1)
            read(dve, "var_s")
            link(nc.vector.reciprocal(n2, n2))
            link(tt(n1, n1, n2, MUL))
            for c in range(NC):
                link(ts(n1[:, c, :], n1[:, c, :], param("ln_x_w", c, c + 1), param("ln_x_b", c, c + 1), MUL, ADD))
            link(tt(n1, n1, R, ADD))
            link(tt(o_t, n1, gate, MUL), signal=a_ready, at=1)
            dve.wait_ge(an_in, 48)
            for x, n in ((an, NS), (buf("bc"), P)):
                for i in range(4):
                    part = slice(i * D, (i + 1) * D)
                    link(stt(x[0:n, part], x[0:n, part], 1.0 if i == 2 else 0.0, buf("bb")[0:n, part], ADD, ADD))
            for br in "AB":
                for m in range(KD):
                    read(dve, f"g{br}{m}")
                    full(dve, f"u{br}{m}")
                    o = bank(f"u{br}{m}")[:, :]
                    if br == "A":
                        link(tt(mixed[:, m, 0:T], sg[:, m % 2, 0:T], o, MUL), job=f"uA{m}")
                    else:
                        link(tt(sg[:, m % 2, 0:T], sg[:, m % 2, 0:T], o, MUL))
                        link(tt(mixed[:, m, 0:T], mixed[:, m, 0:T], sg[:, m % 2, 0:T], ADD), job=f"uB{m}")
                read(dve, f"gs{br}")
                full(dve, f"us{br}")
                sgs = blocks("sgs", KD)
                o = bank(f"us{br}")[:, 0:KD * NS].rearrange("p (k b) -> p k b", k=KD)
                if br == "A":
                    link(tt(mixed[:, :, T:TT], sgs, o, MUL), job="usA")
                else:
                    link(tt(sgs, sgs, o, MUL))
                    link(tt(mixed[:, :, T:TT], mixed[:, :, T:TT], sgs, ADD), job="usB")
            end_phase(dve, MIX)

            link(nc.vector.tensor_copy(buf("g2s")[0:8, :], an[0:8, 3 * D:4 * D]))
            dve.wait_ge(x2_in, 32)
            dve.wait_ge(lng_in, 64)
            norms = [0]

            def layer_norm(x, n, i):
                norms[0] += 1
                for u in range(2):
                    link(nc.vector.bn_stats(stats[0:n, 6 * u:6 * u + 6], x[:, 512 * u:512 * (u + 1)]))
                link(nc.vector.bn_aggr(stats[0:n, 12:14], stats[0:n, 0:12]), signal=var_ready, at=norms[0])
                dve.wait_ge(root_ready, norms[0])
                link(nc.vector.reciprocal(stats[0:n, 15:16], stats[0:n, 14:15]))
                link(ts(x, x, stats[0:n, 12:13], stats[0:n, 15:16], SUB, MUL))
                link(tt(x, x, lng[0:n, i, :], MUL))
                return tt(x, x, lng[0:n, i + 1, :], ADD)

            def mod(i, t, n):
                return bc[:, i, :] if t < NT else an[0:8, i * D:(i + 1) * D]

            for u in range(2):
                for t in range(NT + 1):
                    n = P if t < NT else NS
                    full(dve, f"wo{u}_{t}")
                    part = slice(512 * u, 512 * (u + 1))
                    link(tt(x1[0:n, t, part], bank(f"wo{u}_{t}")[0:n, :], mod(0, t, n)[:, part], MUL), job=f"wo{u}_{t}")
            for t in range(NT + 1):
                n = P if t < NT else NS
                x0 = buf("x2")[:, t * D:(t + 1) * D] if t < NT else buf("xs2")[0:8, :]
                link(stt(x1[0:n, t, :], x0, ALPHA, x1[0:n, t, :], MUL, ADD))
                link(layer_norm(x1[0:n, t, :], n, 0))
                link(tt(h2[0:n, t, :], x1[0:n, t, :], mod(2, t, n), MUL))
                link(tt(h2[0:n, t, :], h2[0:n, t, :], mod(1, t, n), ADD), signal=h2_ready, at=t + 1)
            end_phase(dve, OUT)

            top = buf("top")

            def field(at, n):
                return top[:, at:at + n]

            own, spare, cand, grid = (field(256 * k, 256) for k in range(4))
            own, spare = own.rearrange("p (e n) -> p e n", e=2), spare.rearrange("p (e n) -> p e n", e=2)
            t1v = field(1024, 32).rearrange("p (e k) -> p e k", e=2)
            ti = field(1056, 32).bitcast(U32).rearrange("p (e k) -> p e k", e=2)
            tif = field(1088, 32).rearrange("p (e k) -> p e k", e=2)
            cv, cp = field(1120, 16).unsqueeze(1), field(1136, 16).bitcast(U32).unsqueeze(1)
            pos = field(1152, 32).rearrange("p (e k) -> p e k", e=2)
            posf = field(1184, 32).rearrange("p (e k) -> p e k", e=2)
            ssum, smax = field(1216, 8), field(1224, 8)

            def top16(link, values, indices, src, spare):
                rows = range(src.shape[1])
                steps = (lambda i: nc.vector.max(values[:, i, 0:8], src[:, i, :]),
                         lambda i: nc.vector.max_index(indices[:, i, 0:8], values[:, i, 0:8], src[:, i, :]),
                         lambda i: nc.vector.match_replace(spare[:, i, :], values[:, i, 0:8], src[:, i, :], LOW),
                         lambda i: nc.vector.max(values[:, i, 8:16], spare[:, i, :]),
                         lambda i: nc.vector.max_index(indices[:, i, 8:16], values[:, i, 8:16], spare[:, i, :]))
                for step in steps:
                    dve.sem_inc(sort_tick, 1)
                    for i in rows:
                        link(step(i), wait=i == rows[-1])

            CHOOSE = 30

            def choose_head(link, t, i, head=0):
                link(nc.vector.tensor_copy(own, buf("ta" if t % 2 == 0 else "tb")[:, ds(i * 256 + head * 256, 256)]
                                           .rearrange("p (e n) -> p e n", e=2)))
                top16(link, t1v, ti, own, spare)
                square = [P, TOP, TOP]
                g4 = grid.rearrange("p (x i) -> p x i", i=TOP)
                link(tt(cand.rearrange("p (i j) -> p i j", i=TOP), along(t1v[:, 0, :], square, 2),
                        along(t1v[:, 1, :], square, 1), ADD))
                top16(link, cv, cp, cand.unsqueeze(1), grid.unsqueeze(1))
                link(ts(pos[:, 0, :].bitcast(U32), cp[:, 0, :], 4, None, ALU.logical_shift_right))
                link(ts(pos[:, 1, :].bitcast(U32), cp[:, 0, :], TOP - 1, None, ALU.bitwise_and))
                link(nc.vector.tensor_copy(tif, ti))
                link(nc.vector.tensor_copy(posf, pos.bitcast(U32)))
                for e in range(2):
                    link(tt(g4, along(posf[:, e, :], square, 2), along(iota, square, 1), ALU.is_equal))
                    link(tt(g4, g4, along(tif[:, e, :], square, 1), MUL))
                    link(red(posf[:, e, :], g4, AX.X, ADD))
                link(stt(idx_f[:, ds(i * TOP + head * TOP, TOP)], posf[:, 0, :], float(KEYS), posf[:, 1, :], MUL, ADD))
                link(nc.vector.tensor_copy(idx_u[:, ds(i * TOP + (t * SLOTS + head * TOP), TOP)],
                                           idx_f[:, ds(i * TOP + head * TOP, TOP)]))
                link(nc.vector.tensor_copy(coef_cols[:, ds(i * TOP + (t * SLOTS + head * TOP), TOP)], cv[:, 0, :]))

            def gates(t):
                n = P if t < NT else NS
                gate_t = coef[0:n, t, :].rearrange("p (h k) -> p h k", h=PH)
                link(nc.vector.tensor_copy(smax[0:n], gate_t[:, :, 0]), signal=top_done, at=t + 1)
                link(tt(gate_t, gate_t, along(smax[0:n], [n, PH, TOP], 2), SUB), signal=gate_ready, at=t + 1)
                dve.wait_ge(gate_exps, t + 1)
                link(red(ssum[0:n], gate_t, AX.X, ADD))
                link(nc.vector.reciprocal(ssum[0:n], ssum[0:n]))
                link(tt(gate_t, gate_t, along(ssum[0:n], [n, PH, TOP], 2), MUL),
                     signal=idx_ready if t < NT else top_s_ready, at=t + 1 if t < NT else 1)

            for gg in range(4):
                read(dve, f"s0_{gg}")
                with dve.Fori(0, 2) as i:
                    choose_head(link.in_loop(i, 2, CHOOSE), 0, i, 2 * gg)
            gates(0)
            for j in range(RING):
                dve.sem_inc(row_free[j], 2)
            dve.sem_inc(dots_kept, 1)
            end_phase(dve, QUERY)

            link(nc.vector.memset(zero, 0.0), signal=zero_ready, at=1)

            def gelu_times_gate(x, y, gate_x, count):
                link(tt(y, x, x, MUL))
                link(ts(y, y, 0.044715, 1.0, MUL, ADD))
                link(tt(y, y, x, MUL), signal=gelu_arg, at=count)
                dve.wait_ge(gelu_tanh, count)
                link(stt(y, y, 1.0, x, ADD, MUL))
                return lambda out: stt(out, y, 0.5, gate_x, MUL, MUL)

            def output(t, n):
                for u in range(2):
                    part = slice(512 * u, 512 * (u + 1))
                    job = f"y{t}_{u}" if t < NT else f"ys_{u}"
                    full(dve, job)
                    g2 = bc[:, 3, part] if t < NT else buf("g2s")[0:8, part]
                    link(tt(h2[0:n, t, part], bank(job)[0:n, :], g2, MUL), job=job)
                link(stt(h2[0:n, t, :], x1[0:n, t, :], ALPHA, h2[0:n, t, :], MUL, ADD))
                link(layer_norm(h2[0:n, t, :], n, 2), signal=y_ready, at=t + 1)

            dot = gelu[:, 2 * SLOTS:2 * SLOTS + TOP]

            def first_pass(t, chosen):
                n = 2 if t else 1
                first = TURN[t - 1]
                read(dve, f"s{chosen}_3")
                with dve.Fori(0, SLOTS // TOP) as i:
                    for x in range(TOP):
                        j = n * x % RING
                        dve.wait_ge(row_in[j], i * (32 * n) + 16 * (first + n * x // RING + 1))
                        if x == 0:
                            dve.wait_ge(dots_kept, i + (PH * t + 1))
                        nc.vector.tensor_tensor_reduce(
                            out=gathered[:, j, :], in0=gathered[:, j, :], in1=h2[:, t, :], scale=1.0, scalar=0.0,
                            op0=MUL, op1=ADD, accum_out=dot[:, x:x + 1]).then_inc(row_free[j], 1)
                    for j in range(0, RING, n):
                        dve.wait_ge(row_free[j], i * (2 * n) + (first + 2 * n + 2))
                    nc.vector.tensor_copy(gelu[:, ds(i * TOP + SLOTS, TOP)], dot).then_inc(dots_kept, 1)
                    choose_head(link.in_loop(i, PH, CHOOSE), chosen, i)
                dve.wait_ge(dots_kept, PH * (t + 1) + 1)
                done = gelu_times_gate(gelu[:, SLOTS:2 * SLOTS], gelu[:, 0:SLOTS], coef[:, t, :], t + 1)
                link(done(coef[:, t, :]), signal=coef_ready, at=t + 1)
                gates(chosen)

            first_pass(0, 1)
            for t in range(NT):
                if t < NT - 1:
                    first_pass(t + 1, t + 2)
                else:
                    full(dve, "tg")
                    link(nc.vector.tensor_copy(idx_s, bank("tg")[:, 0:NS]), signal=idx_ready, at=NT + 1)
                output(t, P)
            link(nc.vector.tensor_copy(gelu[:, 16:24], bank("tg")[:, NS:2 * NS]), job="tg")
            for b in range(NS):
                dve.wait_ge(row_in[b], 16 * (TURN[NT] + 1))
                for u in range(2):
                    full(dve, f"hb{b}_{u}")
                    part = slice(512 * u, 512 * (u + 1))
                    at = 24 + 2 * b + u
                    link(nc.vector.tensor_tensor_reduce(
                        out=bc[:, 0, part], in0=gathered[:, b, part], in1=bank(f"hb{b}_{u}")[:, :], scale=1.0,
                        scalar=0.0, op0=MUL, op1=ADD, accum_out=gelu[:, at:at + 1]), job=f"hb{b}_{u}")
                dve.sem_inc(row_free[b], 1)
            pairs = gelu[:, 24:40].rearrange("p (b u) -> p b u", u=2)
            link(tt(gelu[:, 8:16], pairs[:, :, 0], pairs[:, :, 1], ADD))
            done = gelu_times_gate(gelu[:, 8:16], gelu[:, 0:8], gelu[:, 16:24], NT + 1)
            link(done(gelu[:, 16:24]))
            link(tt(coef_s, along(gelu[:, 16:24], [P, NS, NS], 2), eye, MUL),
                 signal=coef_s_ready, at=1)
            output(NT, NS)


INPUTS = ["x_prompt", "x_sample", "cache_k", "cache_v", "cache_logf", "state_wkv", "state_shift", "page_table",
          "c_prompt", "c_sample", "w_ada", "b_ada", "w_in", "mu_shift", "w0", "w2_decay", "a0", "a2_iclr", "g2_gate",
          "k_k", "k_a", "r_k", "ln_x_w", "ln_x_b", "b_forget", "w_up_a", "w_up_b", "w_o", "ln1_g", "ln1_b",
          "peer_wq", "peer_keys1", "peer_keys2", "peer_u", "peer_v", "ln2_g", "ln2_b"]
OUTPUT_SHAPES = [(1, T, D), (NS, 1, D), (1, 1, T, H, HD), (1, 1, T, H, HD), (1, 1, T, H), (1, 1, H, HD, HD),
                 (1, 1, SHIFT), (1, NS, 1, H, HD), (1, NS, 1, H, HD), (1, NS, 1, H), (1, NS, H, HD, HD), (1, NS, SHIFT)]


def kernel(**inputs):
    import concourse.bacc as bacc
    from concourse.bass_utils import run_bass_kernel_spmd

    nc = bacc.Bacc("TRN2", target_bir_lowering=False, num_devices=1)
    arrays, args = {}, []
    for name in INPUTS:
        a = np.ascontiguousarray(inputs[name])
        arrays[f"in_{name}"] = a
        args.append(nc.dram_tensor(f"in_{name}", a.shape, mybir.dt.from_np(a.dtype), kind="ExternalInput").ap())
    arrays["in_constants"] = constants()
    args.append(nc.dram_tensor("in_constants", (P, CONST_COLS), mybir.dt.float32, kind="ExternalInput").ap())
    args.append(nc.dram_tensor("scratch_heads", (6, NS, W), mybir.dt.float32, kind="Internal").ap())
    args.append(nc.dram_tensor("scratch_out", (NS, W), mybir.dt.float32, kind="Internal").ap())
    args.append(nc.dram_tensor("scratch_modulations", (NS + 1, 4 * D), mybir.dt.float32, kind="Internal").ap())
    for i, shape in enumerate(OUTPUT_SHAPES):
        args.append(nc.dram_tensor(f"out_{i}", shape, mybir.dt.float32, kind="ExternalOutput").ap())
    hybrid_step(nc, *args)
    r = run_bass_kernel_spmd(nc, [arrays], core_ids=[0])
    return tuple(r.results[0][f"out_{i}"] for i in range(len(OUTPUT_SHAPES)))
```
